# Optimizing a Trainium2 kernel written in Bass

```python
import math
import numpy as np
import jax
import jax.numpy as jnp
from jax import lax
import jax, jax.numpy as jnp

D_MODEL = 1024
BATCH = 1
SEQ = 256
DEPTH = 1

HEAD_DIM = 64
GRID_W = 64
NA_HEADS = 8
NA_WIN_ROWS = 8
NA_WIN_COLS = 16
NA_QCOL_BLOCK = 16
NA_KCOL_BLOCK = NA_QCOL_BLOCK + NA_WIN_COLS
DIL_CONFIGS = ((128, 1), (512, 4), (2048, 16))
DIL_HEADS_PER_GROUP = 4
DIL_N_GROUPS = len(DIL_CONFIGS)
DIL_QBLOCK = 64
ROT_DIM = HEAD_DIM // 4
ROPE_THETA = 500000.0
NA_WIDTH = NA_HEADS * HEAD_DIM
DIL_WIDTH = DIL_N_GROUPS * DIL_HEADS_PER_GROUP * HEAD_DIM
DIL_OUT_WIDTH = DIL_HEADS_PER_GROUP * HEAD_DIM
IN_WIDTH = 3 * NA_WIDTH + 3 * DIL_WIDTH + 2 * D_MODEL
PEER_HEADS = 8
PEER_NKEYS = 128
PEER_NEXPERTS = PEER_NKEYS * PEER_NKEYS
PEER_QDIM = 256
PEER_TOPK = 16
PEER_CHUNK = 256
PLE_DIM = 256
RMS_EPS = 1e-6


def rms_norm(x, gain):
    x32 = x.astype(jnp.float32)
    y = x32 * lax.rsqrt(jnp.mean(x32 * x32, axis=-1, keepdims=True) + RMS_EPS)
    return (y * gain.astype(jnp.float32)).astype(x.dtype)

def partial_rotary(x, pos):
    half = ROT_DIM // 2
    inv_freq = jnp.power(jnp.float32(ROPE_THETA), -jnp.arange(half, dtype=jnp.float32) * 2.0 / ROT_DIM)
    ang = pos.astype(jnp.float32)[:, None] * inv_freq[None, :]
    cos = jnp.cos(ang)[:, None, :]
    sin = jnp.sin(ang)[:, None, :]
    xr = x[..., :ROT_DIM].astype(jnp.float32)
    x1, x2 = xr[..., :half], xr[..., half:]
    rot = jnp.concatenate([x1 * cos - x2 * sin, x2 * cos + x1 * sin], axis=-1)
    return jnp.concatenate([rot.astype(x.dtype), x[..., ROT_DIM:]], axis=-1)

def _na_static(width):
    ncb = width // NA_QCOL_BLOCK
    qc = np.arange(width).reshape(ncb, NA_QCOL_BLOCK)
    kc_start = np.clip(np.arange(ncb) * NA_QCOL_BLOCK - NA_WIN_COLS // 2, 0, width - NA_KCOL_BLOCK)
    kc = kc_start[:, None] + np.arange(NA_KCOL_BLOCK)[None, :]
    cs = np.clip(qc - NA_WIN_COLS // 2, 0, width - NA_WIN_COLS)
    kcb = kc[:, None, :]
    mask = (kcb >= cs[..., None]) & (kcb < cs[..., None] + NA_WIN_COLS)
    dc_idx = np.clip(kcb - qc[..., None] + NA_WIN_COLS - 1, 0, 2 * NA_WIN_COLS - 2)
    return kc, mask, dc_idx

def neighbourhood_attention(q, k, v, rpb):
    B, S, H, dh = q.shape
    rows = S // GRID_W
    kh = min(NA_WIN_ROWS, rows)
    ncb = GRID_W // NA_QCOL_BLOCK
    kc, mask, dc_idx = _na_static(GRID_W)
    mask_j = jnp.asarray(mask)[None, None, :, :, None, :]
    qg = q.reshape(B, rows, GRID_W, H, dh)
    kg = k.reshape(B, rows, GRID_W, H, dh)
    vg = v.reshape(B, rows, GRID_W, H, dh)
    scale = HEAD_DIM ** -0.5

    def one_row(r):
        rs = jnp.clip(r - kh // 2, 0, rows - kh)
        q_row = lax.dynamic_index_in_dim(qg, r, axis=1, keepdims=False)
        k_rows = lax.dynamic_slice_in_dim(kg, rs, kh, axis=1)
        v_rows = lax.dynamic_slice_in_dim(vg, rs, kh, axis=1)
        q_cb = q_row.reshape(B, ncb, NA_QCOL_BLOCK, H, dh)
        k_cb = jnp.take(k_rows, kc, axis=2)
        v_cb = jnp.take(v_rows, kc, axis=2)
        s = jnp.einsum('bjqhd,bljkhd->bhjqlk', q_cb, k_cb).astype(jnp.float32) * scale
        dr_idx = rs + jnp.arange(kh) - r + NA_WIN_ROWS - 1
        bias = rpb[:, dr_idx][:, :, dc_idx]
        bias = bias.transpose(0, 2, 3, 1, 4).astype(jnp.float32)
        s = jnp.where(mask_j, s + bias[None], -jnp.inf)
        shp = s.shape
        pr = jax.nn.softmax(s.reshape(shp[:4] + (kh * NA_KCOL_BLOCK,)), axis=-1).reshape(shp)
        o = jnp.einsum('bhjqlk,bljkhd->bjqhd', pr.astype(v.dtype), v_cb)
        return o.reshape(B, GRID_W, H, dh)

    out = lax.map(one_row, jnp.arange(rows))
    return out.transpose(1, 0, 2, 3, 4).reshape(B, S, H * dh)

def dilated_window_attention(q, k, v, window, dilation):
    B, S, H, dh = q.shape
    n = window // (2 * dilation)
    L = S // dilation
    qbs = math.gcd(L, DIL_QBLOCK)
    nblk = L // qbs
    kbs = qbs + 2 * n

    def to_res(t):
        return t.reshape(B, L, dilation, H, dh).transpose(0, 2, 1, 3, 4)

    qr, kr, vr = to_res(q), to_res(k), to_res(v)
    pad = ((0, 0), (0, 0), (n, n), (0, 0), (0, 0))
    kp = jnp.pad(kr, pad)
    vp = jnp.pad(vr, pad)
    kidx = (np.arange(nblk) * qbs)[:, None] + np.arange(kbs)[None, :]
    kb = jnp.take(kp, kidx, axis=2)
    vb = jnp.take(vp, kidx, axis=2)
    qb = qr.reshape(B, dilation, nblk, qbs, H, dh)
    s = jnp.einsum('brnqhd,brnkhd->brnhqk', qb, kb).astype(jnp.float32) * (HEAD_DIM ** -0.5)
    qi = np.arange(qbs)[:, None]
    kj = np.arange(kbs)[None, :]
    band = (kj - qi >= 0) & (kj - qi <= 2 * n)
    m_key = kidx - n
    inside = (m_key >= 0) & (m_key < L)
    mask = band[None] & inside[:, None, :]
    s = jnp.where(jnp.asarray(mask)[None, None, :, None, :, :], s, -jnp.inf)
    lse = jax.nn.logsumexp(s, axis=-1, keepdims=True)
    pr = jnp.exp(s - lse).astype(v.dtype)
    o = jnp.einsum('brnhqk,brnkhd->brnqhd', pr, vb)
    o = o.reshape(B, dilation, L, H, dh).transpose(0, 2, 1, 3, 4).reshape(B, S, H, dh)
    lse = lse[..., 0].transpose(0, 1, 2, 4, 3).reshape(B, dilation, L, H)
    lse = lse.transpose(0, 2, 1, 3).reshape(B, S, H)
    return o, lse

def peer_ffn(h, w_query, sub_keys, expert_u, expert_v):
    B, S, D = h.shape
    T = B * S
    chunk = math.gcd(T, PEER_CHUNK)
    half = PEER_QDIM // 2
    hf = h.reshape(T // chunk, chunk, D)
    k1 = sub_keys[0].astype(jnp.float32)
    k2 = sub_keys[1].astype(jnp.float32)

    def run(hc):
        q = (hc @ w_query).reshape(chunk, PEER_HEADS, PEER_QDIM).astype(jnp.float32)
        s1 = jnp.einsum('thd,nd->thn', q[..., :half], k1)
        s2 = jnp.einsum('thd,nd->thn', q[..., half:], k2)
        v1, i1 = lax.top_k(s1, PEER_TOPK)
        v2, i2 = lax.top_k(s2, PEER_TOPK)
        cand = (v1[..., :, None] + v2[..., None, :]).reshape(chunk, PEER_HEADS, PEER_TOPK * PEER_TOPK)
        cidx = (i1[..., :, None] * PEER_NKEYS + i2[..., None, :]).reshape(chunk, PEER_HEADS, PEER_TOPK * PEER_TOPK)
        sc, pos = lax.top_k(cand, PEER_TOPK)
        eidx = jnp.take_along_axis(cidx, pos, axis=-1)
        g = jax.nn.softmax(sc, axis=-1)
        u = jnp.take(expert_u, eidx, axis=0)
        a = jnp.einsum('thkd,td->thk', u, hc).astype(jnp.float32)
        act = (jax.nn.gelu(a, approximate=False) * g).astype(hc.dtype)
        vv = jnp.take(expert_v, eidx, axis=0)
        return jnp.einsum('thk,thkd->td', act, vv)

    return lax.map(run, hf).reshape(B, S, D)

def first_inputs(seed: int = 0) -> dict:
    key = jax.random.key(seed)
    ks = jax.random.split(key, 20)

    def nrm(k, shape, scale):
        return jax.random.normal(k, shape, jnp.float32) * scale

    def gain(k, shape):
        return 1.0 + 0.05 * jax.random.normal(k, shape, jnp.float32)

    return {
        "x": nrm(ks[0], (BATCH, SEQ, D_MODEL), 1.0),
        "p": nrm(ks[1], (DEPTH, BATCH, SEQ, PLE_DIM), 1.0),
        "norm_mix": gain(ks[2], (DEPTH, D_MODEL)),
        "w_in": nrm(ks[3], (DEPTH, D_MODEL, IN_WIDTH), D_MODEL ** -0.5),
        "qk_norm_na": gain(ks[4], (DEPTH, 2, HEAD_DIM)),
        "na_rel_bias": nrm(ks[5], (DEPTH, NA_HEADS, 2 * NA_WIN_ROWS - 1, 2 * NA_WIN_COLS - 1), 0.2),
        "qk_norm_dil": gain(ks[6], (DEPTH, 2, HEAD_DIM)),
        "w_branch_na": nrm(ks[7], (DEPTH, NA_WIDTH, D_MODEL), NA_WIDTH ** -0.5),
        "w_branch_dil": nrm(ks[8], (DEPTH, DIL_OUT_WIDTH, D_MODEL), DIL_OUT_WIDTH ** -0.5),
        "w_out": nrm(ks[9], (DEPTH, D_MODEL, D_MODEL), D_MODEL ** -0.5),
        "norm_ffn": gain(ks[10], (DEPTH, D_MODEL)),
        "peer_w_query": nrm(ks[11], (DEPTH, D_MODEL, PEER_HEADS * PEER_QDIM), D_MODEL ** -0.5),
        "peer_sub_keys": nrm(ks[12], (DEPTH, 2, PEER_NKEYS, PEER_QDIM // 2), (PEER_QDIM // 2) ** -0.5),
        "peer_expert_u": nrm(ks[13], (DEPTH, PEER_NEXPERTS, D_MODEL), D_MODEL ** -0.5),
        "peer_expert_v": nrm(ks[14], (DEPTH, PEER_NEXPERTS, D_MODEL), PEER_HEADS ** -0.5),
        "norm_ple": gain(ks[15], (DEPTH, D_MODEL)),
        "w_ple_gate": nrm(ks[16], (DEPTH, D_MODEL, D_MODEL), D_MODEL ** -0.5),
        "w_ple": nrm(ks[17], (DEPTH, PLE_DIM, D_MODEL), PLE_DIM ** -0.5),
    }

def first_block(x, p, norm_mix, w_in, qk_norm_na, na_rel_bias, qk_norm_dil, w_branch_na, w_branch_dil,
              w_out, norm_ffn, peer_w_query, peer_sub_keys, peer_expert_u, peer_expert_v,
              norm_ple, w_ple_gate, w_ple):
    B, S, D = x.shape
    pos = jnp.arange(S)
    splits = [int(c) for c in np.cumsum([NA_WIDTH] * 3 + [DIL_WIDTH] * 3 + [D_MODEL])]
    n_dil_heads = DIL_N_GROUPS * DIL_HEADS_PER_GROUP
    for i in range(DEPTH):
        h = rms_norm(x, norm_mix[i])
        proj = h @ w_in[i]
        qa, ka, va, qd, kd, vd, gate_na, gate_dil = jnp.split(proj, splits, axis=-1)

        qa = rms_norm(qa.reshape(B, S, NA_HEADS, HEAD_DIM), qk_norm_na[i, 0])
        ka = rms_norm(ka.reshape(B, S, NA_HEADS, HEAD_DIM), qk_norm_na[i, 1])
        va = va.reshape(B, S, NA_HEADS, HEAD_DIM)
        out_na = neighbourhood_attention(qa, ka, va, na_rel_bias[i])

        qd = partial_rotary(rms_norm(qd.reshape(B, S, n_dil_heads, HEAD_DIM), qk_norm_dil[i, 0]), pos)
        kd = partial_rotary(rms_norm(kd.reshape(B, S, n_dil_heads, HEAD_DIM), qk_norm_dil[i, 1]), pos)
        qd = qd.reshape(B, S, DIL_N_GROUPS, DIL_HEADS_PER_GROUP, HEAD_DIM)
        kd = kd.reshape(B, S, DIL_N_GROUPS, DIL_HEADS_PER_GROUP, HEAD_DIM)
        vd = vd.reshape(B, S, DIL_N_GROUPS, DIL_HEADS_PER_GROUP, HEAD_DIM)
        outs, lses = [], []
        for g, (window, dilation) in enumerate(DIL_CONFIGS):
            o_g, lse_g = dilated_window_attention(qd[:, :, g], kd[:, :, g], vd[:, :, g], window, dilation)
            outs.append(o_g)
            lses.append(lse_g)
        wts = jax.nn.softmax(jnp.stack(lses, axis=2), axis=2)
        out_dil = jnp.sum(wts[..., None] * jnp.stack(outs, axis=2).astype(jnp.float32), axis=2)
        out_dil = out_dil.astype(x.dtype).reshape(B, S, DIL_OUT_WIDTH)

        merged = (jax.nn.sigmoid(gate_na) * (out_na @ w_branch_na[i])
                  + jax.nn.sigmoid(gate_dil) * (out_dil @ w_branch_dil[i]))
        x = x + merged @ w_out[i]

        h = rms_norm(x, norm_ffn[i])
        x = x + peer_ffn(h, peer_w_query[i], peer_sub_keys[i], peer_expert_u[i], peer_expert_v[i])

        h = rms_norm(x, norm_ple[i])
        x = x + jax.nn.sigmoid(h @ w_ple_gate[i]) * (p[i] @ w_ple[i])
    return x


N_META = 16
EPS = 1e-6

SB_HEADS = 8
SB_HEAD_DIM = D_MODEL // 16
SB_WIDTH = SB_HEADS * SB_HEAD_DIM
SB_BLOCK = 128

GLA_HEADS = 4
GLA_DV = D_MODEL // 8
GLA_DK = GLA_DV // 2
GLA_WIDTH = GLA_HEADS * GLA_DV
GLA_KW = GLA_HEADS * GLA_DK
GLA_GATE_RANK = 16
GLA_TAU = 16.0
GLA_CHUNK = 64

MIX_WIDTH = SB_WIDTH + GLA_WIDTH
IN_SPLITS = [SB_WIDTH, SB_WIDTH, SB_WIDTH, GLA_KW, GLA_KW, GLA_WIDTH, GLA_WIDTH, GLA_GATE_RANK]
IN_COLS = sum(IN_SPLITS)

PEER_QDIM_2 = 128
PEER_HALF = PEER_QDIM_2 // 2
N_EXPERTS = PEER_NKEYS * PEER_NKEYS
PEER_BLOCK = 256


def rmsnorm(x, g):
    xf = x.astype(jnp.float32)
    y = xf * lax.rsqrt(jnp.mean(xf * xf, axis=-1, keepdims=True) + EPS)
    return (y * g.astype(jnp.float32)).astype(x.dtype)

def split_heads(t, n):
    b, l, _ = t.shape
    return t.reshape(b, l, n, -1).transpose(0, 2, 1, 3)

def merge_heads(t):
    b, h, l, d = t.shape
    return t.transpose(0, 2, 1, 3).reshape(b, l, h * d)

def sb_query_block(q_blk, q_pos, k, v):
    L = k.shape[2]
    z = jnp.einsum('bhqd,bhkd->bhqk', q_blk, k).astype(jnp.float32) * (SB_HEAD_DIM ** -0.5)
    mask = jnp.arange(L)[None, :] < q_pos[:, None]
    log_1m = jnp.where(mask, jax.nn.log_sigmoid(-z), 0.0)
    between = lax.cumsum(log_1m, axis=3, reverse=True) - log_1m
    a = jnp.where(mask, jnp.exp(jax.nn.log_sigmoid(z) + between), 0.0)
    return jnp.einsum('bhqk,bhkd->bhqd', a, v.astype(jnp.float32)).astype(v.dtype)

def stick_breaking_attention(q, k, v):
    b, h, L, d = q.shape
    n_real = L - N_META
    o_meta = sb_query_block(q[:, :, :N_META], jnp.arange(N_META), k, v)
    starts = N_META + jnp.arange(n_real // SB_BLOCK) * SB_BLOCK

    def body(start):
        qb = lax.dynamic_slice_in_dim(q, start, SB_BLOCK, axis=2)
        return sb_query_block(qb, start + jnp.arange(SB_BLOCK), k, v)

    o_real = lax.map(body, starts)
    o_real = jnp.moveaxis(o_real, 0, 2).reshape(b, h, n_real, d)
    return jnp.concatenate([o_meta, o_real], axis=2)

def gla_chunk(state, xs):
    q, k, v, lg = xs
    C = q.shape[2]
    bcum = jnp.cumsum(lg, axis=2)
    o_inter = jnp.einsum('bhtd,bhde->bhte', q * jnp.exp(bcum), state)
    causal = (jnp.arange(C)[:, None] >= jnp.arange(C)[None, :])[:, :, None]
    diff = bcum[:, :, :, None, :] - bcum[:, :, None, :, :]
    decay = jnp.where(causal, jnp.exp(jnp.where(causal, diff, 0.0)), 0.0)
    attn = jnp.einsum('bhtd,bhsd,bhtsd->bhts', q, k, decay)
    o = o_inter + jnp.einsum('bhts,bhse->bhte', attn, v)
    b_last = bcum[:, :, -1:, :]
    new_state = jnp.exp(b_last[:, :, 0, :])[..., None] * state + \
        jnp.einsum('bhsd,bhse->bhde', k * jnp.exp(b_last - bcum), v)
    return new_state, o

def gated_linear_attention(q, k, v, lg):
    out_dtype = v.dtype
    q, k, v, lg = (t.astype(jnp.float32) for t in (q, k, v, lg))
    b, h, L, dk = q.shape
    dv = v.shape[-1]
    n_real = L - N_META
    n_chunks = n_real // GLA_CHUNK
    state0 = jnp.zeros((b, h, dk, dv), jnp.float32)
    state, o_meta = gla_chunk(state0, (q[:, :, :N_META], k[:, :, :N_META], v[:, :, :N_META], lg[:, :, :N_META]))

    def to_chunks(t):
        return jnp.moveaxis(t[:, :, N_META:].reshape(b, h, n_chunks, GLA_CHUNK, t.shape[-1]), 2, 0)

    _, o_real = lax.scan(gla_chunk, state, (to_chunks(q), to_chunks(k), to_chunks(v), to_chunks(lg)))
    o_real = jnp.moveaxis(o_real, 0, 2).reshape(b, h, n_real, dv)
    return jnp.concatenate([o_meta, o_real], axis=2).astype(out_dtype)

def hybrid_mixer(hn, w_in, w_gate_up, b_gate_up, sb_norm_g, gla_norm_g, w_out):
    proj = hn @ w_in
    offsets = list(np.cumsum(IN_SPLITS)[:-1])
    sbq, sbk, sbv, gq, gk, gv, gr, glr = jnp.split(proj, offsets, axis=-1)
    sb_o = stick_breaking_attention(split_heads(sbq, SB_HEADS), split_heads(sbk, SB_HEADS),
                                    split_heads(sbv, SB_HEADS))
    sb_o = merge_heads(rmsnorm(sb_o, sb_norm_g.reshape(SB_HEADS, 1, SB_HEAD_DIM)))
    lg = jax.nn.log_sigmoid((glr @ w_gate_up + b_gate_up).astype(jnp.float32)) / GLA_TAU
    gla_o = gated_linear_attention(split_heads(gq, GLA_HEADS) * (GLA_DK ** -0.5),
                                   split_heads(gk, GLA_HEADS), split_heads(gv, GLA_HEADS),
                                   split_heads(lg, GLA_HEADS))
    gla_o = merge_heads(rmsnorm(gla_o, gla_norm_g.reshape(GLA_HEADS, 1, GLA_DV))) * jax.nn.silu(gr)
    return jnp.concatenate([sb_o, gla_o], axis=-1) @ w_out

def peer_ffn_2(hn, w_peer_q, sub_keys1, sub_keys2, expert_u, expert_v):
    b, L, d = hn.shape
    t = hn.reshape(b * L, d)
    T = t.shape[0]
    q = (t @ w_peer_q).reshape(T, PEER_HEADS, 2, PEER_HALF)
    s1 = jnp.einsum('thd,hkd->thk', q[:, :, 0], sub_keys1).astype(jnp.float32)
    s2 = jnp.einsum('thd,hkd->thk', q[:, :, 1], sub_keys2).astype(jnp.float32)
    v1, i1 = lax.top_k(s1, PEER_TOPK)
    v2, i2 = lax.top_k(s2, PEER_TOPK)
    cand = (v1[..., :, None] + v2[..., None, :]).reshape(T, PEER_HEADS, PEER_TOPK * PEER_TOPK)
    cidx = (i1[..., :, None] * PEER_NKEYS + i2[..., None, :]).reshape(T, PEER_HEADS, PEER_TOPK * PEER_TOPK)
    sc, pos = lax.top_k(cand, PEER_TOPK)
    eidx = jnp.take_along_axis(cidx, pos, axis=-1).reshape(T, PEER_HEADS * PEER_TOPK)
    gates = jax.nn.softmax(sc, axis=-1).reshape(T, PEER_HEADS * PEER_TOPK).astype(hn.dtype)
    n_blocks = -(-T // PEER_BLOCK)
    pad = n_blocks * PEER_BLOCK - T
    tb = jnp.pad(t, ((0, pad), (0, 0))).reshape(n_blocks, PEER_BLOCK, d)
    eb = jnp.pad(eidx, ((0, pad), (0, 0))).reshape(n_blocks, PEER_BLOCK, -1)
    gb = jnp.pad(gates, ((0, pad), (0, 0))).reshape(n_blocks, PEER_BLOCK, -1)

    def block(args):
        xt, e, g = args
        act = jax.nn.gelu(jnp.einsum('nkd,nd->nk', expert_u[e], xt), approximate=False)
        return jnp.einsum('nk,nkd->nd', g * act, expert_v[e])

    y = lax.map(block, (tb, eb, gb)).reshape(n_blocks * PEER_BLOCK, d)[:T]
    return y.reshape(b, L, d)

def second_inputs(seed: int = 0) -> dict:
    key = jax.random.key(seed)
    ks = jax.random.split(key, 20)
    n = jax.random.normal
    f = jnp.float32
    return {
        "x": n(ks[0], (BATCH, SEQ, D_MODEL), f),
        "meta_tokens": n(ks[1], (N_META, D_MODEL), f),
        "norm1_g": 1.0 + 0.02 * n(ks[2], (DEPTH, D_MODEL), f),
        "w_in": n(ks[3], (DEPTH, D_MODEL, IN_COLS), f) * D_MODEL ** -0.5,
        "w_gate_up": n(ks[4], (DEPTH, GLA_GATE_RANK, GLA_KW), f) * GLA_GATE_RANK ** -0.5,
        "b_gate_up": 0.1 * n(ks[5], (DEPTH, GLA_KW), f),
        "sb_norm_g": 1.0 + 0.02 * n(ks[6], (DEPTH, SB_WIDTH), f),
        "gla_norm_g": 1.0 + 0.02 * n(ks[7], (DEPTH, GLA_WIDTH), f),
        "w_out": n(ks[8], (DEPTH, MIX_WIDTH, D_MODEL), f) * MIX_WIDTH ** -0.5,
        "norm2_g": 1.0 + 0.02 * n(ks[9], (DEPTH, D_MODEL), f),
        "w_peer_q": n(ks[10], (DEPTH, D_MODEL, PEER_HEADS * PEER_QDIM_2), f) * D_MODEL ** -0.5,
        "sub_keys1": n(ks[11], (DEPTH, PEER_HEADS, PEER_NKEYS, PEER_HALF), f) * PEER_HALF ** -0.5,
        "sub_keys2": n(ks[12], (DEPTH, PEER_HEADS, PEER_NKEYS, PEER_HALF), f) * PEER_HALF ** -0.5,
        "expert_u": n(ks[13], (DEPTH, N_EXPERTS, D_MODEL), f) * D_MODEL ** -0.5,
        "expert_v": n(ks[14], (DEPTH, N_EXPERTS, D_MODEL), f) * PEER_HEADS ** -0.5,
        "norm_f_g": 1.0 + 0.02 * n(ks[15], (D_MODEL,), f),
    }

def second_block(x, meta_tokens, norm1_g, w_in, w_gate_up, b_gate_up, sb_norm_g, gla_norm_g, w_out,
              norm2_g, w_peer_q, sub_keys1, sub_keys2, expert_u, expert_v, norm_f_g):
    b = x.shape[0]
    meta = jnp.broadcast_to(meta_tokens.astype(x.dtype)[None], (b, N_META, x.shape[-1]))
    h = jnp.concatenate([meta, x], axis=1)
    for l in range(DEPTH):
        h = h + hybrid_mixer(rmsnorm(h, norm1_g[l]), w_in[l], w_gate_up[l], b_gate_up[l],
                             sb_norm_g[l], gla_norm_g[l], w_out[l])
        h = h + peer_ffn_2(rmsnorm(h, norm2_g[l]), w_peer_q[l], sub_keys1[l], sub_keys2[l],
                         expert_u[l], expert_v[l])
    return rmsnorm(h, norm_f_g)[:, N_META:]


def setup_inputs(seed=0):
    out = dict(first_inputs(seed))
    for name, value in second_inputs(seed + 1).items():
        if name != "x":
            out[name + "_2"] = value
    return out


def reference(
    x, p, norm_mix, w_in, qk_norm_na, na_rel_bias, qk_norm_dil, w_branch_na, w_branch_dil,
    w_out, norm_ffn, peer_w_query, peer_sub_keys, peer_expert_u, peer_expert_v, norm_ple,
    w_ple_gate, w_ple, meta_tokens_2, norm1_g_2, w_in_2, w_gate_up_2, b_gate_up_2, sb_norm_g_2,
    gla_norm_g_2, w_out_2, norm2_g_2, w_peer_q_2, sub_keys1_2, sub_keys2_2, expert_u_2,
    expert_v_2, norm_f_g_2,
):
    x = first_block(
        x, p, norm_mix, w_in, qk_norm_na, na_rel_bias, qk_norm_dil, w_branch_na, w_branch_dil,
        w_out, norm_ffn, peer_w_query, peer_sub_keys, peer_expert_u, peer_expert_v, norm_ple,
        w_ple_gate, w_ple,
    )
    return second_block(
        x, meta_tokens_2, norm1_g_2, w_in_2, w_gate_up_2, b_gate_up_2, sb_norm_g_2,
        gla_norm_g_2, w_out_2, norm2_g_2, w_peer_q_2, sub_keys1_2, sub_keys2_2, expert_u_2,
        expert_v_2, norm_f_g_2,
    )


_drawn_inputs = setup_inputs


def setup_inputs(seed=0):
    import zlib

    import numpy as np

    out = dict(_drawn_inputs(seed))
    spreads = {}
    factors = {'qk_norm_dil': 2.736,
     'norm_ple': 3.172,
     'b_gate_up_2': 2.716,
     'sb_norm_g_2': 9.507,
     'gla_norm_g_2': 16.177,
     'norm2_g_2': 9.083,
     'norm_f_g_2': 8.279}
    for name, (base, spread) in spreads.items():
        noise = np.random.default_rng([zlib.crc32(name.encode()), seed]).standard_normal(out[name].shape)
        drawn = base * np.exp(spread * noise) if base else spread * noise
        out[name] = jnp.asarray(drawn.astype(out[name].dtype))
    for name, factor in factors.items():
        out[name] = (out[name] * factor).astype(out[name].dtype)
    return out
```

```python
from contextlib import ExitStack

import numpy as np

import concourse.bass as bass
from concourse import mybir

F32 = mybir.dt.float32
U32 = mybir.dt.uint32
ALU = mybir.AluOpType
ACT = mybir.ActivationFunctionType
AX = mybir.AxisListType

P = 128
D = 1024
DC = D // P
TILES = 2
SEQ = TILES * P
EPS = 1e-6
NEG = -1e30
META = 16
HEAD = 64
NA_HEADS = 8
DIL_GROUPS, DIL_SLOTS = 3, 4
DIL_HEADS = DIL_GROUPS * DIL_SLOTS
GRID_W, GRID_ROWS = 64, SEQ // 64
NA_WIN_ROWS, NA_WIN_COLS = 8, 16
ROT_HALF = 8
ROPE_THETA = 500000.0
QK_HEADS = 2 * NA_HEADS + 2 * DIL_HEADS
PAIRS = QK_HEADS // 2
V_COLS = (NA_HEADS + DIL_HEADS) * HEAD
SB_HEADS = 8
GLA_HEADS, GLA_DK, GLA_DV = 4, 64, 128
RANK = 16
GLA_TAU = 16.0
LEVELS = 8
INTER, LAST = LEVELS, LEVELS + 1
PEER_HEADS, KEYS, TOPK = 8, 128, 16
SLOTS = PEER_HEADS * TOPK
EXPERTS = KEYS * KEYS

RING = 8
CHUNK = 4
ITERS = SLOTS // RING
PHASES = 4
WSLOTS = 4
UNIT = 2048
BANKS = 5
OUT_BANK = BANKS

N_IN, N_BRANCH, N_OUT, N_Q1 = 23, 3, 4, 8
N_FIRST = N_IN + N_BRANCH + N_OUT + N_Q1
N_TILE = 4 + 1 + 12 + 4 + 4
N_UNITS = N_FIRST + N_TILE
N_LOADS = N_FIRST + TILES * N_TILE

_at = 0
CONST = {}
for _name, _n in (("ident", P), ("decay", (LEVELS + 2) * P), ("pairs", LEVELS * P), ("later", P), ("ones", P),
                  ("causal", P), ("causal_neg", P), ("iota", TOPK), ("rope", TILES * 2 * ROT_HALF),
                  ("na_cols", GRID_W), ("decay_meta", META)):
    CONST[_name] = (_at, _at + _n)
    _at += _n
N_CONST = _at


def constants():
    c = np.zeros((P, N_CONST), np.float32)

    def put(name, a):
        lo, hi = CONST[name]
        c[:a.shape[0], lo:hi] = a.reshape(a.shape[0], hi - lo)

    i = np.arange(P)
    put("ident", np.eye(P, dtype=np.float32))
    decay = np.zeros((P, LEVELS + 2, P), np.float32)
    pairs = np.zeros((P, LEVELS, P), np.float32)
    pairs[:, 0] = np.eye(P)
    for level in range(1, LEVELS):
        half = 1 << (level - 1)
        mid = (i // (2 * half)) * 2 * half + half
        right = i >= mid
        s, t = i[:, None], i[None, :]
        decay[:, level] = np.where(right[None], (s >= mid[None]) & (s <= t), (s > t) & (s < mid[None]))
        pairs[:, level] = (mid[:, None] == mid[None]) & ~right[:, None] & right[None]
    decay[:, INTER] = i[:, None] <= i[None]
    decay[:, LAST] = i[:, None] > i[None]
    put("decay", decay)
    put("pairs", pairs)
    put("later", (i[:, None] >= i[None]).astype(np.float32))
    put("ones", np.ones((P, P), np.float32))
    put("causal", (i[:, None] < i[None]).astype(np.float32))
    put("causal_neg", np.where(i[:, None] < i[None], 0.0, NEG).astype(np.float32))
    put("iota", np.tile(np.arange(TOPK, dtype=np.float32), (P, 1)))
    freq = np.power(np.float32(ROPE_THETA), -np.arange(ROT_HALF, dtype=np.float32) * 2.0 / (2 * ROT_HALF))
    angle = np.arange(SEQ, dtype=np.float32)[:, None] * freq.astype(np.float32)[None]
    rope = np.stack([np.cos(angle), np.sin(angle)], 1).reshape(TILES, P, 2 * ROT_HALF)
    put("rope", rope.transpose(1, 0, 2).astype(np.float32))
    qc = i % GRID_W
    start = np.clip(qc - NA_WIN_COLS // 2, 0, GRID_W - NA_WIN_COLS)[:, None]
    kc = np.arange(GRID_W)[None]
    put("na_cols", np.where((kc >= start) & (kc < start + NA_WIN_COLS), 0.0, NEG).astype(np.float32))
    m = np.arange(META)
    put("decay_meta", (m[:, None] > m[None]).astype(np.float32))
    q = np.arange(SEQ)[:, None]
    k = np.arange(SEQ)[None]
    seen = np.stack([np.abs(q - k) <= 64, (q - k) % 4 == 0, (q - k) % 16 == 0], 1)
    dil = np.where(seen, 0.0, NEG).astype(np.float32).reshape(TILES, P, DIL_GROUPS * SEQ)
    return c, np.ascontiguousarray(dil.transpose(1, 0, 2))


def build(nc, a, out):
    ctx = ExitStack()
    with ctx:
        def sb(name, shape, dt=F32):
            return ctx.enter_context(nc.sbuf_tensor(name, [P, *shape], dt))

        sems = {}

        def sem(name):
            if name not in sems:
                sems[name] = ctx.enter_context(nc.semaphore(name))
            return sems[name]

        ring = sb("ring", [RING, 2 * D])
        wring = sb("wring", [WSLOTS, UNIT])
        work = sb("work", [7168])
        X = sb("X", [TILES, D])
        hn = sb("hn", [TILES, D])
        hT = sb("hT", [DC, META + SEQ])
        const = sb("const", [N_CONST])
        gain = sb("gain", [3, D])
        head_gain = sb("head_gain", [2, 512])
        gain_col = sb("gain_col", [3, DC])
        qk_gain = sb("qk_gain", [4, HEAD])
        sbk = sb("sbk", [4, META + SEQ])
        sbv = sb("sbv", [3, 512])
        gv = sb("gv", [512])
        state = sb("state", [2, GLA_DV])
        keys1 = sb("keys1", [2, KEYS])
        keys2 = sb("keys2", [PEER_HEADS, KEYS])
        pT = sb("pT", [2, SEQ])
        w_lr = sb("w_lr", [DC, RANK])
        w_gu = sb("w_gu", [GLA_HEADS * GLA_DK])
        eidx = sb("eidx", [TILES, SLOTS], U32)
        gates = sb("gates", [TILES, SLOTS])
        slot_idx = sb("slot_idx", [RING], U32)
        dot = sb("dot", [RING])
        act_dot = sb("act_dot", [RING])
        weight = sb("weight", [RING])
        diag = sb("diag", [RING, P])
        fence = sb("fence", [1])
        stat = sb("stat", [32])
        hstat = sb("hstat", [2, QK_HEADS])
        amax = sb("amax", [16])
        asum = sb("asum", [TILES, 16])
        arec = sb("arec", [16])

        def cst(name, rows=P):
            lo, hi = CONST[name]
            return const[0:rows, lo:hi]

        ident = cst("ident")
        decay = cst("decay")
        pairs = cst("pairs").rearrange("p (l t) -> p l t", l=LEVELS)
        zeros = decay[:, 0:P]

        flat = ring[:, :, :].rearrange("p a b -> p (a b)")

        def cut(base, at, *shape):
            n = int(np.prod(shape))
            v = base[:, at:at + n]
            if len(shape) == 2:
                v = v.rearrange("p (a b) -> p a b", a=shape[0])
            if len(shape) == 3:
                v = v.rearrange("p (a b c) -> p a b c", a=shape[0], b=shape[1])
            return v

        qkT = cut(flat, 0, PAIRS, SEQ)
        val = cut(flat, 5120, TILES, V_COLS)
        sig = cut(flat, 7680, TILES, 2 * D)
        na_bias = cut(flat, 11776, NA_HEADS, 6 * GRID_W)
        dil_mask = cut(flat, 14848, TILES, DIL_GROUPS * SEQ)
        meta_x = cut(flat, 0, D)
        meta_h = cut(flat, D, D)
        raw = cut(work, 0, TILES, QK_HEADS * HEAD)
        sq = cut(work, 5120, 512)
        rot = cut(work, 5632, 4, 2 * DIL_HEADS * ROT_HALF)
        prob = [hn[:, b, 0:768] for b in range(2)]
        probT = cut(work, 5632, 2, 768)
        attn = [raw[:, t, 0:768] for t in range(TILES)]
        qpT = cut(work, 0, 16, SEQ)
        tk = {n: cut(work, 4096 + 128 * k, PEER_HEADS, TOPK)
              for k, n in enumerate(("v1", "v2", "i1f", "i2f", "sc", "pos", "pa", "pb", "ia", "ib", "i1", "i2"))}
        gone = cut(work, 5632, KEYS)
        cand = cut(work, 5760, TOPK * TOPK)
        cand_gone = cut(work, 6016, TOPK * TOPK)
        onehot = cut(work, 6272, 2 * TOPK, TOPK)
        top_exp = cut(work, 6784, PEER_HEADS, TOPK)
        top_sum = cut(work, 6912, PEER_HEADS)
        ple_gate = cut(work, 0, D)
        sb_log = cut(work, 0, 3, 512)
        sb_tmp = cut(work, 1536, 2, 512)
        sb_a = cut(work, 2560, 3, 512)
        sbq = cut(work, 4096, 4, P)
        gqT = cut(work, 4608, 2, P)
        gkT = cut(work, 4864, 2, META + P)
        lg = cut(work, 5152, 256)
        lrT = cut(work, 5408, META + P)
        silu = cut(work, 5552, 512)
        lg_m = cut(work, 6064, 256)
        klast = cut(work, 6320, 2, P)
        klm = cut(work, 6576, 2, META)
        gvm = cut(work, 6608, 512)
        expd = cut(work, 0, (LEVELS + 2) * P)
        gla_q = cut(work, 1280, LEVELS + 1, P)
        gla_k = cut(work, 2432, LEVELS + 1, P)
        gla_a = cut(work, 3584, LEVELS, P)
        sq2 = cut(work, 0, 512)

        acc = ctx.enter_context(nc.psum_tensor("acc", [P, 2, 512], F32))
        bank = [ctx.enter_context(nc.psum_tensor(f"bank{b}", [P, 512], F32)) for b in range(BANKS + 1)]

        job = {}
        turns = {"short": 0, "out": 0}

        def place(name):
            assert name not in job, name
            if name[0] in ("stick_o", "gla_o"):
                b, turn = OUT_BANK, turns["out"]
                turns["out"] += 1
            else:
                b, turn = turns["short"] % BANKS, turns["short"] // BANKS
                turns["short"] += 1
            job[name] = (b, turn)
            return bank[b]

        def filled(eng, name):
            b, turn = job[name]
            eng.wait_ge(sem(f"bank_filled{b}"), turn + 1)
            return bank[b]

        def drained(eng, name):
            b, turn = job[name]
            eng.wait_ge(sem(f"bank_drained{b}"), turn + 1)

        def drain_sem(name):
            return sem(f"bank_drained{job[name][0]}"), job[name][1] + 1

        def na_head(u, i):
            return 4 * (u // 2) + u % 2 + 2 * i

        def key_place(which, g, i):
            return (2 * g + i // 2, i % 2) if which == "key1" else (4 * (g // 2) + i, g % 2)

        NORMS = ["mix0", "mix1", "meta", "ffn0", "ffn1", "ple0", "n10", "n20", "ple1", "n11", "n21", "f0", "f1"]
        norm_no = {n: i for i, n in enumerate(NORMS)}
        GAIN_COL = {"mix": 0, "meta": 2, "ple": 1, "n1": 2}
        GAIN_ROW = {"ffn": 0, "n2": 1, "f": 2}

        def norm_place(name):
            if name == "meta":
                return None, meta_x[0:META, :], meta_h[0:META, :], slice(0, META), META
            t = int(name[-1])
            return t, X[:, t, :], hn[:, t, :], slice(META + t * P, META + (t + 1) * P), P

        X_STATE = {"ffn0": 1, "ffn1": 2, "ple0": 3, "n10": 4, "n20": 5, "ple1": 6, "n11": 7, "n21": 8,
                   "f0": 9, "f1": 10}
        PHASE_TILE = [0, 1, 0, 1]
        PHASE_OPEN = [1, 3, 6, 9]

        BACK = {0: ["pick1"], 1: ["ple0", "n10", "proj0", "sb0", "gla0", "out0", "pick20"],
                2: ["ple1", "n11", "proj1", "sb1", "gla1", "out1", "pick21"], 3: ["final0"]}

        def segments(phase):
            steps = BACK[phase]
            cuts = [round(ITERS * (k + 1) / (len(steps) + 1)) for k in range(len(steps))]
            lo = 0
            for c, s in zip(cuts, steps):
                yield lo, c, s
                lo = c
            yield lo, ITERS, None

        block = ctx.enter_context(nc.Block())

        @block.tensor
        def _(pe):
            units = [0]

            def unit():
                n = units[0]
                units[0] += 1
                pe.wait_ge(sem(f"weights_in{n % WSLOTS}"), 16 * (n // WSLOTS + 1))
                return wring[:, n % WSLOTS, :]

            def begun(ins):
                ins.then_inc(sem("unit_begun"), 1)

            def open_bank(name):
                b = place(name)
                n, turn = job[name]
                if turn:
                    pe.wait_ge(sem(f"bank_drained{n}"), turn)
                return b

            def fill(ins, name):
                ins.then_inc(sem(f"bank_filled{job[name][0]}"), 1)

            def turn_rows(name, src, rows, chunks=DC):
                for half in range(-(-chunks // 4)):
                    b = open_bank((name, half))
                    n = min(4, chunks - 4 * half)
                    for i in range(n):
                        c = 4 * half + i
                        ins = nc.tensor.transpose(b[:, i * rows:(i + 1) * rows], src[:, c * P:(c + 1) * P],
                                                  ident[0:rows, 0:rows])
                    fill(ins, (name, half))

            def norm(name):
                _, _, rows, _, n = norm_place(name)
                pe.wait_ge(sem("rows_normed"), norm_no[name] + 1)
                turn_rows(name, rows, n)

            def to_rows(b, lo, w, cols, n_cols=256, rows=None, first=None):
                m = cols.stop - cols.start
                wv = w.rearrange("p (c n) -> p c n", c=DC)
                for c in range(DC):
                    ins = nc.tensor.matmul(b[0:m, lo:lo + n_cols], hT[:, c, cols], wv[:, c, :],
                                           start=(c == 0), stop=(c == DC - 1))
                    if c == 0 and first:
                        begun(ins)
                return ins

            def to_cols(b, w, cols, first=True, at=0):
                m = cols.stop - cols.start
                wv = w.rearrange("p (c n) -> p c n", c=DC)
                for ct in range(2):
                    for c in range(DC):
                        ins = nc.tensor.matmul(b[:, at + ct * m:at + (ct + 1) * m], wv[:, c, ct * P:(ct + 1) * P],
                                               hT[:, c, cols], start=(c == 0), stop=(c == DC - 1))
                        if first and ct == 0 and c == 0:
                            begun(ins)
                return ins

            tile_cols = [slice(META + t * P, META + (t + 1) * P) for t in range(TILES)]
            both = slice(META, META + SEQ)

            pe.wait_ge(sem("const_in"), 16)
            norm("mix0")
            norm("mix1")
            norm("meta")
            for t in range(TILES):
                drained(pe, (f"mix{t}", 1))
            for u in range(N_IN):
                w = unit()
                blk, side = divmod(u if u < N_IN - 8 else u + 1, 2)
                for t in range(TILES):
                    name = ("in", blk, t)
                    if side == 0:
                        open_bank(name)
                    ins = to_rows(bank[job[name][0]], 256 * side, w, tile_cols[t], first=(t == 0))
                    if side or u == N_IN - 9:
                        fill(ins, name)
            for t in range(TILES):
                pe.wait_ge(sem("qk_ready"), t + 1)
                turn_rows(("qkT", t), raw[:, t, :], P, PAIRS)
            for t in range(TILES):
                drained(pe, (("qkT", t), 4))
            for t in range(TILES):
                q_cols = slice(t * P, (t + 1) * P)

                def scores(u):
                    for i in range(2 if u < 4 else 3):
                        if u < 4:
                            qh, kh = na_head(u, i), NA_HEADS + na_head(u, i)
                        else:
                            qh = 2 * NA_HEADS + i * DIL_SLOTS + u - 4
                            kh = qh + DIL_HEADS
                        if i % 2 == 0:
                            b = open_bank(("score", t, u, i // 2))
                        e = HEAD * (qh % 2)
                        ins = nc.tensor.matmul(b[:, (i % 2) * SEQ:(i % 2 + 1) * SEQ], qkT[e:e + HEAD, qh // 2, q_cols],
                                               qkT[e:e + HEAD, kh // 2, :], start=True, stop=True)
                        if i == 1 or (u >= 4 and i == 2):
                            fill(ins, ("score", t, u, i // 2))

                def weigh(u):
                    n = t * 8 + u
                    pe.wait_ge(sem("prob_ready"), n + 1)
                    turn_rows(("probT", t, u), prob[n % 2], P, 4 if u < 4 else 6)
                    drained(pe, (("probT", t, u), 0 if u < 4 else 1))
                    if n in (0, 8):
                        drained(pe, ("in", 7, 1))
                        if n:
                            pe.wait_ge(sem("attn_ready"), 1)
                    pt = probT[:, n % 2, :]
                    for i in range(2 if u < 4 else 1):
                        blocks = 2 if u < 4 else 6
                        for k in range(blocks):
                            if u < 4:
                                h = na_head(u, i)
                                o, col = acc[:, 0, h * HEAD:(h + 1) * HEAD], h * HEAD
                                p = pt[:, (2 * i + k) * P:(2 * i + k + 1) * P]
                            else:
                                o = acc[:, 1, (u - 4) * HEAD:(u - 3) * HEAD]
                                col = (NA_HEADS + (k // 2) * DIL_SLOTS + u - 4) * HEAD
                                p = pt[:, k * P:(k + 1) * P]
                            ins = nc.tensor.matmul(o, p, val[:, k % 2, col:col + HEAD], start=(k == 0), stop=(k == blocks - 1))
                    ins.then_inc(sem("weighed"), 1)

                scores(0)
                for u in range(8):
                    if u + 1 < 8:
                        scores(u + 1)
                    weigh(u)
            for t in range(TILES):
                pe.wait_ge(sem("attn_ready"), t + 1)
                turn_rows(("attnT", t), attn[t], P, 6)
            for t in range(TILES):
                drained(pe, (("attnT", t), 1))
            for half in range(2):
                w = unit().rearrange("p (c n) -> p c n", c=4)
                for t in range(TILES):
                    b = open_bank(("na", half, t))
                    for c in range(4):
                        ins = nc.tensor.matmul(b[:, :], hT[:, c, tile_cols[t]], w[:, c, :], start=(c == 0), stop=(c == 3))
                        if c == 0 and t == 0:
                            begun(ins)
                    fill(ins, ("na", half, t))
            w = unit().rearrange("p (c n) -> p c n", c=2)
            for half in range(2):
                for t in range(TILES):
                    b = open_bank(("dil", half, t))
                    for c in range(2):
                        ins = nc.tensor.matmul(b[:, :], hT[:, 4 + c, tile_cols[t]], w[:, c, half * 512:(half + 1) * 512],
                                               start=(c == 0), stop=(c == 1))
                        if c == 0 and t == 0 and half == 0:
                            begun(ins)
                    fill(ins, ("dil", half, t))
            for t in range(TILES):
                pe.wait_ge(sem("merged"), t + 1)
                turn_rows(("mergedT", t), hn[:, t, :], P)
            for t in range(TILES):
                drained(pe, (("mergedT", t), 1))

            def project_out(name, tiles):
                for u in range(N_OUT):
                    w = unit()
                    for t in tiles:
                        if u % 2 == 0:
                            open_bank((name, u // 2, t))
                        b = bank[job[(name, u // 2, t)][0]]
                        ins = to_rows(b, 256 * (u % 2), w, tile_cols[t], first=(t == tiles[0]))
                        if u % 2:
                            fill(ins, (name, u // 2, t))

            project_out("out1", range(TILES))

            norm("ffn0")
            norm("ffn1")
            for t in range(TILES):
                drained(pe, (f"ffn{t}", 1))
            for h in range(PEER_HEADS):
                w = unit()
                b = open_bank(("query1", h))
                fill(to_cols(b, w, both), ("query1", h))

            def key_scores1(t):
                drained(pe, ("query1", PEER_HEADS - 1))
                for g in range(4):
                    b = open_bank(("key1", t, g))
                    for i in range(4):
                        ins = nc.tensor.matmul(b[:, i * P:(i + 1) * P], qpT[:, 4 * g + i, t * P:(t + 1) * P],
                                               keys1[:, i % 2, :], start=True, stop=True)
                    fill(ins, ("key1", t, g))

            def key_scores2(t):
                drained(pe, ("query2", t, 1))
                for g in range(4):
                    b = open_bank(("key2", t, g))
                    for i in range(4):
                        h, half = key_place("key2", g, i)
                        e = HEAD * half
                        ins = nc.tensor.matmul(b[:, i * P:(i + 1) * P], qpT[e:e + HEAD, h, 0:P], keys2[e:e + HEAD, h, :],
                                               start=True, stop=True)
                    fill(ins, ("key2", t, g))

            pe.wait_ge(sem("small_in"), SMALL_IN)
            key_scores1(0)

            def ple(t):
                norm(f"ple{t}")
                drained(pe, (f"ple{t}", 1))
                for u in range(4):
                    w = unit()
                    name = ("ple_gate", t, u // 2)
                    if u % 2 == 0:
                        open_bank(name)
                    ins = to_rows(bank[job[name][0]], 256 * (u % 2), w, tile_cols[t], first=True)
                    if u % 2:
                        fill(ins, name)
                w = unit().rearrange("p (c n) -> p c n", c=2)
                for half in range(2):
                    b = open_bank(("ple", t, half))
                    for c in range(2):
                        ins = nc.tensor.matmul(b[:, :], pT[:, c, t * P:(t + 1) * P], w[:, c, half * 512:(half + 1) * 512],
                                               start=(c == 0), stop=(c == 1))
                        if c == 0 and half == 0:
                            begun(ins)
                    fill(ins, ("ple", t, half))

            def block2_cols(t):
                return slice(0, META + P) if t == 0 else tile_cols[t]

            def proj(t):
                kc = block2_cols(t)
                drained(pe, (f"n1{t}", 1))
                for i in range(2):
                    fill(to_cols(open_bank(("sbk", t, i)), unit(), kc), ("sbk", t, i))
                b = open_bank(("sbq", t))
                for i in range(2):
                    ins = to_cols(b, unit(), tile_cols[t], at=2 * P * i)
                fill(ins, ("sbq", t))
                b = open_bank(("lr", t))
                n = kc.stop - kc.start
                for c in range(DC):
                    ins = nc.tensor.matmul(b[0:RANK, 0:n], w_lr[:, c, :], hT[:, c, kc], start=(c == 0), stop=(c == DC - 1))
                fill(ins, ("lr", t))
                fill(to_cols(open_bank(("gk", t)), unit(), kc), ("gk", t))
                fill(to_cols(open_bank(("gq", t)), unit(), tile_cols[t]), ("gq", t))
                drained(pe, ("lr", t))
                b = open_bank(("z", t))
                ins = nc.tensor.matmul(b[:, 0:256], lrT[0:RANK + 1, META:META + P], w_gu[0:RANK + 1, :], start=True, stop=True)
                fill(ins, ("z", t))
                if t == 0:
                    b = open_bank("z_meta")
                    ins = nc.tensor.matmul(b[0:META, 0:256], lrT[0:RANK + 1, 0:META], w_gu[0:RANK + 1, :], start=True, stop=True)
                    fill(ins, "z_meta")
                for name in ("sbv", "gv", "gr"):
                    meta = t == 0 and name != "gr"
                    b = open_bank((name, t))
                    bm = open_bank((name, "meta")) if meta else None
                    for i in range(2):
                        w = unit()
                        ins = to_rows(b, 256 * i, w, tile_cols[t], first=True)
                        if i == 1:
                            fill(ins, (name, t))
                        if meta:
                            ins = to_rows(bm, 256 * i, w, slice(0, META))
                            if i == 1:
                                fill(ins, (name, "meta"))

            def key_blocks(t):
                out = [(slice(0, META), 0, META)]
                return out + [(tile_cols[k], 1 + k, P) for k in range(t + 1)]

            def stick(t):
                drained(pe, ("sbq", t))
                drained(pe, ("sbk", t, 1))
                drained(pe, ("sbv", t))
                if t == 0:
                    drained(pe, ("sbv", "meta"))
                kbs = key_blocks(t)
                out_bank = None
                for hg in range(2):
                    for k, (cols, _, n) in enumerate(kbs):
                        b = open_bank(("stick_z", t, hg, k))
                        for i in range(4):
                            e = HEAD * hg
                            ins = nc.tensor.matmul(b[0:n, i * P:(i + 1) * P], sbk[e:e + HEAD, i, cols],
                                                   sbq[e:e + HEAD, i, :], start=True, stop=True)
                        fill(ins, ("stick_z", t, hg, k))
                    for k, (cols, _, n) in reversed(list(enumerate(kbs))):
                        b = open_bank(("stick_w", t, hg, k))
                        if k == len(kbs) - 1:
                            nc.tensor.matmul(b[0:n, :], ident, cst("causal_neg").unsqueeze(1).to_broadcast([P, 4, P]), start=True, stop=False)
                        pe.wait_ge(sem("stick_log"), STICK_BASE[t] + hg * len(kbs) + len(kbs) - k)
                        for later in range(k + 1, len(kbs)):
                            nc.tensor.matmul(b[0:n, :], cst("ones")[:, 0:n], sb_log[:, later, :], start=(later == k + 1), stop=False)
                        for i in range(4):
                            e = HEAD * hg
                            nc.tensor.matmul(b[0:n, i * P:(i + 1) * P], sbk[e:e + HEAD, i, cols],
                                             sbq[e:e + HEAD, i, :], start=False, stop=False)
                        ins = nc.tensor.matmul(b[0:n, :], cst("later", n)[:, 0:n], sb_log[0:n, k, :], start=False, stop=True)
                        fill(ins, ("stick_w", t, hg, k))
                    if hg == 0:
                        out_bank = open_bank(("stick_o", t))
                    for k in range(len(kbs)):
                        drained(pe, ("stick_w", t, hg, k))
                    for i in range(4):
                        h = 2 * i + hg
                        for k, (_, vi, n) in enumerate(kbs):
                            ins = nc.tensor.matmul(out_bank[:, h * HEAD:(h + 1) * HEAD], sb_a[0:n, k, i * P:(i + 1) * P],
                                                   sbv[0:n, vi, h * HEAD:(h + 1) * HEAD],
                                                   start=(k == 0), stop=(k == len(kbs) - 1))
                    if hg == 0:
                        ins.then_inc(sem("stick_half"), 1)
                    else:
                        fill(ins, ("stick_o", t))

            def gla(t):
                drained(pe, ("gv", t))
                if t == 0:
                    drained(pe, ("gv", "meta"))
                    pe.wait_ge(sem("log_decay_meta"), 1)
                    b = open_bank("decay_meta")
                    for dt in range(2):
                        ins = nc.tensor.matmul(b[:, dt * META:(dt + 1) * META], lg_m[0:META, dt * P:(dt + 1) * P],
                                               cst("decay_meta", META), start=True, stop=True)
                    fill(ins, "decay_meta")
                    pe.wait_ge(sem("key_meta"), 1)
                    b = open_bank("klast_meta")
                    for dt in range(2):
                        ins = nc.tensor.transpose(b[0:META, dt * P:(dt + 1) * P], klm[:, dt, :], ident)
                    fill(ins, "klast_meta")
                    drained(pe, "klast_meta")
                    b = open_bank("state_meta")
                    for h in range(GLA_HEADS):
                        ins = nc.tensor.matmul(b[:, h * P:(h + 1) * P], klast[0:META, h // 2, :], gvm[0:META, h * P:(h + 1) * P],
                                               start=True, stop=True)
                    fill(ins, "state_meta")
                pe.wait_ge(sem("log_decay"), t + 1)
                out_bank = open_bank(("gla_o", t))
                for dt in range(2):
                    for i in range(3):
                        b = open_bank(("decay", t, dt, i))
                        n = min(512, (LEVELS + 2) * P - 512 * i)
                        ins = nc.tensor.matmul(b[:, 0:n], lg[:, dt * P:(dt + 1) * P], decay[:, 512 * i:512 * i + n],
                                               start=True, stop=True)
                        fill(ins, ("decay", t, dt, i))
                    pe.wait_ge(sem("gla_qk"), 2 * t + dt + 1)
                    if t == 0:
                        b = open_bank(("klast", t, dt))
                        fill(nc.tensor.transpose(b[:, 0:P], gla_k[:, LEVELS, :], ident), ("klast", t, dt))
                    for h in (2 * dt, 2 * dt + 1):
                        e = HEAD * (h % 2)
                        for half in range(2):
                            b = open_bank(("gla_a", t, h, half))
                            for i in range(4):
                                level = 4 * half + i
                                ins = nc.tensor.matmul(b[:, i * P:(i + 1) * P], gla_k[e:e + HEAD, level, :],
                                                       gla_q[e:e + HEAD, level, :], start=True, stop=True)
                            fill(ins, ("gla_a", t, h, half))
                        drained(pe, ("gla_a", t, h, 1))
                        if h == 0:
                            drained(pe, "state0" if t else "state_meta")
                        o = out_bank[:, h * P:(h + 1) * P]
                        for level in range(LEVELS):
                            nc.tensor.matmul(o, gla_a[:, level, :], gv[:, h * P:(h + 1) * P], start=(level == 0), stop=False)
                        ins = nc.tensor.matmul(o, gla_q[e:e + HEAD, INTER, :], state[e:e + HEAD, dt, :], start=False, stop=True)
                        if h == GLA_HEADS - 1:
                            fill(ins, ("gla_o", t))
                        else:
                            ins.then_inc(sem("gla_head"), 1)
                if t == 0:
                    drained(pe, ("klast", t, 1))
                    b = open_bank("state0")
                    for h in range(GLA_HEADS):
                        ins = nc.tensor.matmul(b[:, h * P:(h + 1) * P], klast[:, h // 2, :], gv[:, h * P:(h + 1) * P],
                                               start=True, stop=True)
                    fill(ins, "state0")

            def mixed_out(t):
                pe.wait_ge(sem("mixed"), t + 1)
                turn_rows(("mixedT", t), hn[:, t, :], P)
                drained(pe, (("mixedT", t), 1))
                project_out("out2", [t])

            def pick2(t):
                norm(f"n2{t}")
                drained(pe, (f"n2{t}", 1))
                for i in range(2):
                    b = open_bank(("query2", t, i))
                    for k in range(2):
                        ins = to_cols(b, unit(), tile_cols[t], at=2 * P * k)
                    fill(ins, ("query2", t, i))
                key_scores2(t)

            def background(step):
                t = int(step[-1])
                if step == "pick1":
                    key_scores1(1)
                elif step.startswith("ple"):
                    ple(t)
                elif step.startswith("n1"):
                    norm(step)
                elif step.startswith("proj"):
                    proj(t)
                elif step.startswith("sb"):
                    stick(t)
                elif step.startswith("gla"):
                    gla(t)
                elif step.startswith("out"):
                    mixed_out(t)
                elif step.startswith("pick2"):
                    pick2(t)

            for phase in range(PHASES):
                tile = PHASE_TILE[phase]
                pe.wait_ge(sem("x_ready"), PHASE_OPEN[phase])
                if phase == 0:
                    pe.wait_ge(sem("attn_ready"), 2)
                for half in range(2):
                    nc.tensor.matmul(acc[:, half, :], ident, X[:, tile, half * 512:(half + 1) * 512], start=True, stop=False)
                for lo, hi, step in segments(phase):
                    with pe.Fori(phase * ITERS + lo, phase * ITERS + hi) as it:
                        for s in range(RING):
                            pe.wait_ge(sem("diag_ready"), it * RING + s + 1)
                            for half in range(2):
                                ins = nc.tensor.matmul(acc[:, half, :], diag[:, s, :],
                                                       ring[:, s, D + half * 512:D + (half + 1) * 512],
                                                       start=False, stop=False)
                            ins.then_inc(sem("slot_free"), 1)
                    if step:
                        background(step)
                for half in range(2):
                    ins = nc.tensor.matmul(acc[:, half, :], zeros, X[:, tile, half * 512:(half + 1) * 512], start=False, stop=True)
                ins.then_inc(sem("peer_sum"), 1)

        @block.gpsimd
        def _(pool):
            nc.gpsimd.memset(fence[:, :], 0.0).then_inc(sem("fence_set"), 1)
            pool.wait_ge(sem("fence_set"), 1)

            def gather(table, tile, it, i, s):
                nc.gpsimd.tensor_copy(slot_idx[:, s:s + 1], eidx[:, tile, bass.ds(i * RING + s, 1)]).then_inc(sem("idx_copied"), 1)
                pool.wait_ge(sem("idx_copied"), it * RING + s + 1)
                nc.gpsimd.tensor_tensor(fence[:, :], fence[:, :], fence[:, :], ALU.add)
                nc.gpsimd.indirect_dma_start(
                    out=ring[:, s, :], out_offset=None, in_=table,
                    in_offset=bass.IndirectOffsetOnAxis(ap=slot_idx[:, s:s + 1], axis=0)).then_inc(sem(f"row_in{s}"), 16)

            for phase in range(PHASES):
                tile = PHASE_TILE[phase]
                table = a["experts1"] if phase < 2 else a["experts2"]
                pool.wait_ge(sem("experts_picked"), phase + 1)
                if phase == 0:
                    pool.wait_ge(sem("merged"), 2)
                    for s in range(RING):
                        gather(table, tile, 0, 0, s)
                with pool.Fori(1 if phase == 0 else 0, ITERS) as i:
                    for s in range(RING):
                        pool.wait_ge(sem("slot_free"), (i + phase * ITERS) * RING + s + 1 - RING)
                        pool.wait_ge(sem("experts_picked"), phase + 1)
                        gather(table, tile, i + phase * ITERS, i, s)

        @block.sync
        def _(sp):
            sp.dma_start(X[:, 0, :], a["x"][0:P, :]).then_inc(sem("x_in"), 16)
            sp.dma_start(X[:, 1, :], a["x"][P:SEQ, :]).then_inc(sem("x_in"), 16)

            def load(n, s, at):
                sp.dma_start(wring[:, s, :], a["weights"][at]).then_inc(sem(f"weights_in{s}"), 16)

            for s in range(WSLOTS):
                load(s, s, s)
            turns = N_UNITS // WSLOTS
            with sp.Fori(1, turns) as i:
                for s in range(WSLOTS):
                    sp.wait_ge(sem("unit_begun"), i * WSLOTS + s - WSLOTS + 2)
                    load(None, s, i * WSLOTS + s)
            for n in range(turns * WSLOTS, (turns + 1) * WSLOTS):
                sp.wait_ge(sem("unit_begun"), n - WSLOTS + 2)
                load(n, n % WSLOTS, n if n < N_UNITS else n - N_TILE)
            with sp.Fori(turns + 1, N_LOADS // WSLOTS) as i:
                for s in range(WSLOTS):
                    sp.wait_ge(sem("unit_begun"), i * WSLOTS + s - WSLOTS + 2)
                    load(None, s, i * WSLOTS + s - N_TILE)
            for t in range(TILES):
                sp.wait_ge(sem("rows_normed"), norm_no[f"f{t}"] + 1)
                sp.dma_start(out[t * P:(t + 1) * P, :], hn[:, t, :]).then_inc(sem("out_written"), 16)
            sp.wait_ge(sem("out_written"), 32)

        @block.scalar
        def _(act):
            steps = [0]

            def step(ins):
                ins.then_inc(sem("act_step"), 1)
                steps[0] += 1
                act.wait_ge(sem("act_step"), steps[0])

            def drain(ins, name):
                s, _ = drain_sem(name)
                ins.then_inc(s, 1)

            act.dma_start(const[:, :], a["const"]).then_inc(sem("const_in"), 16)
            act.dma_start(gain_col[:, :, :], a["gain_col"]).then_inc(sem("gains_in"), 16)
            act.dma_start(qk_gain[:, :, :], a["qk_gain"].partition_broadcast(P)).then_inc(sem("gains_in"), 16)
            act.dma_start(meta_x[0:META, :], a["meta"]).then_inc(sem("meta_in"), 16)
            act.dma_start(na_bias, a["na_bias"]).then_inc(sem("masks_in"), 16)
            act.dma_start(dil_mask, a["dil_mask"]).then_inc(sem("masks_in"), 16)
            small = [(gain[:, :, :], a["gain"].partition_broadcast(P)), (head_gain[:, :, :], a["head_gain"].partition_broadcast(P)),
                     (keys1[:, :, :], a["keys1"]), (keys2[:, :, :], a["keys2"]), (pT[:, :, :], a["pT"]),
                     (w_lr[:, :, :], a["w_lr"]), (w_gu[0:RANK + 1, :], a["w_gu"])]
            for dst, src in small:
                act.dma_start(dst, src).then_inc(sem("small_in"), 16)
            assert SMALL_IN == 16 * len(small)

            def inv_rms(v, width, last=None):
                step(nc.scalar.activation(v, v, ACT.Ln, scale=1.0 / width, bias=EPS))
                ins = nc.scalar.activation(v, v, ACT.Exp, scale=-0.5)
                if last:
                    ins.then_inc(sem(last), 1)
                else:
                    step(ins)

            def norm(name):
                _, x, rows, cols, n = norm_place(name)
                k = norm_no[name]
                if name in X_STATE:
                    act.wait_ge(sem("x_ready"), X_STATE[name])
                elif name == "meta":
                    act.wait_ge(sem("meta_in"), 16)
                else:
                    act.wait_ge(sem("x_in"), 32)
                v = stat[0:n, k:k + 1]
                step(nc.scalar.activation(rows, x, ACT.Square, accum_out=v))
                inv_rms(v, D, "inv_rms")
                if name[:-1] == "ffn" or name[:-1] == "n2":
                    turned(name, cols)

            def turned(name, cols, chunks=DC):
                for half in range(-(-chunks // 4)):
                    b = filled(act, (name, half))
                    n = min(4, chunks - 4 * half)
                    drain(nc.scalar.copy(hT[:, 4 * half:4 * half + n, cols],
                                         b[:, 0:n * P].rearrange("p (c t) -> p c t", c=n)), (name, half))

            tile_cols = [slice(META + t * P, META + (t + 1) * P) for t in range(TILES)]
            for name in ("mix0", "mix1", "meta"):
                norm(name)
            for blk in range(12):
                for t in range(TILES):
                    if blk < 5:
                        b = filled(act, ("in", blk, t))
                        if blk or t:
                            act.wait_ge(sem("squares_summed"), 2 * blk + t)
                        step(nc.scalar.activation(sq, b[:, :], ACT.Square))
                        drain(nc.scalar.copy(raw[:, t, blk * 512:(blk + 1) * 512], b[:, :]), ("in", blk, t))
                    elif blk >= 8:
                        b = filled(act, ("in", blk, t))
                        drain(nc.scalar.activation(sig[:, t, (blk - 8) * 512:(blk - 7) * 512], b[:, :], ACT.Sigmoid), ("in", blk, t))
            for t in range(TILES):
                act.wait_ge(sem("squares_summed"), 10)
                inv_rms(hstat[:, t, :], HEAD, "qk_inv_rms")
            for t in range(TILES):
                for j in range(5):
                    b = filled(act, (("qkT", t), j))
                    drain(nc.scalar.copy(qkT[:, 4 * j:4 * j + 4, t * P:(t + 1) * P],
                                         b[:, :].rearrange("p (c t) -> p c t", c=4)), (("qkT", t), j))
            for t in range(TILES):
                for u in range(8):
                    n = 8 * t + u
                    act.wait_ge(sem("score_max"), n + 1)
                    p = prob[n % 2]
                    if u < 4:
                        for i in range(2):
                            v = p[:, i * SEQ:(i + 1) * SEQ]
                            ins = nc.scalar.activation(v, v, ACT.Exp, bias=amax[:, 2 * (n % 2) + i:2 * (n % 2) + i + 1],
                                                       accum_out=asum[:, t, na_head(u, i):na_head(u, i) + 1])
                            if i == 0:
                                step(ins)
                    else:
                        ins = nc.scalar.activation(p, p, ACT.Exp, bias=amax[:, 2 * (n % 2):2 * (n % 2) + 1],
                                                   accum_out=asum[:, t, 4 + u:5 + u])
                    ins.then_inc(sem("prob_ready"), 1)
                    for half in range(1 if u < 4 else 2):
                        b = filled(act, (("probT", t, u), half))
                        if half == 0 and n >= 2:
                            act.wait_ge(sem("weighed"), n - 1)
                        w = 512 if half == 0 else 256
                        drain(nc.scalar.copy(probT[:, n % 2, 512 * half:512 * half + w], b[:, 0:w]), (("probT", t, u), half))
            for t in range(TILES):
                turned(("attnT", t), tile_cols[t], 6)
            for t in range(TILES):
                turned(("mergedT", t), tile_cols[t])
            norm("ffn0")
            norm("ffn1")
            for h in range(PEER_HEADS):
                b = filled(act, ("query1", h))
                drain(nc.scalar.copy(qpT[:, 2 * h:2 * h + 2, :], b[:, :].rearrange("p (c t) -> p c t", c=2)), ("query1", h))

            def pick(phase):
                act.wait_ge(sem("top_shifted"), phase + 1)
                nc.scalar.activation(top_exp, top_exp, ACT.Exp).then_inc(sem("top_exp"), 1)

            pick(0)

            def ple(t):
                norm(f"ple{t}")
                for half in range(2):
                    b = filled(act, ("ple_gate", t, half))
                    drain(nc.scalar.activation(ple_gate[:, half * 512:(half + 1) * 512], b[:, :], ACT.Sigmoid), ("ple_gate", t, half))

            def log_sigmoid(name, rows, dst, signal):
                b = filled(act, name)
                step(nc.scalar.activation(dst, b[0:rows, 0:256], ACT.Abs))
                step(nc.scalar.activation(dst, dst, ACT.Exp, scale=-1.0))
                nc.scalar.activation(dst, dst, ACT.Ln, bias=1.0).then_inc(sem(signal), 1)

            def proj(t):
                n = META + P if t == 0 else P
                at = 0 if t == 0 else META + P
                for i in range(2):
                    b = filled(act, ("sbk", t, i))
                    drain(nc.scalar.copy(sbk[:, 2 * i:2 * i + 2, at:at + n],
                                         b[:, 0:2 * n].rearrange("p (c t) -> p c t", c=2)), ("sbk", t, i))
                b = filled(act, ("sbq", t))
                drain(nc.scalar.mul(sbq, b[:, :].rearrange("p (c t) -> p c t", c=4), HEAD ** -0.5), ("sbq", t))
                b = filled(act, ("lr", t))
                act.wait_ge(sem("ones_set"), t + 1)
                drain(nc.scalar.copy(lrT[0:RANK, META + P - n:META + P], b[0:RANK, 0:n]), ("lr", t))
                b = filled(act, ("gk", t))
                drain(nc.scalar.copy(gkT[:, :, META + P - n:META + P], b[:, 0:2 * n].rearrange("p (c t) -> p c t", c=2)), ("gk", t))
                b = filled(act, ("gq", t))
                drain(nc.scalar.mul(gqT, b[:, 0:2 * P].rearrange("p (c t) -> p c t", c=2), GLA_DK ** -0.5), ("gq", t))
                log_sigmoid(("z", t), P, lg, "log_gate")
                if t == 0:
                    log_sigmoid("z_meta", META, lg_m[0:META, :], "log_gate_meta")
                for name, dst, dst_m in (("sbv", sbv[:, 1 + t, :], sbv[0:META, 0, :]), ("gv", gv[:, :], gvm[0:META, :])):
                    b = filled(act, (name, t))
                    drain(nc.scalar.copy(dst, b[:, :]), (name, t))
                    if t == 0:
                        b = filled(act, (name, "meta"))
                        drain(nc.scalar.copy(dst_m, b[0:META, :]), (name, "meta"))
                b = filled(act, ("gr", t))
                nc.scalar.activation(silu, b[:, :], ACT.Sigmoid).then_inc(sem("gr_sigmoid"), 1)

            def stick(t):
                nkb = t + 2
                for hg in range(2):
                    for k in reversed(range(nkb)):
                        n = META if k == 0 else P
                        tmp = sb_tmp[0:n, k % 2, :]
                        b = filled(act, ("stick_z", t, hg, k))
                        if hg * nkb + nkb - k > 2:
                            act.wait_ge(sem("stick_log"), STICK_BASE[t] + hg * nkb + nkb - k - 2)
                        step(nc.scalar.activation(tmp, b[0:n, :], ACT.Abs))
                        step(nc.scalar.activation(tmp, tmp, ACT.Exp, scale=-1.0))
                        nc.scalar.activation(tmp, tmp, ACT.Ln, bias=1.0).then_inc(sem("stick_soft"), 1)
                    for k in reversed(range(nkb)):
                        n = META if k == 0 else P
                        if hg:
                            act.wait_ge(sem("stick_half"), t + 1)
                        b = filled(act, ("stick_w", t, hg, k))
                        drain(nc.scalar.activation(sb_a[0:n, k, :], b[0:n, :], ACT.Exp), ("stick_w", t, hg, k))

            def gla(t):
                if t == 0:
                    b = filled(act, "decay_meta")
                    drain(nc.scalar.activation(klm, b[:, 0:2 * META].rearrange("p (c t) -> p c t", c=2), ACT.Exp), "decay_meta")
                    b = filled(act, "klast_meta")
                    drain(nc.scalar.copy(klast[0:META, :, :], b[0:META, 0:2 * P].rearrange("p (c t) -> p c t", c=2)), "klast_meta")
                for dt in range(2):
                    if dt:
                        act.wait_ge(sem("gla_qk"), 2 * t + 1)
                    for i in range(3):
                        n = min(512, (LEVELS + 2) * P - 512 * i)
                        b = filled(act, ("decay", t, dt, i))
                        drain(nc.scalar.activation(expd[:, 512 * i:512 * i + n], b[:, 0:n], ACT.Exp), ("decay", t, dt, i))
                    if t == 0:
                        b = filled(act, ("klast", t, dt))
                        if dt == 0:
                            filled(act, "state_meta")
                        drain(nc.scalar.copy(klast[:, dt, :], b[:, 0:P]), ("klast", t, dt))

            def head_norms(t):
                act.wait_ge(sem("mix_squares"), t + 1)
                inv_rms(hstat[:, 0, 0:SB_HEADS], HEAD, "")
                inv_rms(hstat[:, 1, 0:GLA_HEADS], GLA_DV, "mix_inv_rms")

            def background(s):
                t = int(s[-1])
                if s == "pick1":
                    pick(1)
                elif s.startswith("ple"):
                    ple(t)
                elif s.startswith("n1"):
                    norm(s)
                elif s.startswith("proj"):
                    proj(t)
                elif s.startswith("sb"):
                    stick(t)
                elif s.startswith("gla"):
                    gla(t)
                elif s.startswith("out"):
                    head_norms(t)
                    turned(("mixedT", t), tile_cols[t])
                elif s.startswith("pick2"):
                    norm(f"n2{t}")
                    for i in range(2):
                        b = filled(act, ("query2", t, i))
                        drain(nc.scalar.copy(qpT[:, 4 * i:4 * i + 4, 0:P], b[:, :].rearrange("p (c t) -> p c t", c=4)), ("query2", t, i))
                    pick(2 + t)
                elif s == "final0":
                    norm("f0")

            for phase in range(PHASES):
                for lo, hi, s_ in segments(phase):
                    with act.Fori(phase * ITERS + lo, phase * ITERS + hi) as it:
                        for j in range(RING // CHUNK):
                            c = slice(CHUNK * j, CHUNK * (j + 1))
                            act.wait_ge(sem("dots"), it * RING + CHUNK * (j + 1))
                            nc.scalar.activation(act_dot[:, c], dot[:, c], ACT.Gelu).then_inc(sem("gelu"), 1)
                            act.wait_ge(sem("weights_ready"), it * (RING // CHUNK) + j + 1)
                            for s in range(CHUNK * j, CHUNK * (j + 1)):
                                nc.scalar.activation(diag[:, s, :], ident, ACT.Copy, scale=weight[:, s:s + 1]).then_inc(sem("diag_ready"), 1)
                    if s_:
                        background(s_)
            norm("f1")

        @block.vector
        def _(dve):
            steps = [0]

            def step(ins):
                ins.then_inc(sem("dve_step"), 1)
                steps[0] += 1
                dve.wait_ge(sem("dve_step"), steps[0])

            def drain(ins, name):
                s, n = drain_sem(name)
                ins.then_inc(s, 1)
                dve.wait_ge(s, n)

            def norm(name):
                _, x, rows, cols, n = norm_place(name)
                k = norm_no[name]
                dve.wait_ge(sem("inv_rms"), k + 1)
                kind = name if name == "meta" else name[:-1]
                if kind in GAIN_ROW:
                    if kind == "ffn":
                        dve.wait_ge(sem("small_in"), SMALL_IN)
                    ins = nc.vector.scalar_tensor_tensor(out=rows, in0=x, scalar=stat[0:n, k:k + 1],
                                                         in1=gain[:, GAIN_ROW[kind], :], op0=ALU.mult, op1=ALU.mult)
                    ins.then_inc(sem("rows_normed"), 1)
                    return
                nc.vector.tensor_scalar(rows, x, stat[0:n, k:k + 1], None, ALU.mult).then_inc(sem("rows_normed"), 1)
                g = gain_col[:, GAIN_COL[kind], :]
                if kind == "mix":
                    dve.wait_ge(sem("gains_in"), 32)
                for half in range(2):
                    b = filled(dve, (name, half))
                    drain(nc.vector.tensor_tensor(hT[:, 4 * half:4 * half + 4, cols],
                                                  b[:, 0:4 * n].rearrange("p (c t) -> p c t", c=4),
                                                  g[:, 4 * half:4 * half + 4].unsqueeze(2).to_broadcast([P, 4, n]), ALU.mult), (name, half))

            dve.wait_ge(sem("const_in"), 16)
            for name in ("mix0", "mix1", "meta"):
                norm(name)
            dve.wait_ge(sem("masks_in"), 32)
            bias = na_bias.rearrange("p h (j k) -> p (h j) k", k=GRID_W)
            step(nc.vector.tensor_tensor(bias, bias, cst("na_cols").unsqueeze(1).to_broadcast([P, NA_HEADS * 6, GRID_W]), ALU.add))
            for blk in range(8):
                for t in range(TILES):
                    if blk < 5:
                        b_, turn = job[("in", blk, t)]
                        dve.wait_ge(sem(f"bank_drained{b_}"), turn + 1)
                        nc.vector.tensor_reduce(hstat[:, t, 8 * blk:8 * blk + 8], sq.rearrange("p (h d) -> p h d", d=HEAD),
                                                AX.X, ALU.add).then_inc(sem("squares_summed"), 1)
                    else:
                        n = 512 if blk < 7 else 256
                        b = filled(dve, ("in", blk, t))
                        drain(nc.vector.tensor_copy(val[:, t, (blk - 5) * 512:(blk - 5) * 512 + n], b[:, 0:n]), ("in", blk, t))
            for t in range(TILES):
                dve.wait_ge(sem("qk_inv_rms"), t + 1)
                r = raw[:, t, :].rearrange("p (h d) -> p h d", d=HEAD)
                step(nc.vector.tensor_tensor(r, r, hstat[:, t, :].unsqueeze(2).to_broadcast([P, QK_HEADS, HEAD]), ALU.mult))
                at = 0
                for k, heads in enumerate((NA_HEADS, NA_HEADS, DIL_HEADS, DIL_HEADS)):
                    v = r[:, at:at + heads, :]
                    step(nc.vector.tensor_tensor(v, v, qk_gain[:, k, :].unsqueeze(1).to_broadcast([P, heads, HEAD]), ALU.mult))
                    at += heads
                x1 = r[:, 2 * NA_HEADS:, 0:ROT_HALF]
                x2 = r[:, 2 * NA_HEADS:, ROT_HALF:2 * ROT_HALF]
                rope = cst("rope")[:, t * 2 * ROT_HALF:(t + 1) * 2 * ROT_HALF]
                cos, sin = [rope[:, k * ROT_HALF:(k + 1) * ROT_HALF].unsqueeze(1).to_broadcast([P, 2 * DIL_HEADS, ROT_HALF]) for k in range(2)]
                p = [rot[:, k, :].rearrange("p (h d) -> p h d", d=ROT_HALF) for k in range(4)]
                for dst, u, v in ((p[0], x1, cos), (p[1], x2, sin), (p[2], x2, cos), (p[3], x1, sin)):
                    step(nc.vector.tensor_tensor(dst, u, v, ALU.mult))
                step(nc.vector.tensor_tensor(x1, p[0], p[1], ALU.subtract))
                nc.vector.tensor_tensor(x2, p[2], p[3], ALU.add).then_inc(sem("qk_ready"), 1)
            for t in range(TILES):
                for u in range(8):
                    n = 8 * t + u
                    if n >= 2:
                        filled(dve, (("probT", (n - 2) // 8, (n - 2) % 8), 0 if (n - 2) % 8 < 4 else 1))
                    p = prob[n % 2]
                    m = amax[:, 2 * (n % 2):2 * (n % 2) + 2]
                    if u < 4:
                        b = filled(dve, ("score", t, u, 0))
                        j = 2 - 2 * t
                        pv = p[:, 0:512].rearrange("p (h k) -> p h k", h=2)
                        drain(nc.vector.scalar_tensor_tensor(out=pv, in0=b[:, :].rearrange("p (h k) -> p h k", h=2), scalar=HEAD ** -0.5,
                                                             in1=na_bias[:, na_head(u, 0):na_head(u, 1) + 1:2, j * GRID_W:(j + 4) * GRID_W],
                                                             op0=ALU.mult, op1=ALU.add), ("score", t, u, 0))
                        nc.vector.tensor_reduce(m, pv, AX.X, ALU.max, negate=True).then_inc(sem("score_max"), 1)
                    else:
                        for half in range(2):
                            w = 512 if half == 0 else 256
                            c = slice(512 * half, 512 * half + w)
                            b = filled(dve, ("score", t, u, half))
                            drain(nc.vector.scalar_tensor_tensor(out=p[:, c], in0=b[:, 0:w], scalar=HEAD ** -0.5, in1=dil_mask[:, t, c],
                                                                 op0=ALU.mult, op1=ALU.add), ("score", t, u, half))
                        nc.vector.tensor_reduce(m[:, 0:1], p, AX.X, ALU.max, negate=True).then_inc(sem("score_max"), 1)
                dve.wait_ge(sem("weighed"), 8 * (t + 1))
                step(nc.vector.reciprocal(arec[:, 0:12], asum[:, t, 0:12]))
                step(nc.vector.tensor_tensor(attn[t][:, 0:512].rearrange("p (h d) -> p h d", d=HEAD),
                                             acc[:, 0, :].rearrange("p (h d) -> p h d", d=HEAD),
                                             arec[:, 0:8].unsqueeze(2).to_broadcast([P, 8, HEAD]), ALU.mult))
                ins = nc.vector.tensor_tensor(attn[t][:, 512:768].rearrange("p (h d) -> p h d", d=HEAD),
                                              acc[:, 1, 0:256].rearrange("p (h d) -> p h d", d=HEAD),
                                              arec[:, 8:12].unsqueeze(2).to_broadcast([P, 4, HEAD]), ALU.mult)
                ins.then_inc(sem("attn_ready"), 1)
            for half in range(2):
                c = slice(512 * half, 512 * half + 512)
                for t in range(TILES):
                    b = filled(dve, ("na", half, t))
                    drain(nc.vector.tensor_tensor(hn[:, t, c], sig[:, t, c], b[:, :], ALU.mult), ("na", half, t))
            for half in range(2):
                c = slice(512 * half, 512 * half + 512)
                for t in range(TILES):
                    b = filled(dve, ("dil", half, t))
                    g = sig[:, t, D + 512 * half:D + 512 * half + 512]
                    drain(nc.vector.tensor_tensor(g, g, b[:, :], ALU.mult), ("dil", half, t))
                    ins = nc.vector.tensor_tensor(hn[:, t, c], hn[:, t, c], g, ALU.add)
                    if half:
                        ins.then_inc(sem("merged"), 1)

            def residual(name, t):
                for half in range(2):
                    c = slice(512 * half, 512 * half + 512)
                    b = filled(dve, (name, half, t))
                    drain(nc.vector.tensor_tensor(X[:, t, c], X[:, t, c], b[:, :], ALU.add), (name, half, t))
                nc.vector.tensor_copy(amax[:, 12:13], X[:, t, 0:1]).then_inc(sem("x_ready"), 1)

            for half in range(2):
                for t in range(TILES):
                    c = slice(512 * half, 512 * half + 512)
                    b = filled(dve, ("out1", half, t))
                    drain(nc.vector.tensor_tensor(X[:, t, c], X[:, t, c], b[:, :], ALU.add), ("out1", half, t))
                    if half:
                        nc.vector.tensor_copy(amax[:, 12:13], X[:, t, 0:1]).then_inc(sem("x_ready"), 1)
            norm("ffn0")
            norm("ffn1")

            def top16(src, gone_, v, i):
                step(nc.vector.max(v[:, 0:8], src))
                step(nc.vector.max_index(i[:, 0:8], v[:, 0:8], src))
                step(nc.vector.match_replace(gone_, v[:, 0:8], src, -3.0e38))
                step(nc.vector.max(v[:, 8:16], gone_))
                step(nc.vector.max_index(i[:, 8:16], v[:, 8:16], gone_))

            def pick(phase):
                t = PHASE_TILE[phase]
                which = "key1" if phase < 2 else "key2"
                u = {n: v.bitcast(U32) for n, v in tk.items()}
                for g in range(4):
                    b = filled(dve, (which, t, g))
                    for i in range(4):
                        h, half = key_place(which, g, i)
                        v, ix = ("v1", "i1") if half == 0 else ("v2", "i2")
                        top16(b[:, i * KEYS:(i + 1) * KEYS], gone, tk[v][:, h, :], u[ix][:, h, :])
                    drain(nc.vector.tensor_copy(amax[:, 13:14], b[:, 0:1]), (which, t, g))
                for h in range(PEER_HEADS):
                    cv = cand.rearrange("p (a b) -> p a b", a=TOPK)
                    step(nc.vector.tensor_tensor(cv, tk["v1"][:, h, :].unsqueeze(2).to_broadcast([P, TOPK, TOPK]),
                                                 tk["v2"][:, h, :].unsqueeze(1).to_broadcast([P, TOPK, TOPK]), ALU.add))
                    top16(cand, cand_gone, tk["sc"][:, h, :], u["pos"][:, h, :])
                step(nc.vector.tensor_single_scalar(u["pa"], u["pos"], 4, ALU.logical_shift_right))
                step(nc.vector.tensor_single_scalar(u["pb"], u["pos"], TOPK - 1, ALU.bitwise_and))
                for n in ("1", "2"):
                    step(nc.vector.tensor_copy(tk[f"i{n}f"], u[f"i{n}"]))
                for place_, keys, dst in (("pa", "i1f", "ia"), ("pb", "i2f", "ib")):
                    for g in range(4):
                        hs = slice(2 * g, 2 * g + 2)
                        o = onehot.rearrange("p (h k) a -> p h k a", h=2)
                        for h in range(2):
                            at = u[place_][:, 2 * g + h, :].unsqueeze(2).to_broadcast([P, TOPK, TOPK])
                            step(nc.vector.tensor_tensor(o[:, h], at, cst("iota").unsqueeze(1).to_broadcast([P, TOPK, TOPK]), ALU.is_equal))
                            step(nc.vector.tensor_tensor(o[:, h], o[:, h], tk[keys][:, 2 * g + h, :].unsqueeze(1).to_broadcast([P, TOPK, TOPK]), ALU.mult))
                        step(nc.vector.tensor_reduce(tk[dst][:, hs, :], o, AX.X, ALU.add))
                step(nc.vector.tensor_tensor(top_exp, tk["sc"], tk["sc"][:, :, 0:1].to_broadcast([P, PEER_HEADS, TOPK]), ALU.subtract))
                nc.vector.tensor_scalar(tk["ia"], tk["ia"], float(KEYS), None, ALU.mult).then_inc(sem("top_shifted"), 1)
                dve.wait_ge(sem("top_shifted"), phase + 1)
                dve.wait_ge(sem("top_exp"), phase + 1)
                step(nc.vector.tensor_reduce(top_sum, top_exp, AX.X, ALU.add))
                step(nc.vector.reciprocal(top_sum, top_sum))
                if phase >= 2:
                    dve.wait_ge(sem("peer_sum"), phase - 1)
                step(nc.vector.tensor_tensor(gates[:, t, :].rearrange("p (h k) -> p h k", h=PEER_HEADS), top_exp,
                                             top_sum.unsqueeze(2).to_broadcast([P, PEER_HEADS, TOPK]), ALU.mult))
                ins = nc.vector.tensor_tensor(eidx[:, t, :].rearrange("p (h k) -> p h k", h=PEER_HEADS), tk["ia"], tk["ib"], ALU.add)
                ins.then_inc(sem("experts_picked"), 1)
                dve.wait_ge(sem("experts_picked"), phase + 1)

            pick(0)

            def ple(t):
                norm(f"ple{t}")
                for half in range(2):
                    c = slice(512 * half, 512 * half + 512)
                    drained(dve, ("ple_gate", t, half))
                    b = filled(dve, ("ple", t, half))
                    drain(nc.vector.tensor_tensor(ple_gate[:, c], ple_gate[:, c], b[:, :], ALU.mult), ("ple", t, half))
                nc.vector.tensor_tensor(X[:, t, :], X[:, t, :], ple_gate, ALU.add).then_inc(sem("x_ready"), 1)

            def log_sigmoid(name, rows, dst, signal):
                b, _ = job[name]
                z = bank[b]
                drain(nc.vector.scalar_tensor_tensor(out=dst, in0=z[0:rows, 0:256], scalar=0.0, in1=dst, op0=ALU.min, op1=ALU.subtract), name)
                nc.vector.tensor_scalar(dst, dst, 1.0 / GLA_TAU, None, ALU.mult).then_inc(sem(signal), 1)

            def proj(t):
                dve.wait_ge(sem("x_ready"), X_STATE[f"n1{t}"])
                nc.vector.memset(lrT[0:32, :], 1.0).then_inc(sem("ones_set"), 1)
                dve.wait_ge(sem("log_gate"), t + 1)
                log_sigmoid(("z", t), P, lg, "log_decay")
                if t == 0:
                    dve.wait_ge(sem("log_gate_meta"), 1)
                    log_sigmoid("z_meta", META, lg_m[0:META, :], "log_decay_meta")
                dve.wait_ge(sem("gr_sigmoid"), t + 1)
                b, _ = job[("gr", t)]
                drain(nc.vector.tensor_tensor(silu, silu, bank[b][:, :], ALU.mult), ("gr", t))

            def stick(t):
                nkb = t + 2
                for hg in range(2):
                    for k in reversed(range(nkb)):
                        n = META if k == 0 else P
                        b = bank[job[("stick_z", t, hg, k)][0]]
                        tmp = sb_tmp[0:n, k % 2, :]
                        dve.wait_ge(sem("stick_soft"), STICK_BASE[t] + hg * nkb + nkb - k)
                        if hg:
                            filled(dve, ("stick_w", t, 0, 0))
                        lv = sb_log[0:n, k, :]
                        drain(nc.vector.scalar_tensor_tensor(out=lv, in0=b[0:n, :], scalar=0.0, in1=tmp, op0=ALU.max, op1=ALU.add), ("stick_z", t, hg, k))
                        if k == nkb - 1:
                            lq = lv.rearrange("p (h q) -> p h q", h=4)
                            ins = nc.vector.scalar_tensor_tensor(out=lq, in0=lq, scalar=-1.0, in1=cst("causal").unsqueeze(1).to_broadcast([P, 4, P]),
                                                                 op0=ALU.mult, op1=ALU.mult)
                        else:
                            ins = nc.vector.tensor_scalar(lv, lv, -1.0, None, ALU.mult)
                        ins.then_inc(sem("stick_log"), 1)
                attention_sums("stick_o", t, 0)

            def attention_sums(name, t, half):
                b = filled(dve, (name, t))
                drain(nc.vector.tensor_copy(hn[:, t, 512 * half:512 * half + 512], b[:, :]), (name, t))

            def gla(t):
                if t == 0:
                    drained(dve, "decay_meta")
                    nc.vector.tensor_tensor(klm, klm, gkT[:, :, 0:META], ALU.mult).then_inc(sem("key_meta"), 1)
                    b = filled(dve, "state_meta")
                    for h in range(GLA_HEADS):
                        e = HEAD * (h % 2)
                        ins = nc.vector.tensor_copy(state[e:e + HEAD, h // 2, :], b[e:e + HEAD, h * P:(h + 1) * P])
                        if h < GLA_HEADS - 1:
                            step(ins)
                        else:
                            drain(ins, "state_meta")
                heads = 0
                for dt in range(2):
                    for i in range(3):
                        drained(dve, ("decay", t, dt, i))
                    ev = expd.rearrange("p (l t) -> p l t", t=P)
                    if dt:
                        dve.wait_ge(sem("gla_head"), 3 * t + 2)
                    step(nc.vector.tensor_tensor(gla_q, ev[:, 0:LEVELS + 1, :], gqT[:, dt, :].unsqueeze(1).to_broadcast([P, LEVELS + 1, P]), ALU.mult))
                    if t == 0:
                        step(nc.vector.tensor_copy(arec[:, dt:dt + 1], ev[:, INTER, P - 1:P]))
                    kk = gkT[:, dt, META:META + P]
                    step(nc.vector.tensor_tensor(gla_k[:, LEVELS, :], ev[:, LAST, :], kk, ALU.mult))
                    nc.vector.tensor_tensor(gla_k[:, 0:LEVELS, :], ev[:, 0:LEVELS, :], kk.unsqueeze(1).to_broadcast([P, LEVELS, P]), ALU.mult) \
                        .then_inc(sem("gla_qk"), 1)
                    for h in (2 * dt, 2 * dt + 1):
                        if h:
                            dve.wait_ge(sem("gla_head"), 3 * t + h)
                        for half in range(2):
                            b = filled(dve, ("gla_a", t, h, half))
                            ls = slice(4 * half, 4 * half + 4)
                            drain(nc.vector.tensor_tensor(gla_a[:, ls, :], b[:, :].rearrange("p (l t) -> p l t", l=4), pairs[:, ls, :], ALU.mult),
                                  ("gla_a", t, h, half))
                if t == 0:
                    b = filled(dve, "state0")
                    for h in range(GLA_HEADS):
                        e = HEAD * (h % 2)
                        ins = nc.vector.scalar_tensor_tensor(out=state[e:e + HEAD, h // 2, :], in0=state[e:e + HEAD, h // 2, :],
                                                             scalar=arec[e:e + HEAD, h // 2:h // 2 + 1], in1=b[e:e + HEAD, h * P:(h + 1) * P],
                                                             op0=ALU.mult, op1=ALU.add)
                        if h < GLA_HEADS - 1:
                            step(ins)
                        else:
                            drain(ins, "state0")

            def mixed_out(t):
                attention_sums("gla_o", t, 1)
                for k, heads in enumerate((SB_HEADS, GLA_HEADS)):
                    o = hn[:, t, 512 * k:512 * k + 512]
                    step(nc.vector.tensor_tensor(sq2, o, o, ALU.mult))
                    ins = nc.vector.tensor_reduce(hstat[:, k, 0:heads], sq2.rearrange("p (h d) -> p h d", h=heads), AX.X, ALU.add)
                    if k == 0:
                        step(ins)
                    else:
                        ins.then_inc(sem("mix_squares"), 1)
                dve.wait_ge(sem("mix_inv_rms"), t + 1)
                for k, (heads, w) in enumerate(((SB_HEADS, HEAD), (GLA_HEADS, GLA_DV))):
                    o = hn[:, t, 512 * k:512 * k + 512]
                    ov = o.rearrange("p (h d) -> p h d", h=heads)
                    step(nc.vector.tensor_tensor(ov, ov, hstat[:, k, 0:heads].unsqueeze(2).to_broadcast([P, heads, w]), ALU.mult))
                    step(nc.vector.tensor_tensor(o, o, head_gain[:, k, :], ALU.mult))
                o = hn[:, t, 512:D]
                nc.vector.tensor_tensor(o, o, silu, ALU.mult).then_inc(sem("mixed"), 1)
                residual("out2", t)

            def background(s):
                t = int(s[-1])
                if s == "pick1":
                    pick(1)
                elif s.startswith("ple"):
                    ple(t)
                elif s.startswith("n1"):
                    norm(s)
                elif s.startswith("proj"):
                    proj(t)
                elif s.startswith("sb"):
                    stick(t)
                elif s.startswith("gla"):
                    gla(t)
                elif s.startswith("out"):
                    mixed_out(t)
                elif s.startswith("pick2"):
                    norm(f"n2{t}")
                    pick(2 + t)
                elif s == "final0":
                    norm("f0")

            for phase in range(PHASES):
                t = PHASE_TILE[phase]
                g_all = gates[:, t, :].rearrange("p (i g k) -> p i g k", g=RING // CHUNK, k=CHUNK)
                for lo, hi, s_ in segments(phase):
                    with dve.Fori(lo, hi) as i:
                        it = i + phase * ITERS
                        for j in range(RING // CHUNK):
                            for s in range(CHUNK * j, CHUNK * (j + 1)):
                                dve.wait_ge(sem(f"row_in{s}"), (it + 1) * 16)
                                u = ring[:, s, 0:D]
                                nc.vector.tensor_tensor_reduce(out=u, in0=u, in1=hn[:, t, :], scale=1.0, scalar=0.0, op0=ALU.mult, op1=ALU.add,
                                                               accum_out=dot[:, s:s + 1]).then_inc(sem("dots"), 1)
                            c = slice(CHUNK * j, CHUNK * (j + 1))
                            dve.wait_ge(sem("gelu"), it * (RING // CHUNK) + j + 1)
                            nc.vector.tensor_tensor(weight[:, c], act_dot[:, c], gates[:, t, bass.ds(i * RING + CHUNK * j, CHUNK)], ALU.mult) \
                                .then_inc(sem("weights_ready"), 1)
                    if s_:
                        background(s_)
                dve.wait_ge(sem("peer_sum"), phase + 1)
                nc.vector.tensor_copy(X[:, t, :].rearrange("p (h d) -> p h d", h=2), acc[:, :, :]).then_inc(sem("x_ready"), 1)
            norm("f1")


SMALL_IN = 16 * 7
STICK_BASE = [0, 4]


def units_of(w, width=256):
    n = w.shape[1]
    return [np.ascontiguousarray(w[:, c:c + width].reshape(w.shape[0] // P, P, width).transpose(1, 0, 2)).reshape(P, -1)
            for c in range(0, n, width)]


def layout(i):
    const, dil = constants()
    w_in = i["w_in"][0]
    w_in = np.concatenate([w_in[:, 0:1024], w_in[:, 1536:3072], w_in[:, 1024:1536], w_in[:, 3072:5888]], 1)
    units = units_of(w_in)
    units += units_of(i["w_branch_na"][0], 512) + units_of(i["w_branch_dil"][0], 1024)
    units += units_of(i["w_out"][0]) + units_of(i["peer_w_query"][0])
    units += units_of(i["w_ple_gate"][0]) + units_of(i["w_ple"][0], 1024)
    w2 = i["w_in_2"][0]
    for lo, hi in ((512, 1024), (0, 512), (1792, 2048), (1536, 1792), (1024, 1536), (2048, 2560), (2560, 3072)):
        units += units_of(w2[:, lo:hi])
    units += units_of(i["w_out_2"][0]) + units_of(i["w_peer_q_2"][0])
    assert len(units) == N_UNITS and all(u.shape == (P, UNIT) for u in units)
    qc = np.arange(P) % GRID_W
    half = np.arange(P) // GRID_W
    rows = np.arange(6)[None, :, None] + 5 - half[:, None, None]
    cols = np.clip(np.arange(GRID_W)[None, None] - qc[:, None, None] + NA_WIN_COLS - 1, 0, 2 * NA_WIN_COLS - 2)
    bias = i["na_rel_bias"][0][:, rows, cols].transpose(1, 0, 2, 3)
    qk = np.stack([i["qk_norm_na"][0, 0], i["qk_norm_na"][0, 1], i["qk_norm_dil"][0, 0], i["qk_norm_dil"][0, 1]])
    cols_of = lambda g: g.reshape(DC, P).T
    keys2 = np.concatenate([i["sub_keys1_2"][0].transpose(2, 0, 1), i["sub_keys2_2"][0].transpose(2, 0, 1)], 0)
    return {
        "x": i["x"][0],
        "meta": i["meta_tokens_2"],
        "weights": np.stack(units),
        "const": const,
        "dil_mask": dil,
        "na_bias": bias.reshape(P, NA_HEADS, 6 * GRID_W),
        "gain": np.stack([i["norm_ffn"][0], i["norm2_g_2"][0], i["norm_f_g_2"]]),
        "head_gain": np.stack([i["sb_norm_g_2"][0], i["gla_norm_g_2"][0]]),
        "gain_col": np.stack([cols_of(i["norm_mix"][0]), cols_of(i["norm_ple"][0]), cols_of(i["norm1_g_2"][0])], 1),
        "qk_gain": qk,
        "keys1": i["peer_sub_keys"][0].transpose(2, 0, 1),
        "keys2": keys2,
        "pT": i["p"][0, 0].T.reshape(2, P, SEQ).transpose(1, 0, 2),
        "w_lr": w2[:, 3072:3088].reshape(DC, P, RANK).transpose(1, 0, 2),
        "w_gu": np.concatenate([i["w_gate_up_2"][0], i["b_gate_up_2"]], 0),
        "experts1": np.concatenate([i["peer_expert_u"][0], i["peer_expert_v"][0]], 1),
        "experts2": np.concatenate([i["expert_u_2"][0], i["expert_v_2"][0]], 1),
    }


def kernel(**inputs):
    import concourse.bacc as bacc
    from concourse.bass_utils import run_bass_kernel_spmd

    nc = bacc.Bacc("TRN2", target_bir_lowering=False, num_devices=1)
    arrays = {"in_" + k: np.ascontiguousarray(v) for k, v in layout({k: np.asarray(v) for k, v in inputs.items()}).items()}
    aps = {k[3:]: nc.dram_tensor(k, v.shape, mybir.dt.from_np(v.dtype), kind="ExternalInput").ap() for k, v in arrays.items()}
    out = nc.dram_tensor("out", (SEQ, D), F32, kind="ExternalOutput").ap()
    build(nc, aps, out)
    r = run_bass_kernel_spmd(nc, [arrays], core_ids=[0])
    return r.results[0]["out"].reshape(1, SEQ, D)
```

```python
from contextlib import ExitStack

import numpy as np

import concourse.bass as bass
from concourse import mybir

F32 = mybir.dt.float32
U32 = mybir.dt.uint32
ALU = mybir.AluOpType
ACT = mybir.ActivationFunctionType
AX = mybir.AxisListType

P = 128
D = 1024
DC = D // P
TILES = 2
SEQ = TILES * P
EPS = 1e-6
NEG = -1e30
META = 16
HEAD = 64
NA_HEADS = 8
DIL_GROUPS, DIL_SLOTS = 3, 4
DIL_HEADS = DIL_GROUPS * DIL_SLOTS
GRID_W, GRID_ROWS = 64, SEQ // 64
NA_WIN_ROWS, NA_WIN_COLS = 8, 16
ROT_HALF = 8
ROPE_THETA = 500000.0
QK_HEADS = 2 * NA_HEADS + 2 * DIL_HEADS
PAIRS = QK_HEADS // 2
V_COLS = (NA_HEADS + DIL_HEADS) * HEAD
SB_HEADS = 8
GLA_HEADS, GLA_DK, GLA_DV = 4, 64, 128
RANK = 16
GLA_TAU = 16.0
LEVELS = 8
INTER, LAST = LEVELS, LEVELS + 1
PEER_HEADS, KEYS, TOPK = 8, 128, 16
SLOTS = PEER_HEADS * TOPK
EXPERTS = KEYS * KEYS

RING = 8
CHUNK = 4
ITERS = SLOTS // RING
PHASES = 4
PAIR_HEADS = 2
PICKS = PEER_HEADS // PAIR_HEADS
PICK_ITERS = ITERS // PICKS
WSLOTS = 4
UNIT = 2048
BANKS = 5
OUT_BANK = BANKS

N_IN, N_BRANCH, N_OUT, N_Q1 = 23, 3, 4, 8
N_FIRST = N_IN + N_BRANCH + N_OUT + N_Q1
N_TILE = 4 + 1 + 12 + 4 + 4
N_UNITS = N_FIRST + N_TILE
N_LOADS = N_FIRST + TILES * N_TILE

_at = 0
CONST = {}
for _name, _n in (("ident", P), ("decay", (LEVELS + 2) * P), ("pairs", LEVELS * P), ("later", P), ("ones", P),
                  ("causal", P), ("causal_neg", P), ("iota", TOPK), ("rope", TILES * 2 * ROT_HALF),
                  ("na_cols", GRID_W), ("decay_meta", META)):
    CONST[_name] = (_at, _at + _n)
    _at += _n
N_CONST = _at


def constants():
    c = np.zeros((P, N_CONST), np.float32)

    def put(name, a):
        lo, hi = CONST[name]
        c[:a.shape[0], lo:hi] = a.reshape(a.shape[0], hi - lo)

    i = np.arange(P)
    put("ident", np.eye(P, dtype=np.float32))
    decay = np.zeros((P, LEVELS + 2, P), np.float32)
    pairs = np.zeros((P, LEVELS, P), np.float32)
    pairs[:, 0] = np.eye(P)
    for level in range(1, LEVELS):
        half = 1 << (level - 1)
        mid = (i // (2 * half)) * 2 * half + half
        right = i >= mid
        s, t = i[:, None], i[None, :]
        decay[:, level] = np.where(right[None], (s >= mid[None]) & (s <= t), (s > t) & (s < mid[None]))
        pairs[:, level] = (mid[:, None] == mid[None]) & ~right[:, None] & right[None]
    decay[:, INTER] = i[:, None] <= i[None]
    decay[:, LAST] = i[:, None] > i[None]
    put("decay", decay)
    put("pairs", pairs)
    put("later", (i[:, None] >= i[None]).astype(np.float32))
    put("ones", np.ones((P, P), np.float32))
    put("causal", (i[:, None] < i[None]).astype(np.float32))
    put("causal_neg", np.where(i[:, None] < i[None], 0.0, NEG).astype(np.float32))
    put("iota", np.tile(np.arange(TOPK, dtype=np.float32), (P, 1)))
    freq = np.power(np.float32(ROPE_THETA), -np.arange(ROT_HALF, dtype=np.float32) * 2.0 / (2 * ROT_HALF))
    angle = np.arange(SEQ, dtype=np.float32)[:, None] * freq.astype(np.float32)[None]
    rope = np.stack([np.cos(angle), np.sin(angle)], 1).reshape(TILES, P, 2 * ROT_HALF)
    put("rope", rope.transpose(1, 0, 2).astype(np.float32))
    qc = i % GRID_W
    start = np.clip(qc - NA_WIN_COLS // 2, 0, GRID_W - NA_WIN_COLS)[:, None]
    kc = np.arange(GRID_W)[None]
    put("na_cols", np.where((kc >= start) & (kc < start + NA_WIN_COLS), 0.0, NEG).astype(np.float32))
    m = np.arange(META)
    put("decay_meta", (m[:, None] > m[None]).astype(np.float32))
    q = np.arange(SEQ)[:, None]
    k = np.arange(SEQ)[None]
    seen = np.stack([np.abs(q - k) <= 64, (q - k) % 4 == 0, (q - k) % 16 == 0], 1)
    dil = np.where(seen, 0.0, NEG).astype(np.float32).reshape(TILES, P, DIL_GROUPS * SEQ)
    return c, np.ascontiguousarray(dil.transpose(1, 0, 2))


def build(nc, a, out):
    ctx = ExitStack()
    with ctx:
        def sb(name, shape, dt=F32):
            return ctx.enter_context(nc.sbuf_tensor(name, [P, *shape], dt))

        sems = {}

        def sem(name):
            if name not in sems:
                sems[name] = ctx.enter_context(nc.semaphore(name))
            return sems[name]

        ring = sb("ring", [RING, 2 * D])
        wring = sb("wring", [WSLOTS, UNIT])
        work = sb("work", [7168])
        pick_tmp = sb("pick_tmp", [13 * PAIR_HEADS * TOPK + 1024 + PAIR_HEADS])
        query2T = sb("query2T", [PEER_HEADS, P])
        X = sb("X", [TILES, D])
        hn = sb("hn", [TILES, D])
        hT = sb("hT", [DC, META + SEQ])
        const = sb("const", [N_CONST])
        gain = sb("gain", [1, D])
        head_gain = sb("head_gain", [2, 512])
        gain_col = sb("gain_col", [3, DC])
        sbk = sb("sbk", [4, META + SEQ])
        sbv = sb("sbv", [3, 512])
        gv = sb("gv", [512])
        state = sb("state", [2, GLA_DV])
        keys1 = sb("keys1", [2, KEYS])
        keys2 = sb("keys2", [PEER_HEADS, KEYS])
        pT = sb("pT", [2, SEQ])
        w_lr = sb("w_lr", [DC, RANK])
        w_gu = sb("w_gu", [GLA_HEADS * GLA_DK])
        eidx = sb("eidx", [TILES, SLOTS], U32)
        gates = sb("gates", [TILES, SLOTS])
        slot_idx = sb("slot_idx", [RING], U32)
        dot = sb("dot", [RING])
        act_dot = sb("act_dot", [RING])
        weight = sb("weight", [RING])
        diag = sb("diag", [RING, P])
        fence = sb("fence", [1])
        stat = sb("stat", [32])
        hstat = sb("hstat", [2, QK_HEADS])
        amax = sb("amax", [16])
        asum = sb("asum", [TILES, 16])
        arec = sb("arec", [16])

        def cst(name, rows=P):
            lo, hi = CONST[name]
            return const[0:rows, lo:hi]

        ident = cst("ident")
        decay = cst("decay")
        pairs = cst("pairs").rearrange("p (l t) -> p l t", l=LEVELS)
        zeros = decay[:, 0:P]

        flat = ring[:, :, :].rearrange("p a b -> p (a b)")

        def cut(base, at, *shape):
            n = int(np.prod(shape))
            v = base[:, at:at + n]
            if len(shape) == 2:
                v = v.rearrange("p (a b) -> p a b", a=shape[0])
            if len(shape) == 3:
                v = v.rearrange("p (a b c) -> p a b c", a=shape[0], b=shape[1])
            return v

        qkT = cut(flat, 0, PAIRS, SEQ)
        val = cut(flat, 5120, TILES, V_COLS)
        sig = cut(flat, 7680, TILES, 2 * D)
        na_bias = cut(flat, 11776, NA_HEADS, 6 * GRID_W)
        dil_mask = cut(flat, 14848, TILES, DIL_GROUPS * SEQ)
        meta_x = cut(flat, 0, D)
        meta_h = cut(flat, D, D)
        raw = cut(work, 0, TILES, QK_HEADS * HEAD)
        sq = cut(work, 5120, 512)
        qk_gain = cut(work, 6400, 4, HEAD)
        rot = cut(work, 5632, 4, 2 * DIL_HEADS * ROT_HALF)
        prob = [hn[:, b, 0:768] for b in range(2)]
        probT = cut(work, 5632, 2, 768)
        attn = [raw[:, t, 0:768] for t in range(TILES)]
        qpT = cut(work, 0, 2 * PEER_HEADS, SEQ)
        tk = {n: cut(pick_tmp, PAIR_HEADS * TOPK * k, PAIR_HEADS, TOPK)
              for k, n in enumerate(("v1", "v2", "i1f", "i2f", "sc", "pos", "pa", "pb", "ia", "ib", "i1", "i2", "exp"))}
        at = len(tk) * PAIR_HEADS * TOPK
        cand = cut(pick_tmp, at, PAIR_HEADS, TOPK * TOPK)
        cand_gone = cut(pick_tmp, at + 512, PAIR_HEADS, TOPK * TOPK)
        top_sum = cut(pick_tmp, at + 1024, PAIR_HEADS)
        keys_gone = cut(pick_tmp, at, 2 * PAIR_HEADS, KEYS)
        onehot = cut(pick_tmp, at, 2, PAIR_HEADS * TOPK * TOPK)
        ple_gate = cut(work, 0, D)
        sb_log = cut(work, 0, 3, 512)
        sb_tmp = cut(work, 1536, 2, 512)
        sb_a = cut(work, 2560, 3, 512)
        sbq = cut(work, 4096, 4, P)
        gqT = cut(work, 4608, 2, P)
        gkT = cut(work, 4864, 2, META + P)
        lg = cut(work, 5152, 256)
        lrT = cut(work, 5408, META + P)
        silu = cut(work, 5552, 512)
        lg_m = cut(work, 6064, 256)
        klast = cut(work, 6320, 2, P)
        klm = cut(work, 6576, 2, META)
        gvm = cut(work, 6608, 512)
        expd = cut(work, 0, (LEVELS + 2) * P)
        gla_q = cut(work, 1280, LEVELS + 1, P)
        gla_k = cut(work, 2432, LEVELS + 1, P)
        gla_a = cut(work, 3584, LEVELS, P)
        sq2 = cut(work, 0, 512)

        acc = ctx.enter_context(nc.psum_tensor("acc", [P, 2, 512], F32))
        bank = [ctx.enter_context(nc.psum_tensor(f"bank{b}", [P, 512], F32)) for b in range(BANKS + 1)]

        job = {}
        turns = {"short": 0, "out": 0}

        def place(name):
            assert name not in job, name
            if name[0] in ("stick_o", "gla_o"):
                b, turn = OUT_BANK, turns["out"]
                turns["out"] += 1
            else:
                b, turn = turns["short"] % BANKS, turns["short"] // BANKS
                turns["short"] += 1
            job[name] = (b, turn)
            return bank[b]

        def filled(eng, name):
            b, turn = job[name]
            eng.wait_ge(sem(f"bank_filled{b}"), turn + 1)
            return bank[b]

        def drained(eng, name):
            b, turn = job[name]
            eng.wait_ge(sem(f"bank_drained{b}"), turn + 1)

        def drain_sem(name):
            return sem(f"bank_drained{job[name][0]}"), job[name][1] + 1

        def na_head(u, i):
            return 4 * (u // 2) + u % 2 + 2 * i

        NORMS = ["mix0", "mix1", "meta", "ffn0", "ffn1", "ple0", "n10", "n20", "ple1", "n11", "n21", "f0", "f1"]
        norm_no = {n: i for i, n in enumerate(NORMS)}
        GAIN_COL = {"mix": 0, "meta": 2, "ple": 1, "n1": 2}
        GAIN_ROW = {"ffn": 0, "n2": 1, "f": 2}

        def norm_place(name):
            if name == "meta":
                return None, meta_x[0:META, :], meta_h[0:META, :], slice(0, META), META
            t = int(name[-1])
            return t, X[:, t, :], hn[:, t, :], slice(META + t * P, META + (t + 1) * P), P

        X_STATE = {"ffn0": 1, "ffn1": 2, "ple0": 3, "n10": 4, "n20": 5, "ple1": 6, "n11": 7, "n21": 8,
                   "f0": 9, "f1": 10}
        PHASE_TILE = [0, 1, 0, 1]
        PHASE_OPEN = [1, 3, 6, 9]

        def block2_steps(t):
            return {0: [("ple_norm", t), ("ple_gate", t, 0)], 1: [("ple_gate", t, 1), ("ple_up", t)],
                    2: [("norm1", t), ("sbk", t)], 3: [("sbq", t), ("low_rank", t)], 4: [("gla_keys", t), ("gate_up", t)],
                    5: [("sbv", t)], 6: [("gv", t), ("stick_scores", t, 0)], 7: [("stick_sums", t, 0), ("stick_scores", t, 1)],
                    8: [("gr", t), ("stick_sums", t, 1)], 9: [("gla_start", t), ("gla", t, 0)], 10: [("gla", t, 1), ("gla_end", t)],
                    11: [("mixed", t), ("out2", t, 0)], 12: [("out2", t, 1), ("norm2", t)], 13: [("query2", t, 0)],
                    14: [("query2", t, 1)], 15: [("pick_keys", 2 + t, 0), ("pick", 2 + t, 0)]}

        PLAN = [{} for _ in range(PHASES)]

        def plan(phase, steps):
            for turn, names in steps.items():
                PLAN[phase].setdefault(turn, []).extend(names)

        plan(0, {g - 1: [("query1", g)] for g in range(1, PICKS)})
        for g in range(1, PICKS):
            plan(0, {2 * g - 1: [("pick_keys", 0, g)], 2 * g: [("pick", 0, g)]})
        for g in range(PICKS):
            plan(0, {2 * g + 7: [("pick_keys", 1, g)], 2 * g + 8: [("pick", 1, g)]})
        plan(1, block2_steps(0))
        plan(2, block2_steps(1))
        for phase in (2, 3):
            for g in range(1, PICKS):
                plan(phase, {3 * g - 2: [("pick_keys", phase, g)], 3 * g - 1: [("pick", phase, g)]})
        plan(3, {3: [("final", 0)]})

        def segments(phase):
            turns_at = sorted(PLAN[phase])
            if turns_at[0]:
                yield [], 0, turns_at[0]
            for k, turn in enumerate(turns_at):
                yield PLAN[phase][turn], turn, turns_at[k + 1] if k + 1 < len(turns_at) else ITERS

        block = ctx.enter_context(nc.Block())

        @block.tensor
        def _(pe):
            units = [0]

            def unit():
                n = units[0]
                units[0] += 1
                pe.wait_ge(sem(f"weights_in{n % WSLOTS}"), 16 * (n // WSLOTS + 1))
                return wring[:, n % WSLOTS, :]

            def begun(ins):
                ins.then_inc(sem("unit_begun"), 1)

            def open_bank(name):
                b = place(name)
                n, turn = job[name]
                if turn:
                    pe.wait_ge(sem(f"bank_drained{n}"), turn)
                return b

            def fill(ins, name):
                ins.then_inc(sem(f"bank_filled{job[name][0]}"), 1)

            def turn_rows(name, src, rows, chunks=DC):
                for half in range(-(-chunks // 4)):
                    b = open_bank((name, half))
                    n = min(4, chunks - 4 * half)
                    for i in range(n):
                        c = 4 * half + i
                        ins = nc.tensor.transpose(b[:, i * rows:(i + 1) * rows], src[:, c * P:(c + 1) * P],
                                                  ident[0:rows, 0:rows])
                    fill(ins, (name, half))

            def norm(name):
                _, _, rows, _, n = norm_place(name)
                pe.wait_ge(sem("rows_normed"), norm_no[name] + 1)
                turn_rows(name, rows, n)

            def to_rows(b, lo, w, cols, n_cols=256, rows=None, first=None):
                m = cols.stop - cols.start
                wv = w.rearrange("p (c n) -> p c n", c=DC)
                for c in range(DC):
                    ins = nc.tensor.matmul(b[0:m, lo:lo + n_cols], hT[:, c, cols], wv[:, c, :],
                                           start=(c == 0), stop=(c == DC - 1))
                    if c == 0 and first:
                        begun(ins)
                return ins

            def to_cols(b, w, cols, first=True, at=0):
                m = cols.stop - cols.start
                wv = w.rearrange("p (c n) -> p c n", c=DC)
                for ct in range(2):
                    for c in range(DC):
                        ins = nc.tensor.matmul(b[:, at + ct * m:at + (ct + 1) * m], wv[:, c, ct * P:(ct + 1) * P],
                                               hT[:, c, cols], start=(c == 0), stop=(c == DC - 1))
                        if first and ct == 0 and c == 0:
                            begun(ins)
                return ins

            tile_cols = [slice(META + t * P, META + (t + 1) * P) for t in range(TILES)]
            both = slice(META, META + SEQ)

            pe.wait_ge(sem("const_in"), 16)
            norm("mix0")
            norm("mix1")
            norm("meta")
            for t in range(TILES):
                drained(pe, (f"mix{t}", 1))
            for u in range(N_IN):
                w = unit()
                blk, side = divmod(u if u < N_IN - 8 else u + 1, 2)
                for t in range(TILES):
                    name = ("in", blk, t)
                    if side == 0:
                        open_bank(name)
                    ins = to_rows(bank[job[name][0]], 256 * side, w, tile_cols[t], first=(t == 0))
                    if side or u == N_IN - 9:
                        fill(ins, name)
            for t in range(TILES):
                pe.wait_ge(sem("qk_ready"), t + 1)
                turn_rows(("qkT", t), raw[:, t, :], P, PAIRS)
            for t in range(TILES):
                drained(pe, (("qkT", t), 4))
            for t in range(TILES):
                q_cols = slice(t * P, (t + 1) * P)

                def scores(u):
                    for i in range(2 if u < 4 else 3):
                        if u < 4:
                            qh, kh = na_head(u, i), NA_HEADS + na_head(u, i)
                        else:
                            qh = 2 * NA_HEADS + i * DIL_SLOTS + u - 4
                            kh = qh + DIL_HEADS
                        if i % 2 == 0:
                            b = open_bank(("score", t, u, i // 2))
                        e = HEAD * (qh % 2)
                        ins = nc.tensor.matmul(b[:, (i % 2) * SEQ:(i % 2 + 1) * SEQ], qkT[e:e + HEAD, qh // 2, q_cols],
                                               qkT[e:e + HEAD, kh // 2, :], start=True, stop=True)
                        if i == 1 or (u >= 4 and i == 2):
                            fill(ins, ("score", t, u, i // 2))

                def weigh(u):
                    n = t * 8 + u
                    pe.wait_ge(sem("prob_ready"), n + 1)
                    turn_rows(("probT", t, u), prob[n % 2], P, 4 if u < 4 else 6)
                    drained(pe, (("probT", t, u), 0 if u < 4 else 1))
                    if n in (0, 8):
                        drained(pe, ("in", 7, 1))
                        if n:
                            pe.wait_ge(sem("attn_ready"), 1)
                    pt = probT[:, n % 2, :]
                    for i in range(2 if u < 4 else 1):
                        blocks = 2 if u < 4 else 6
                        for k in range(blocks):
                            if u < 4:
                                h = na_head(u, i)
                                o, col = acc[:, 0, h * HEAD:(h + 1) * HEAD], h * HEAD
                                p = pt[:, (2 * i + k) * P:(2 * i + k + 1) * P]
                            else:
                                o = acc[:, 1, (u - 4) * HEAD:(u - 3) * HEAD]
                                col = (NA_HEADS + (k // 2) * DIL_SLOTS + u - 4) * HEAD
                                p = pt[:, k * P:(k + 1) * P]
                            ins = nc.tensor.matmul(o, p, val[:, k % 2, col:col + HEAD], start=(k == 0), stop=(k == blocks - 1))
                    ins.then_inc(sem("weighed"), 1)

                scores(0)
                for u in range(8):
                    if u + 1 < 8:
                        scores(u + 1)
                    weigh(u)
            for t in range(TILES):
                pe.wait_ge(sem("attn_ready"), t + 1)
                turn_rows(("attnT", t), attn[t], P, 6)
            for t in range(TILES):
                drained(pe, (("attnT", t), 1))
            for half in range(2):
                w = unit().rearrange("p (c n) -> p c n", c=4)
                for t in range(TILES):
                    b = open_bank(("na", half, t))
                    for c in range(4):
                        ins = nc.tensor.matmul(b[:, :], hT[:, c, tile_cols[t]], w[:, c, :], start=(c == 0), stop=(c == 3))
                        if c == 0 and t == 0:
                            begun(ins)
                    fill(ins, ("na", half, t))
            w = unit().rearrange("p (c n) -> p c n", c=2)
            for half in range(2):
                for t in range(TILES):
                    b = open_bank(("dil", half, t))
                    for c in range(2):
                        ins = nc.tensor.matmul(b[:, :], hT[:, 4 + c, tile_cols[t]], w[:, c, half * 512:(half + 1) * 512],
                                               start=(c == 0), stop=(c == 1))
                        if c == 0 and t == 0 and half == 0:
                            begun(ins)
                    fill(ins, ("dil", half, t))
            for t in range(TILES):
                pe.wait_ge(sem("merged"), t + 1)
                turn_rows(("mergedT", t), hn[:, t, :], P)
            for t in range(TILES):
                drained(pe, (("mergedT", t), 1))

            def project_out(name, tiles):
                for u in range(N_OUT):
                    w = unit()
                    for t in tiles:
                        if u % 2 == 0:
                            open_bank((name, u // 2, t))
                        b = bank[job[(name, u // 2, t)][0]]
                        ins = to_rows(b, 256 * (u % 2), w, tile_cols[t], first=(t == tiles[0]))
                        if u % 2:
                            fill(ins, (name, u // 2, t))

            project_out("out1", range(TILES))

            norm("ffn0")
            norm("ffn1")
            for t in range(TILES):
                drained(pe, (f"ffn{t}", 1))

            def query1(g):
                for h in (2 * g, 2 * g + 1):
                    fill(to_cols(open_bank(("query1", h)), unit(), both), ("query1", h))
                drained(pe, ("query1", 2 * g + 1))
                key_scores(0, g)

            def key_scores(phase, g):
                t = PHASE_TILE[phase]
                for half in range(2):
                    b = open_bank(("key", phase, g, half))
                    for i in range(PAIR_HEADS):
                        h = PAIR_HEADS * g + i
                        e = HEAD * half
                        if phase < 2:
                            q, k = qpT[:, 2 * h + half, t * P:(t + 1) * P], keys1[:, half, :]
                        else:
                            q, k = query2T[e:e + HEAD, h, :], keys2[e:e + HEAD, h, :]
                        ins = nc.tensor.matmul(b[:, i * P:(i + 1) * P], q, k, start=True, stop=True)
                    fill(ins, ("key", phase, g, half))

            def pick_keys(phase, g):
                if phase >= 2 and g == 0:
                    drained(pe, ("query2", phase - 2, 1))
                if phase:
                    key_scores(phase, g)

            pe.wait_ge(sem("small_in"), SMALL_IN)
            query1(0)

            def ple_norm(t):
                norm(f"ple{t}")
                drained(pe, (f"ple{t}", 1))

            def ple_gate_(t, half):
                name = ("ple_gate", t, half)
                b = open_bank(name)
                for u in range(2):
                    ins = to_rows(b, 256 * u, unit(), tile_cols[t], first=True)
                fill(ins, name)

            def ple_up(t):
                w = unit().rearrange("p (c n) -> p c n", c=2)
                for half in range(2):
                    b = open_bank(("ple", t, half))
                    for c in range(2):
                        ins = nc.tensor.matmul(b[:, :], pT[:, c, t * P:(t + 1) * P], w[:, c, half * 512:(half + 1) * 512],
                                               start=(c == 0), stop=(c == 1))
                        if c == 0 and half == 0:
                            begun(ins)
                    fill(ins, ("ple", t, half))

            def block2_cols(t):
                return slice(0, META + P) if t == 0 else tile_cols[t]

            def norm1(t):
                norm(f"n1{t}")
                drained(pe, (f"n1{t}", 1))

            def sbk_(t):
                for i in range(2):
                    fill(to_cols(open_bank(("sbk", t, i)), unit(), block2_cols(t)), ("sbk", t, i))

            def sbq_(t):
                b = open_bank(("sbq", t))
                for i in range(2):
                    ins = to_cols(b, unit(), tile_cols[t], at=2 * P * i)
                fill(ins, ("sbq", t))

            def low_rank(t):
                kc = block2_cols(t)
                b = open_bank(("lr", t))
                for c in range(DC):
                    ins = nc.tensor.matmul(b[0:RANK, 0:kc.stop - kc.start], w_lr[:, c, :], hT[:, c, kc], start=(c == 0), stop=(c == DC - 1))
                fill(ins, ("lr", t))

            def gla_keys(t):
                fill(to_cols(open_bank(("gk", t)), unit(), block2_cols(t)), ("gk", t))
                fill(to_cols(open_bank(("gq", t)), unit(), tile_cols[t]), ("gq", t))

            def gate_up(t):
                drained(pe, ("lr", t))
                b = open_bank(("z", t))
                ins = nc.tensor.matmul(b[:, 0:256], lrT[0:RANK + 1, META:META + P], w_gu[0:RANK + 1, :], start=True, stop=True)
                fill(ins, ("z", t))
                if t == 0:
                    b = open_bank("z_meta")
                    ins = nc.tensor.matmul(b[0:META, 0:256], lrT[0:RANK + 1, 0:META], w_gu[0:RANK + 1, :], start=True, stop=True)
                    fill(ins, "z_meta")

            def token_rows(name, t, meta):
                b = open_bank((name, t))
                bm = open_bank((name, "meta")) if meta else None
                for i in range(2):
                    w = unit()
                    ins = to_rows(b, 256 * i, w, tile_cols[t], first=True)
                    if i == 1:
                        fill(ins, (name, t))
                    if meta:
                        ins = to_rows(bm, 256 * i, w, slice(0, META))
                        if i == 1:
                            fill(ins, (name, "meta"))

            def sbv_(t):
                token_rows("sbv", t, t == 0)

            def gv_(t):
                token_rows("gv", t, t == 0)

            def gr(t):
                token_rows("gr", t, False)

            def key_blocks(t):
                out = [(slice(0, META), 0, META)]
                return out + [(tile_cols[k], 1 + k, P) for k in range(t + 1)]

            def stick_scores(t, hg):
                if hg == 0:
                    drained(pe, ("sbq", t))
                    drained(pe, ("sbk", t, 1))
                    drained(pe, ("sbv", t))
                    if t == 0:
                        drained(pe, ("sbv", "meta"))
                e = HEAD * hg
                for k, (cols, _, n) in enumerate(key_blocks(t)):
                    b = open_bank(("stick_z", t, hg, k))
                    for i in range(4):
                        ins = nc.tensor.matmul(b[0:n, i * P:(i + 1) * P], sbk[e:e + HEAD, i, cols],
                                               sbq[e:e + HEAD, i, :], start=True, stop=True)
                    fill(ins, ("stick_z", t, hg, k))

            def stick_sums(t, hg):
                kbs = key_blocks(t)
                for k, (cols, _, n) in reversed(list(enumerate(kbs))):
                    b = open_bank(("stick_w", t, hg, k))
                    if k == len(kbs) - 1:
                        nc.tensor.matmul(b[0:n, :], ident, cst("causal_neg").unsqueeze(1).to_broadcast([P, 4, P]), start=True, stop=False)
                    pe.wait_ge(sem("stick_log"), STICK_BASE[t] + hg * len(kbs) + len(kbs) - k)
                    for later in range(k + 1, len(kbs)):
                        nc.tensor.matmul(b[0:n, :], cst("ones")[:, 0:n], sb_log[:, later, :], start=(later == k + 1), stop=False)
                    for i in range(4):
                        e = HEAD * hg
                        nc.tensor.matmul(b[0:n, i * P:(i + 1) * P], sbk[e:e + HEAD, i, cols],
                                         sbq[e:e + HEAD, i, :], start=False, stop=False)
                    ins = nc.tensor.matmul(b[0:n, :], cst("later", n)[:, 0:n], sb_log[0:n, k, :], start=False, stop=True)
                    fill(ins, ("stick_w", t, hg, k))
                out_bank = open_bank(("stick_o", t)) if hg == 0 else bank[OUT_BANK]
                for k in range(len(kbs)):
                    drained(pe, ("stick_w", t, hg, k))
                for i in range(4):
                    h = 2 * i + hg
                    for k, (_, vi, n) in enumerate(kbs):
                        ins = nc.tensor.matmul(out_bank[:, h * HEAD:(h + 1) * HEAD], sb_a[0:n, k, i * P:(i + 1) * P],
                                               sbv[0:n, vi, h * HEAD:(h + 1) * HEAD],
                                               start=(k == 0), stop=(k == len(kbs) - 1))
                if hg == 0:
                    ins.then_inc(sem("stick_half"), 1)
                else:
                    fill(ins, ("stick_o", t))

            def gla_start(t):
                drained(pe, ("gv", t))
                if t == 0:
                    drained(pe, ("gv", "meta"))
                    pe.wait_ge(sem("log_decay_meta"), 1)
                    b = open_bank("decay_meta")
                    for dt in range(2):
                        ins = nc.tensor.matmul(b[:, dt * META:(dt + 1) * META], lg_m[0:META, dt * P:(dt + 1) * P],
                                               cst("decay_meta", META), start=True, stop=True)
                    fill(ins, "decay_meta")
                    pe.wait_ge(sem("key_meta"), 1)
                    b = open_bank("klast_meta")
                    for dt in range(2):
                        ins = nc.tensor.transpose(b[0:META, dt * P:(dt + 1) * P], klm[:, dt, :], ident)
                    fill(ins, "klast_meta")
                    drained(pe, "klast_meta")
                    b = open_bank("state_meta")
                    for h in range(GLA_HEADS):
                        ins = nc.tensor.matmul(b[:, h * P:(h + 1) * P], klast[0:META, h // 2, :], gvm[0:META, h * P:(h + 1) * P],
                                               start=True, stop=True)
                    fill(ins, "state_meta")
                pe.wait_ge(sem("log_decay"), t + 1)
                open_bank(("gla_o", t))

            def gla(t, dt):
                out_bank = bank[OUT_BANK]
                for i in range(3):
                    b = open_bank(("decay", t, dt, i))
                    n = min(512, (LEVELS + 2) * P - 512 * i)
                    ins = nc.tensor.matmul(b[:, 0:n], lg[:, dt * P:(dt + 1) * P], decay[:, 512 * i:512 * i + n],
                                           start=True, stop=True)
                    fill(ins, ("decay", t, dt, i))
                pe.wait_ge(sem("gla_qk"), 2 * t + dt + 1)
                if t == 0:
                    b = open_bank(("klast", t, dt))
                    fill(nc.tensor.transpose(b[:, 0:P], gla_k[:, LEVELS, :], ident), ("klast", t, dt))
                for h in (2 * dt, 2 * dt + 1):
                    e = HEAD * (h % 2)
                    for half in range(2):
                        b = open_bank(("gla_a", t, h, half))
                        for i in range(4):
                            level = 4 * half + i
                            ins = nc.tensor.matmul(b[:, i * P:(i + 1) * P], gla_k[e:e + HEAD, level, :],
                                                   gla_q[e:e + HEAD, level, :], start=True, stop=True)
                        fill(ins, ("gla_a", t, h, half))
                    drained(pe, ("gla_a", t, h, 1))
                    if h == 0:
                        drained(pe, "state0" if t else "state_meta")
                    o = out_bank[:, h * P:(h + 1) * P]
                    for level in range(LEVELS):
                        nc.tensor.matmul(o, gla_a[:, level, :], gv[:, h * P:(h + 1) * P], start=(level == 0), stop=False)
                    ins = nc.tensor.matmul(o, gla_q[e:e + HEAD, INTER, :], state[e:e + HEAD, dt, :], start=False, stop=True)
                    if h == GLA_HEADS - 1:
                        fill(ins, ("gla_o", t))
                    else:
                        ins.then_inc(sem("gla_head"), 1)

            def gla_end(t):
                if t == 0:
                    drained(pe, ("klast", t, 1))
                    b = open_bank("state0")
                    for h in range(GLA_HEADS):
                        ins = nc.tensor.matmul(b[:, h * P:(h + 1) * P], klast[:, h // 2, :], gv[:, h * P:(h + 1) * P],
                                               start=True, stop=True)
                    fill(ins, "state0")

            def mixed(t):
                pe.wait_ge(sem("mixed"), t + 1)
                turn_rows(("mixedT", t), hn[:, t, :], P)
                drained(pe, (("mixedT", t), 1))

            def out2(t, half):
                name = ("out2", half, t)
                b = open_bank(name)
                for u in range(2):
                    ins = to_rows(b, 256 * u, unit(), tile_cols[t], first=True)
                fill(ins, name)

            def norm2(t):
                norm(f"n2{t}")
                drained(pe, (f"n2{t}", 1))

            def query2(t, i):
                b = open_bank(("query2", t, i))
                for k in range(2):
                    ins = to_cols(b, unit(), tile_cols[t], at=2 * P * k)
                fill(ins, ("query2", t, i))

            STEPS = {"query1": query1, "pick_keys": pick_keys, "ple_norm": ple_norm, "ple_gate": ple_gate_, "ple_up": ple_up,
                     "norm1": norm1, "sbk": sbk_, "sbq": sbq_, "low_rank": low_rank, "gla_keys": gla_keys, "gate_up": gate_up,
                     "sbv": sbv_, "gv": gv_, "gr": gr, "stick_scores": stick_scores, "stick_sums": stick_sums,
                     "gla_start": gla_start, "gla": gla, "gla_end": gla_end, "mixed": mixed, "out2": out2, "norm2": norm2,
                     "query2": query2}

            def background(steps):
                for name, *where in steps:
                    if name in STEPS:
                        STEPS[name](*where)

            for phase in range(PHASES):
                tile = PHASE_TILE[phase]
                pe.wait_ge(sem("x_ready"), PHASE_OPEN[phase])
                if phase == 0:
                    pe.wait_ge(sem("attn_ready"), 2)
                for half in range(2):
                    nc.tensor.matmul(acc[:, half, :], ident, X[:, tile, half * 512:(half + 1) * 512], start=True, stop=False)
                for steps, lo, hi in segments(phase):
                    background(steps)
                    with pe.Fori(phase * ITERS + lo, phase * ITERS + hi) as it:
                        for s in range(RING):
                            pe.wait_ge(sem("diag_ready"), it * RING + s + 1)
                            for half in range(2):
                                ins = nc.tensor.matmul(acc[:, half, :], diag[:, s, :],
                                                       ring[:, s, D + half * 512:D + (half + 1) * 512],
                                                       start=False, stop=False)
                            ins.then_inc(sem("slot_free"), 1)
                for half in range(2):
                    ins = nc.tensor.matmul(acc[:, half, :], zeros, X[:, tile, half * 512:(half + 1) * 512], start=False, stop=True)
                ins.then_inc(sem("peer_sum"), 1)

        @block.gpsimd
        def _(pool):
            nc.gpsimd.memset(fence[:, :], 0.0).then_inc(sem("fence_set"), 1)
            pool.wait_ge(sem("fence_set"), 1)

            def gather(table, tile, it, i, s):
                nc.gpsimd.tensor_copy(slot_idx[:, s:s + 1], eidx[:, tile, bass.ds(i * RING + s, 1)]).then_inc(sem("idx_copied"), 1)
                pool.wait_ge(sem("idx_copied"), it * RING + s + 1)
                nc.gpsimd.tensor_tensor(fence[:, :], fence[:, :], fence[:, :], ALU.add)
                nc.gpsimd.indirect_dma_start(
                    out=ring[:, s, :], out_offset=None, in_=table,
                    in_offset=bass.IndirectOffsetOnAxis(ap=slot_idx[:, s:s + 1], axis=0)).then_inc(sem(f"row_in{s}"), 16)

            for phase in range(PHASES):
                tile = PHASE_TILE[phase]
                table = a["experts1"] if phase < 2 else a["experts2"]
                for g in range(PICKS):
                    pool.wait_ge(sem("experts_picked"), phase * PICKS + g + 1)
                    first = g * PICK_ITERS
                    if phase == 0 and g == 0:
                        pool.wait_ge(sem("merged"), 2)
                        for s in range(RING):
                            gather(table, tile, 0, 0, s)
                        first = 1
                    with pool.Fori(first, (g + 1) * PICK_ITERS) as i:
                        for s in range(RING):
                            pool.wait_ge(sem("slot_free"), (i + phase * ITERS) * RING + s + 1 - RING)
                            gather(table, tile, i + phase * ITERS, i, s)

        @block.sync
        def _(sp):
            sp.dma_start(X[:, 0, :], a["x"][0:P, :]).then_inc(sem("x_in"), 16)
            sp.dma_start(X[:, 1, :], a["x"][P:SEQ, :]).then_inc(sem("x_in"), 16)

            def load(n, s, at):
                sp.dma_start(wring[:, s, :], a["weights"][at]).then_inc(sem(f"weights_in{s}"), 16)

            for s in range(WSLOTS):
                load(s, s, s)
            turns = N_UNITS // WSLOTS
            with sp.Fori(1, turns) as i:
                for s in range(WSLOTS):
                    sp.wait_ge(sem("unit_begun"), i * WSLOTS + s - WSLOTS + 2)
                    load(None, s, i * WSLOTS + s)
            for n in range(turns * WSLOTS, (turns + 1) * WSLOTS):
                sp.wait_ge(sem("unit_begun"), n - WSLOTS + 2)
                load(n, n % WSLOTS, n if n < N_UNITS else n - N_TILE)
            with sp.Fori(turns + 1, N_LOADS // WSLOTS) as i:
                for s in range(WSLOTS):
                    sp.wait_ge(sem("unit_begun"), i * WSLOTS + s - WSLOTS + 2)
                    load(None, s, i * WSLOTS + s - N_TILE)
            for t in range(TILES):
                sp.wait_ge(sem("rows_normed"), norm_no[f"f{t}"] + 1)
                sp.dma_start(out[t * P:(t + 1) * P, :], hn[:, t, :]).then_inc(sem("out_written"), 16)
            sp.wait_ge(sem("out_written"), 32)

        @block.scalar
        def _(act):
            own = [0]

            def step(ins):
                ins.then_inc(sem("act_step"), 1)
                own[0] += 1
                act.wait_ge(sem("act_step"), own[0])

            def drain(ins, name):
                s, _ = drain_sem(name)
                ins.then_inc(s, 1)

            act.dma_start(const[:, :], a["const"]).then_inc(sem("const_in"), 16)
            act.dma_start(gain_col[:, :, :], a["gain_col"]).then_inc(sem("gains_in"), 16)
            act.dma_start(qk_gain, a["qk_gain"].partition_broadcast(P)).then_inc(sem("gains_in"), 16)
            act.dma_start(meta_x[0:META, :], a["meta"]).then_inc(sem("meta_in"), 16)
            act.dma_start(na_bias, a["na_bias"]).then_inc(sem("masks_in"), 16)
            act.dma_start(dil_mask, a["dil_mask"]).then_inc(sem("masks_in"), 16)
            small = [(gain[:, :, :], a["gain"][0:1].partition_broadcast(P)), (head_gain[:, :, :], a["head_gain"].partition_broadcast(P)),
                     (keys1[:, :, :], a["keys1"]), (keys2[:, :, :], a["keys2"]), (pT[:, :, :], a["pT"]),
                     (w_lr[:, :, :], a["w_lr"]), (w_gu[0:RANK + 1, :], a["w_gu"])]
            for dst, src in small:
                act.dma_start(dst, src).then_inc(sem("small_in"), 16)
            assert SMALL_IN == 16 * len(small)

            def inv_rms(v, width, last=None):
                step(nc.scalar.activation(v, v, ACT.Ln, scale=1.0 / width, bias=EPS))
                ins = nc.scalar.activation(v, v, ACT.Exp, scale=-0.5)
                if last:
                    ins.then_inc(sem(last), 1)
                else:
                    step(ins)

            def norm(name):
                _, x, rows, cols, n = norm_place(name)
                k = norm_no[name]
                if name in X_STATE:
                    act.wait_ge(sem("x_ready"), X_STATE[name])
                elif name == "meta":
                    act.wait_ge(sem("meta_in"), 16)
                else:
                    act.wait_ge(sem("x_in"), 32)
                v = stat[0:n, k:k + 1]
                step(nc.scalar.activation(rows, x, ACT.Square, accum_out=v))
                inv_rms(v, D, "inv_rms")
                if name[:-1] == "ffn" or name[:-1] == "n2":
                    turned(name, cols)

            def turned(name, cols, chunks=DC):
                for half in range(-(-chunks // 4)):
                    b = filled(act, (name, half))
                    n = min(4, chunks - 4 * half)
                    drain(nc.scalar.copy(hT[:, 4 * half:4 * half + n, cols],
                                         b[:, 0:n * P].rearrange("p (c t) -> p c t", c=n)), (name, half))

            tile_cols = [slice(META + t * P, META + (t + 1) * P) for t in range(TILES)]
            for name in ("mix0", "mix1", "meta"):
                norm(name)
            for blk in range(12):
                for t in range(TILES):
                    if blk < 5:
                        b = filled(act, ("in", blk, t))
                        if blk or t:
                            act.wait_ge(sem("squares_summed"), 2 * blk + t)
                        step(nc.scalar.activation(sq, b[:, :], ACT.Square))
                        drain(nc.scalar.copy(raw[:, t, blk * 512:(blk + 1) * 512], b[:, :]), ("in", blk, t))
                    elif blk >= 8:
                        b = filled(act, ("in", blk, t))
                        drain(nc.scalar.activation(sig[:, t, (blk - 8) * 512:(blk - 7) * 512], b[:, :], ACT.Sigmoid), ("in", blk, t))
            for t in range(TILES):
                act.wait_ge(sem("squares_summed"), 10)
                inv_rms(hstat[:, t, :], HEAD, "qk_inv_rms")
            for t in range(TILES):
                for j in range(5):
                    b = filled(act, (("qkT", t), j))
                    drain(nc.scalar.copy(qkT[:, 4 * j:4 * j + 4, t * P:(t + 1) * P],
                                         b[:, :].rearrange("p (c t) -> p c t", c=4)), (("qkT", t), j))
            for t in range(TILES):
                for u in range(8):
                    n = 8 * t + u
                    act.wait_ge(sem("score_max"), n + 1)
                    p = prob[n % 2]
                    if u < 4:
                        for i in range(2):
                            v = p[:, i * SEQ:(i + 1) * SEQ]
                            ins = nc.scalar.activation(v, v, ACT.Exp, bias=amax[:, 2 * (n % 2) + i:2 * (n % 2) + i + 1],
                                                       accum_out=asum[:, t, na_head(u, i):na_head(u, i) + 1])
                            if i == 0:
                                step(ins)
                    else:
                        ins = nc.scalar.activation(p, p, ACT.Exp, bias=amax[:, 2 * (n % 2):2 * (n % 2) + 1],
                                                   accum_out=asum[:, t, 4 + u:5 + u])
                    ins.then_inc(sem("prob_ready"), 1)
                    for half in range(1 if u < 4 else 2):
                        b = filled(act, (("probT", t, u), half))
                        if half == 0 and n >= 2:
                            act.wait_ge(sem("weighed"), n - 1)
                        w = 512 if half == 0 else 256
                        drain(nc.scalar.copy(probT[:, n % 2, 512 * half:512 * half + w], b[:, 0:w]), (("probT", t, u), half))
            for t in range(TILES):
                turned(("attnT", t), tile_cols[t], 6)
            for t in range(TILES):
                turned(("mergedT", t), tile_cols[t])
            norm("ffn0")
            norm("ffn1")

            def next_gain(row, last):
                act.wait_ge(sem("rows_normed"), norm_no[last] + 1)
                act.dma_start(gain[:, :, :], a["gain"][row:row + 1].partition_broadcast(P)).then_inc(sem("next_gain_in"), 16)

            next_gain(1, "ffn1")

            def query1(g):
                for h in (2 * g, 2 * g + 1):
                    b = filled(act, ("query1", h))
                    drain(nc.scalar.copy(qpT[:, 2 * h:2 * h + 2, :], b[:, :].rearrange("p (c t) -> p c t", c=2)), ("query1", h))

            def pick(phase, g):
                act.wait_ge(sem("top_shifted"), PICKS * phase + g + 1)
                nc.scalar.activation(tk["exp"], tk["exp"], ACT.Exp).then_inc(sem("top_exp"), 1)

            query1(0)
            pick(0, 0)

            def ple_norm(t):
                norm(f"ple{t}")

            def ple_gate_(t, half):
                b = filled(act, ("ple_gate", t, half))
                drain(nc.scalar.activation(ple_gate[:, half * 512:(half + 1) * 512], b[:, :], ACT.Sigmoid), ("ple_gate", t, half))

            def log_sigmoid(name, rows, dst, signal):
                b = filled(act, name)
                step(nc.scalar.activation(dst, b[0:rows, 0:256], ACT.Abs))
                step(nc.scalar.activation(dst, dst, ACT.Exp, scale=-1.0))
                nc.scalar.activation(dst, dst, ACT.Ln, bias=1.0).then_inc(sem(signal), 1)

            def norm1(t):
                norm(f"n1{t}")

            def new_cols(t):
                return (0, META + P) if t == 0 else (META + P, P)

            def sbk_(t):
                at, n = new_cols(t)
                for i in range(2):
                    b = filled(act, ("sbk", t, i))
                    drain(nc.scalar.copy(sbk[:, 2 * i:2 * i + 2, at:at + n],
                                         b[:, 0:2 * n].rearrange("p (c t) -> p c t", c=2)), ("sbk", t, i))

            def sbq_(t):
                b = filled(act, ("sbq", t))
                drain(nc.scalar.mul(sbq, b[:, :].rearrange("p (c t) -> p c t", c=4), HEAD ** -0.5), ("sbq", t))

            def low_rank(t):
                _, n = new_cols(t)
                b = filled(act, ("lr", t))
                act.wait_ge(sem("ones_set"), t + 1)
                drain(nc.scalar.copy(lrT[0:RANK, META + P - n:META + P], b[0:RANK, 0:n]), ("lr", t))

            def gla_keys(t):
                _, n = new_cols(t)
                b = filled(act, ("gk", t))
                drain(nc.scalar.copy(gkT[:, :, META + P - n:META + P], b[:, 0:2 * n].rearrange("p (c t) -> p c t", c=2)), ("gk", t))
                b = filled(act, ("gq", t))
                drain(nc.scalar.mul(gqT, b[:, 0:2 * P].rearrange("p (c t) -> p c t", c=2), GLA_DK ** -0.5), ("gq", t))

            def gate_up(t):
                log_sigmoid(("z", t), P, lg, "log_gate")
                if t == 0:
                    log_sigmoid("z_meta", META, lg_m[0:META, :], "log_gate_meta")

            def token_rows(name, t, dst, dst_meta):
                b = filled(act, (name, t))
                drain(nc.scalar.copy(dst, b[:, :]), (name, t))
                if t == 0:
                    b = filled(act, (name, "meta"))
                    drain(nc.scalar.copy(dst_meta, b[0:META, :]), (name, "meta"))

            def sbv_(t):
                token_rows("sbv", t, sbv[:, 1 + t, :], sbv[0:META, 0, :])

            def gv_(t):
                token_rows("gv", t, gv[:, :], gvm[0:META, :])

            def gr(t):
                b = filled(act, ("gr", t))
                nc.scalar.activation(silu, b[:, :], ACT.Sigmoid).then_inc(sem("gr_sigmoid"), 1)

            def stick_scores(t, hg):
                nkb = t + 2
                for k in reversed(range(nkb)):
                    n = META if k == 0 else P
                    tmp = sb_tmp[0:n, k % 2, :]
                    b = filled(act, ("stick_z", t, hg, k))
                    if hg * nkb + nkb - k > 2:
                        act.wait_ge(sem("stick_log"), STICK_BASE[t] + hg * nkb + nkb - k - 2)
                    step(nc.scalar.activation(tmp, b[0:n, :], ACT.Abs))
                    step(nc.scalar.activation(tmp, tmp, ACT.Exp, scale=-1.0))
                    nc.scalar.activation(tmp, tmp, ACT.Ln, bias=1.0).then_inc(sem("stick_soft"), 1)

            def stick_sums(t, hg):
                if hg:
                    act.wait_ge(sem("stick_half"), t + 1)
                for k in reversed(range(t + 2)):
                    n = META if k == 0 else P
                    b = filled(act, ("stick_w", t, hg, k))
                    drain(nc.scalar.activation(sb_a[0:n, k, :], b[0:n, :], ACT.Exp), ("stick_w", t, hg, k))

            def gla_start(t):
                if t == 0:
                    b = filled(act, "decay_meta")
                    drain(nc.scalar.activation(klm, b[:, 0:2 * META].rearrange("p (c t) -> p c t", c=2), ACT.Exp), "decay_meta")
                    b = filled(act, "klast_meta")
                    drain(nc.scalar.copy(klast[0:META, :, :], b[0:META, 0:2 * P].rearrange("p (c t) -> p c t", c=2)), "klast_meta")

            def gla(t, dt):
                if dt:
                    act.wait_ge(sem("gla_qk"), 2 * t + 1)
                for i in range(3):
                    n = min(512, (LEVELS + 2) * P - 512 * i)
                    b = filled(act, ("decay", t, dt, i))
                    drain(nc.scalar.activation(expd[:, 512 * i:512 * i + n], b[:, 0:n], ACT.Exp), ("decay", t, dt, i))
                if t == 0:
                    b = filled(act, ("klast", t, dt))
                    if dt == 0:
                        filled(act, "state_meta")
                    drain(nc.scalar.copy(klast[:, dt, :], b[:, 0:P]), ("klast", t, dt))

            def head_norms(t):
                act.wait_ge(sem("mix_squares"), t + 1)
                inv_rms(hstat[:, 0, 0:SB_HEADS], HEAD, "")
                inv_rms(hstat[:, 1, 0:GLA_HEADS], GLA_DV, "mix_inv_rms")

            def mixed(t):
                head_norms(t)
                turned(("mixedT", t), tile_cols[t])

            def norm2(t):
                norm(f"n2{t}")

            def query2(t, i):
                b = filled(act, ("query2", t, i))
                drain(nc.scalar.copy(query2T[:, 4 * i:4 * i + 4, :], b[:, :].rearrange("p (c t) -> p c t", c=4)), ("query2", t, i))

            def final(t):
                next_gain(2, "n21")
                norm(f"f{t}")

            STEPS = {"query1": query1, "pick": pick, "ple_norm": ple_norm, "ple_gate": ple_gate_, "norm1": norm1, "sbk": sbk_,
                     "sbq": sbq_, "low_rank": low_rank, "gla_keys": gla_keys, "gate_up": gate_up, "sbv": sbv_, "gv": gv_, "gr": gr,
                     "stick_scores": stick_scores, "stick_sums": stick_sums, "gla_start": gla_start, "gla": gla, "mixed": mixed,
                     "norm2": norm2, "query2": query2, "final": final}

            def background(steps):
                for name, *where in steps:
                    if name in STEPS:
                        STEPS[name](*where)

            for phase in range(PHASES):
                for steps, lo, hi in segments(phase):
                    background(steps)
                    with act.Fori(phase * ITERS + lo, phase * ITERS + hi) as it:
                        for j in range(RING // CHUNK):
                            c = slice(CHUNK * j, CHUNK * (j + 1))
                            act.wait_ge(sem("dots"), it * RING + CHUNK * (j + 1))
                            nc.scalar.activation(act_dot[:, c], dot[:, c], ACT.Gelu).then_inc(sem("gelu"), 1)
                            act.wait_ge(sem("weights_ready"), it * (RING // CHUNK) + j + 1)
                            for s in range(CHUNK * j, CHUNK * (j + 1)):
                                nc.scalar.activation(diag[:, s, :], ident, ACT.Copy, scale=weight[:, s:s + 1]).then_inc(sem("diag_ready"), 1)
            norm("f1")

        @block.vector
        def _(dve):
            own = [0]

            def step(ins):
                ins.then_inc(sem("dve_step"), 1)
                own[0] += 1
                dve.wait_ge(sem("dve_step"), own[0])

            def drain(ins, name):
                s, n = drain_sem(name)
                ins.then_inc(s, 1)
                dve.wait_ge(s, n)

            def norm(name):
                _, x, rows, cols, n = norm_place(name)
                k = norm_no[name]
                dve.wait_ge(sem("inv_rms"), k + 1)
                kind = name if name == "meta" else name[:-1]
                if kind in GAIN_ROW:
                    if kind == "ffn":
                        dve.wait_ge(sem("small_in"), SMALL_IN)
                    else:
                        dve.wait_ge(sem("next_gain_in"), 16 * GAIN_ROW[kind])
                    ins = nc.vector.scalar_tensor_tensor(out=rows, in0=x, scalar=stat[0:n, k:k + 1],
                                                         in1=gain[:, 0, :], op0=ALU.mult, op1=ALU.mult)
                    ins.then_inc(sem("rows_normed"), 1)
                    return
                nc.vector.tensor_scalar(rows, x, stat[0:n, k:k + 1], None, ALU.mult).then_inc(sem("rows_normed"), 1)
                g = gain_col[:, GAIN_COL[kind], :]
                if kind == "mix":
                    dve.wait_ge(sem("gains_in"), 32)
                for half in range(2):
                    b = filled(dve, (name, half))
                    drain(nc.vector.tensor_tensor(hT[:, 4 * half:4 * half + 4, cols],
                                                  b[:, 0:4 * n].rearrange("p (c t) -> p c t", c=4),
                                                  g[:, 4 * half:4 * half + 4].unsqueeze(2).to_broadcast([P, 4, n]), ALU.mult), (name, half))

            dve.wait_ge(sem("const_in"), 16)
            for name in ("mix0", "mix1", "meta"):
                norm(name)
            dve.wait_ge(sem("masks_in"), 32)
            bias = na_bias.rearrange("p h (j k) -> p (h j) k", k=GRID_W)
            step(nc.vector.tensor_tensor(bias, bias, cst("na_cols").unsqueeze(1).to_broadcast([P, NA_HEADS * 6, GRID_W]), ALU.add))
            for blk in range(8):
                for t in range(TILES):
                    if blk < 5:
                        b_, turn = job[("in", blk, t)]
                        dve.wait_ge(sem(f"bank_drained{b_}"), turn + 1)
                        nc.vector.tensor_reduce(hstat[:, t, 8 * blk:8 * blk + 8], sq.rearrange("p (h d) -> p h d", d=HEAD),
                                                AX.X, ALU.add).then_inc(sem("squares_summed"), 1)
                    else:
                        n = 512 if blk < 7 else 256
                        b = filled(dve, ("in", blk, t))
                        drain(nc.vector.tensor_copy(val[:, t, (blk - 5) * 512:(blk - 5) * 512 + n], b[:, 0:n]), ("in", blk, t))
            for t in range(TILES):
                dve.wait_ge(sem("qk_inv_rms"), t + 1)
                r = raw[:, t, :].rearrange("p (h d) -> p h d", d=HEAD)
                step(nc.vector.tensor_tensor(r, r, hstat[:, t, :].unsqueeze(2).to_broadcast([P, QK_HEADS, HEAD]), ALU.mult))
                at = 0
                for k, heads in enumerate((NA_HEADS, NA_HEADS, DIL_HEADS, DIL_HEADS)):
                    v = r[:, at:at + heads, :]
                    step(nc.vector.tensor_tensor(v, v, qk_gain[:, k, :].unsqueeze(1).to_broadcast([P, heads, HEAD]), ALU.mult))
                    at += heads
                x1 = r[:, 2 * NA_HEADS:, 0:ROT_HALF]
                x2 = r[:, 2 * NA_HEADS:, ROT_HALF:2 * ROT_HALF]
                rope = cst("rope")[:, t * 2 * ROT_HALF:(t + 1) * 2 * ROT_HALF]
                cos, sin = [rope[:, k * ROT_HALF:(k + 1) * ROT_HALF].unsqueeze(1).to_broadcast([P, 2 * DIL_HEADS, ROT_HALF]) for k in range(2)]
                p = [rot[:, k, :].rearrange("p (h d) -> p h d", d=ROT_HALF) for k in range(4)]
                for dst, u, v in ((p[0], x1, cos), (p[1], x2, sin), (p[2], x2, cos), (p[3], x1, sin)):
                    step(nc.vector.tensor_tensor(dst, u, v, ALU.mult))
                step(nc.vector.tensor_tensor(x1, p[0], p[1], ALU.subtract))
                nc.vector.tensor_tensor(x2, p[2], p[3], ALU.add).then_inc(sem("qk_ready"), 1)
            for t in range(TILES):
                for u in range(8):
                    n = 8 * t + u
                    if n >= 2:
                        filled(dve, (("probT", (n - 2) // 8, (n - 2) % 8), 0 if (n - 2) % 8 < 4 else 1))
                    p = prob[n % 2]
                    m = amax[:, 2 * (n % 2):2 * (n % 2) + 2]
                    if u < 4:
                        b = filled(dve, ("score", t, u, 0))
                        j = 2 - 2 * t
                        pv = p[:, 0:512].rearrange("p (h k) -> p h k", h=2)
                        drain(nc.vector.scalar_tensor_tensor(out=pv, in0=b[:, :].rearrange("p (h k) -> p h k", h=2), scalar=HEAD ** -0.5,
                                                             in1=na_bias[:, na_head(u, 0):na_head(u, 1) + 1:2, j * GRID_W:(j + 4) * GRID_W],
                                                             op0=ALU.mult, op1=ALU.add), ("score", t, u, 0))
                        nc.vector.tensor_reduce(m, pv, AX.X, ALU.max, negate=True).then_inc(sem("score_max"), 1)
                    else:
                        for half in range(2):
                            w = 512 if half == 0 else 256
                            c = slice(512 * half, 512 * half + w)
                            b = filled(dve, ("score", t, u, half))
                            drain(nc.vector.scalar_tensor_tensor(out=p[:, c], in0=b[:, 0:w], scalar=HEAD ** -0.5, in1=dil_mask[:, t, c],
                                                                 op0=ALU.mult, op1=ALU.add), ("score", t, u, half))
                        nc.vector.tensor_reduce(m[:, 0:1], p, AX.X, ALU.max, negate=True).then_inc(sem("score_max"), 1)
                dve.wait_ge(sem("weighed"), 8 * (t + 1))
                step(nc.vector.reciprocal(arec[:, 0:12], asum[:, t, 0:12]))
                step(nc.vector.tensor_tensor(attn[t][:, 0:512].rearrange("p (h d) -> p h d", d=HEAD),
                                             acc[:, 0, :].rearrange("p (h d) -> p h d", d=HEAD),
                                             arec[:, 0:8].unsqueeze(2).to_broadcast([P, 8, HEAD]), ALU.mult))
                ins = nc.vector.tensor_tensor(attn[t][:, 512:768].rearrange("p (h d) -> p h d", d=HEAD),
                                              acc[:, 1, 0:256].rearrange("p (h d) -> p h d", d=HEAD),
                                              arec[:, 8:12].unsqueeze(2).to_broadcast([P, 4, HEAD]), ALU.mult)
                ins.then_inc(sem("attn_ready"), 1)
            for half in range(2):
                c = slice(512 * half, 512 * half + 512)
                for t in range(TILES):
                    b = filled(dve, ("na", half, t))
                    drain(nc.vector.tensor_tensor(hn[:, t, c], sig[:, t, c], b[:, :], ALU.mult), ("na", half, t))
            for half in range(2):
                c = slice(512 * half, 512 * half + 512)
                for t in range(TILES):
                    b = filled(dve, ("dil", half, t))
                    g = sig[:, t, D + 512 * half:D + 512 * half + 512]
                    drain(nc.vector.tensor_tensor(g, g, b[:, :], ALU.mult), ("dil", half, t))
                    ins = nc.vector.tensor_tensor(hn[:, t, c], hn[:, t, c], g, ALU.add)
                    if half:
                        ins.then_inc(sem("merged"), 1)

            for half in range(2):
                for t in range(TILES):
                    c = slice(512 * half, 512 * half + 512)
                    b = filled(dve, ("out1", half, t))
                    drain(nc.vector.tensor_tensor(X[:, t, c], X[:, t, c], b[:, :], ALU.add), ("out1", half, t))
                    if half:
                        nc.vector.tensor_copy(amax[:, 12:13], X[:, t, 0:1]).then_inc(sem("x_ready"), 1)
            norm("ffn0")
            norm("ffn1")

            def mark(ins):
                ins.then_inc(sem("dve_step"), 1)
                own[0] += 1
                return own[0]

            def after(n):
                dve.wait_ge(sem("dve_step"), n)

            u32 = {n: v.bitcast(U32) for n, v in tk.items()}

            def top16(sources, last_read=None):
                done = [own[0]] * len(sources)
                for k, (src, gone, v, i) in enumerate(sources):
                    done[k] = mark(nc.vector.max(v[:, 0:8], src))
                for k, (src, gone, v, i) in enumerate(sources):
                    after(done[k])
                    mark(nc.vector.max_index(i[:, 0:8], v[:, 0:8], src))
                for k, (src, gone, v, i) in enumerate(sources):
                    ins = nc.vector.match_replace(gone, v[:, 0:8], src, -3.0e38)
                    if last_read and last_read[k]:
                        drain(ins, last_read[k])
                    else:
                        done[k] = mark(ins)
                for k, (src, gone, v, i) in enumerate(sources):
                    after(done[k])
                    done[k] = mark(nc.vector.max(v[:, 8:16], gone))
                for k, (src, gone, v, i) in enumerate(sources):
                    after(done[k])
                    n = mark(nc.vector.max_index(i[:, 8:16], v[:, 8:16], gone))
                after(n)

            def pick_keys(phase, g):
                sources = []
                for half, (v, ix) in enumerate((("v1", "i1"), ("v2", "i2"))):
                    b = filled(dve, ("key", phase, g, half))
                    for i in range(PAIR_HEADS):
                        sources.append((b[:, i * KEYS:(i + 1) * KEYS], keys_gone[:, 2 * half + i, :], tk[v][:, i, :], u32[ix][:, i, :]))
                top16(sources, [None, ("key", phase, g, 0), None, ("key", phase, g, 1)])

            def pick(phase, g):
                t = PHASE_TILE[phase]
                here = slice(PAIR_HEADS * g * TOPK, PAIR_HEADS * (g + 1) * TOPK)
                pairs_of = lambda v: v.rearrange("p (h k) -> p h k", h=PAIR_HEADS)
                flat_of = lambda v: v.rearrange("p h k -> p (h k)")
                for h in range(PAIR_HEADS):
                    n = mark(nc.vector.tensor_tensor(cand[:, h, :].rearrange("p (a b) -> p a b", a=TOPK),
                                                     tk["v1"][:, h, :].unsqueeze(2).to_broadcast([P, TOPK, TOPK]),
                                                     tk["v2"][:, h, :].unsqueeze(1).to_broadcast([P, TOPK, TOPK]), ALU.add))
                after(n)
                top16([(cand[:, h, :], cand_gone[:, h, :], tk["sc"][:, h, :], u32["pos"][:, h, :]) for h in range(PAIR_HEADS)])
                nc.vector.tensor_tensor(tk["exp"], tk["sc"], tk["sc"][:, :, 0:1].to_broadcast([P, PAIR_HEADS, TOPK]), ALU.subtract) \
                    .then_inc(sem("top_shifted"), 1)
                mark(nc.vector.tensor_single_scalar(u32["pa"], u32["pos"], 4, ALU.logical_shift_right))
                mark(nc.vector.tensor_single_scalar(u32["pb"], u32["pos"], TOPK - 1, ALU.bitwise_and))
                mark(nc.vector.tensor_copy(tk["i1f"], u32["i1"]))
                after(mark(nc.vector.tensor_copy(tk["i2f"], u32["i2"])))
                o = [onehot[:, k, :].rearrange("p (h k a) -> p h k a", h=PAIR_HEADS, k=TOPK) for k in range(2)]
                o3 = [onehot[:, k, :].rearrange("p (h a) -> p h a", a=TOPK) for k in range(2)]
                chosen = (("pa", "i1f", "ia"), ("pb", "i2f", "ib"))
                wide = [P, PAIR_HEADS * TOPK, TOPK]
                n = [mark(nc.vector.tensor_tensor(o3[k], flat_of(u32[place_]).unsqueeze(2).to_broadcast(wide),
                                                  cst("iota").unsqueeze(1).to_broadcast(wide), ALU.is_equal))
                     for k, (place_, _, _) in enumerate(chosen)]
                for k, (_, keys, _) in enumerate(chosen):
                    after(n[k])
                    n[k] = mark(nc.vector.tensor_tensor(o[k], o[k], tk[keys].unsqueeze(2).to_broadcast([P, PAIR_HEADS, TOPK, TOPK]), ALU.mult))
                for k, (_, _, dst) in enumerate(chosen):
                    after(n[k])
                    n[k] = mark(nc.vector.tensor_reduce(flat_of(tk[dst]), o3[k], AX.X, ALU.add))
                after(n[1])
                if phase >= 2:
                    dve.wait_ge(sem("peer_sum"), phase - 1)
                n = mark(nc.vector.scalar_tensor_tensor(out=pairs_of(eidx[:, t, here]), in0=tk["ia"], scalar=float(KEYS), in1=tk["ib"],
                                                        op0=ALU.mult, op1=ALU.add))
                dve.wait_ge(sem("top_exp"), PICKS * phase + g + 1)
                step(nc.vector.tensor_reduce(top_sum, tk["exp"], AX.X, ALU.add))
                step(nc.vector.reciprocal(top_sum, top_sum))
                nc.vector.tensor_tensor(pairs_of(gates[:, t, here]), tk["exp"],
                                        top_sum.unsqueeze(2).to_broadcast([P, PAIR_HEADS, TOPK]), ALU.mult).then_inc(sem("experts_picked"), 1)
                dve.wait_ge(sem("experts_picked"), PICKS * phase + g + 1)

            pick_keys(0, 0)
            pick(0, 0)

            def ple_norm(t):
                norm(f"ple{t}")

            def ple_up(t):
                for half in range(2):
                    c = slice(512 * half, 512 * half + 512)
                    drained(dve, ("ple_gate", t, half))
                    b = filled(dve, ("ple", t, half))
                    drain(nc.vector.tensor_tensor(ple_gate[:, c], ple_gate[:, c], b[:, :], ALU.mult), ("ple", t, half))
                nc.vector.tensor_tensor(X[:, t, :], X[:, t, :], ple_gate, ALU.add).then_inc(sem("x_ready"), 1)

            def norm1(t):
                norm(f"n1{t}")

            def log_sigmoid(name, rows, dst, signal):
                b, _ = job[name]
                z = bank[b]
                drain(nc.vector.scalar_tensor_tensor(out=dst, in0=z[0:rows, 0:256], scalar=0.0, in1=dst, op0=ALU.min, op1=ALU.subtract), name)
                nc.vector.tensor_scalar(dst, dst, 1.0 / GLA_TAU, None, ALU.mult).then_inc(sem(signal), 1)

            def low_rank(t):
                dve.wait_ge(sem("x_ready"), X_STATE[f"n1{t}"])
                nc.vector.memset(lrT[0:32, :], 1.0).then_inc(sem("ones_set"), 1)

            def gate_up(t):
                dve.wait_ge(sem("log_gate"), t + 1)
                log_sigmoid(("z", t), P, lg, "log_decay")
                if t == 0:
                    dve.wait_ge(sem("log_gate_meta"), 1)
                    log_sigmoid("z_meta", META, lg_m[0:META, :], "log_decay_meta")

            def gr(t):
                dve.wait_ge(sem("gr_sigmoid"), t + 1)
                b, _ = job[("gr", t)]
                drain(nc.vector.tensor_tensor(silu, silu, bank[b][:, :], ALU.mult), ("gr", t))

            def stick_scores(t, hg):
                nkb = t + 2
                for k in reversed(range(nkb)):
                    n = META if k == 0 else P
                    b = bank[job[("stick_z", t, hg, k)][0]]
                    tmp = sb_tmp[0:n, k % 2, :]
                    dve.wait_ge(sem("stick_soft"), STICK_BASE[t] + hg * nkb + nkb - k)
                    if hg:
                        filled(dve, ("stick_w", t, 0, 0))
                    lv = sb_log[0:n, k, :]
                    drain(nc.vector.scalar_tensor_tensor(out=lv, in0=b[0:n, :], scalar=0.0, in1=tmp, op0=ALU.max, op1=ALU.add), ("stick_z", t, hg, k))
                    if k == nkb - 1:
                        lq = lv.rearrange("p (h q) -> p h q", h=4)
                        ins = nc.vector.scalar_tensor_tensor(out=lq, in0=lq, scalar=-1.0, in1=cst("causal").unsqueeze(1).to_broadcast([P, 4, P]),
                                                             op0=ALU.mult, op1=ALU.mult)
                    else:
                        ins = nc.vector.tensor_scalar(lv, lv, -1.0, None, ALU.mult)
                    ins.then_inc(sem("stick_log"), 1)

            def stick_sums(t, hg):
                if hg:
                    attention_sums("stick_o", t, 0)

            def attention_sums(name, t, half):
                b = filled(dve, (name, t))
                drain(nc.vector.tensor_copy(hn[:, t, 512 * half:512 * half + 512], b[:, :]), (name, t))

            def gla_start(t):
                if t == 0:
                    drained(dve, "decay_meta")
                    nc.vector.tensor_tensor(klm, klm, gkT[:, :, 0:META], ALU.mult).then_inc(sem("key_meta"), 1)
                    b = filled(dve, "state_meta")
                    for h in range(GLA_HEADS):
                        e = HEAD * (h % 2)
                        ins = nc.vector.tensor_copy(state[e:e + HEAD, h // 2, :], b[e:e + HEAD, h * P:(h + 1) * P])
                        if h < GLA_HEADS - 1:
                            step(ins)
                        else:
                            drain(ins, "state_meta")

            def gla(t, dt):
                for i in range(3):
                    drained(dve, ("decay", t, dt, i))
                ev = expd.rearrange("p (l t) -> p l t", t=P)
                if dt:
                    dve.wait_ge(sem("gla_head"), 3 * t + 2)
                step(nc.vector.tensor_tensor(gla_q, ev[:, 0:LEVELS + 1, :], gqT[:, dt, :].unsqueeze(1).to_broadcast([P, LEVELS + 1, P]), ALU.mult))
                if t == 0:
                    step(nc.vector.tensor_copy(arec[:, dt:dt + 1], ev[:, INTER, P - 1:P]))
                kk = gkT[:, dt, META:META + P]
                step(nc.vector.tensor_tensor(gla_k[:, LEVELS, :], ev[:, LAST, :], kk, ALU.mult))
                nc.vector.tensor_tensor(gla_k[:, 0:LEVELS, :], ev[:, 0:LEVELS, :], kk.unsqueeze(1).to_broadcast([P, LEVELS, P]), ALU.mult) \
                    .then_inc(sem("gla_qk"), 1)
                for h in (2 * dt, 2 * dt + 1):
                    if h:
                        dve.wait_ge(sem("gla_head"), 3 * t + h)
                    for half in range(2):
                        b = filled(dve, ("gla_a", t, h, half))
                        ls = slice(4 * half, 4 * half + 4)
                        drain(nc.vector.tensor_tensor(gla_a[:, ls, :], b[:, :].rearrange("p (l t) -> p l t", l=4), pairs[:, ls, :], ALU.mult),
                              ("gla_a", t, h, half))

            def gla_end(t):
                attention_sums("gla_o", t, 1)
                if t == 0:
                    b = filled(dve, "state0")
                    for h in range(GLA_HEADS):
                        e = HEAD * (h % 2)
                        ins = nc.vector.scalar_tensor_tensor(out=state[e:e + HEAD, h // 2, :], in0=state[e:e + HEAD, h // 2, :],
                                                             scalar=arec[e:e + HEAD, h // 2:h // 2 + 1], in1=b[e:e + HEAD, h * P:(h + 1) * P],
                                                             op0=ALU.mult, op1=ALU.add)
                        if h < GLA_HEADS - 1:
                            step(ins)
                        else:
                            drain(ins, "state0")

            def mixed(t):
                for k, heads in enumerate((SB_HEADS, GLA_HEADS)):
                    o = hn[:, t, 512 * k:512 * k + 512]
                    step(nc.vector.tensor_tensor(sq2, o, o, ALU.mult))
                    ins = nc.vector.tensor_reduce(hstat[:, k, 0:heads], sq2.rearrange("p (h d) -> p h d", h=heads), AX.X, ALU.add)
                    if k == 0:
                        step(ins)
                    else:
                        ins.then_inc(sem("mix_squares"), 1)
                dve.wait_ge(sem("mix_inv_rms"), t + 1)
                for k, (heads, w) in enumerate(((SB_HEADS, HEAD), (GLA_HEADS, GLA_DV))):
                    o = hn[:, t, 512 * k:512 * k + 512]
                    ov = o.rearrange("p (h d) -> p h d", h=heads)
                    step(nc.vector.tensor_tensor(ov, ov, hstat[:, k, 0:heads].unsqueeze(2).to_broadcast([P, heads, w]), ALU.mult))
                    step(nc.vector.tensor_tensor(o, o, head_gain[:, k, :], ALU.mult))
                o = hn[:, t, 512:D]
                nc.vector.tensor_tensor(o, o, silu, ALU.mult).then_inc(sem("mixed"), 1)

            def out2(t, half):
                c = slice(512 * half, 512 * half + 512)
                name = ("out2", half, t)
                b = filled(dve, name)
                drain(nc.vector.tensor_tensor(X[:, t, c], X[:, t, c], b[:, :], ALU.add), name)
                if half:
                    nc.vector.tensor_copy(amax[:, 12:13], X[:, t, 0:1]).then_inc(sem("x_ready"), 1)

            def norm2(t):
                norm(f"n2{t}")

            def final(t):
                norm(f"f{t}")

            STEPS = {"pick_keys": pick_keys, "pick": pick, "ple_norm": ple_norm, "ple_up": ple_up, "norm1": norm1, "low_rank": low_rank,
                     "gate_up": gate_up, "gr": gr, "stick_scores": stick_scores, "stick_sums": stick_sums, "gla_start": gla_start,
                     "gla": gla, "gla_end": gla_end, "mixed": mixed, "out2": out2, "norm2": norm2, "final": final}

            def background(steps):
                for name, *where in steps:
                    if name in STEPS:
                        STEPS[name](*where)

            for phase in range(PHASES):
                t = PHASE_TILE[phase]
                for steps, lo, hi in segments(phase):
                    background(steps)
                    with dve.Fori(lo, hi) as i:
                        it = i + phase * ITERS
                        for j in range(RING // CHUNK):
                            for s in range(CHUNK * j, CHUNK * (j + 1)):
                                dve.wait_ge(sem(f"row_in{s}"), (it + 1) * 16)
                                u = ring[:, s, 0:D]
                                nc.vector.tensor_tensor_reduce(out=u, in0=u, in1=hn[:, t, :], scale=1.0, scalar=0.0, op0=ALU.mult, op1=ALU.add,
                                                               accum_out=dot[:, s:s + 1]).then_inc(sem("dots"), 1)
                            c = slice(CHUNK * j, CHUNK * (j + 1))
                            dve.wait_ge(sem("gelu"), it * (RING // CHUNK) + j + 1)
                            nc.vector.tensor_tensor(weight[:, c], act_dot[:, c], gates[:, t, bass.ds(i * RING + CHUNK * j, CHUNK)], ALU.mult) \
                                .then_inc(sem("weights_ready"), 1)
                dve.wait_ge(sem("peer_sum"), phase + 1)
                nc.vector.tensor_copy(X[:, t, :].rearrange("p (h d) -> p h d", h=2), acc[:, :, :]).then_inc(sem("x_ready"), 1)
            norm("f1")


SMALL_IN = 16 * 7
STICK_BASE = [0, 4]


def units_of(w, width=256):
    n = w.shape[1]
    return [np.ascontiguousarray(w[:, c:c + width].reshape(w.shape[0] // P, P, width).transpose(1, 0, 2)).reshape(P, -1)
            for c in range(0, n, width)]


def layout(i):
    const, dil = constants()
    w_in = i["w_in"][0]
    w_in = np.concatenate([w_in[:, 0:1024], w_in[:, 1536:3072], w_in[:, 1024:1536], w_in[:, 3072:5888]], 1)
    units = units_of(w_in)
    units += units_of(i["w_branch_na"][0], 512) + units_of(i["w_branch_dil"][0], 1024)
    units += units_of(i["w_out"][0]) + units_of(i["peer_w_query"][0])
    units += units_of(i["w_ple_gate"][0]) + units_of(i["w_ple"][0], 1024)
    w2 = i["w_in_2"][0]
    for lo, hi in ((512, 1024), (0, 512), (1792, 2048), (1536, 1792), (1024, 1536), (2048, 2560), (2560, 3072)):
        units += units_of(w2[:, lo:hi])
    units += units_of(i["w_out_2"][0]) + units_of(i["w_peer_q_2"][0])
    assert len(units) == N_UNITS and all(u.shape == (P, UNIT) for u in units)
    qc = np.arange(P) % GRID_W
    half = np.arange(P) // GRID_W
    rows = np.arange(6)[None, :, None] + 5 - half[:, None, None]
    cols = np.clip(np.arange(GRID_W)[None, None] - qc[:, None, None] + NA_WIN_COLS - 1, 0, 2 * NA_WIN_COLS - 2)
    bias = i["na_rel_bias"][0][:, rows, cols].transpose(1, 0, 2, 3)
    qk = np.stack([i["qk_norm_na"][0, 0], i["qk_norm_na"][0, 1], i["qk_norm_dil"][0, 0], i["qk_norm_dil"][0, 1]])
    cols_of = lambda g: g.reshape(DC, P).T
    keys2 = np.concatenate([i["sub_keys1_2"][0].transpose(2, 0, 1), i["sub_keys2_2"][0].transpose(2, 0, 1)], 0)
    return {
        "x": i["x"][0],
        "meta": i["meta_tokens_2"],
        "weights": np.stack(units),
        "const": const,
        "dil_mask": dil,
        "na_bias": bias.reshape(P, NA_HEADS, 6 * GRID_W),
        "gain": np.stack([i["norm_ffn"][0], i["norm2_g_2"][0], i["norm_f_g_2"]]),
        "head_gain": np.stack([i["sb_norm_g_2"][0], i["gla_norm_g_2"][0]]),
        "gain_col": np.stack([cols_of(i["norm_mix"][0]), cols_of(i["norm_ple"][0]), cols_of(i["norm1_g_2"][0])], 1),
        "qk_gain": qk,
        "keys1": i["peer_sub_keys"][0].transpose(2, 0, 1),
        "keys2": keys2,
        "pT": i["p"][0, 0].T.reshape(2, P, SEQ).transpose(1, 0, 2),
        "w_lr": w2[:, 3072:3088].reshape(DC, P, RANK).transpose(1, 0, 2),
        "w_gu": np.concatenate([i["w_gate_up_2"][0], i["b_gate_up_2"]], 0),
        "experts1": np.concatenate([i["peer_expert_u"][0], i["peer_expert_v"][0]], 1),
        "experts2": np.concatenate([i["expert_u_2"][0], i["expert_v_2"][0]], 1),
    }


def kernel(**inputs):
    import concourse.bacc as bacc
    from concourse.bass_utils import run_bass_kernel_spmd

    nc = bacc.Bacc("TRN2", target_bir_lowering=False, num_devices=1)
    arrays = {"in_" + k: np.ascontiguousarray(v) for k, v in layout({k: np.asarray(v) for k, v in inputs.items()}).items()}
    aps = {k[3:]: nc.dram_tensor(k, v.shape, mybir.dt.from_np(v.dtype), kind="ExternalInput").ap() for k, v in arrays.items()}
    out = nc.dram_tensor("out", (SEQ, D), F32, kind="ExternalOutput").ap()
    build(nc, aps, out)
    r = run_bass_kernel_spmd(nc, [arrays], core_ids=[0])
    return r.results[0]["out"].reshape(1, SEQ, D)
```

```python
from contextlib import ExitStack

import numpy as np

import concourse.bass as bass
from concourse import mybir

F32 = mybir.dt.float32
F32R = mybir.dt.float32r
U32 = mybir.dt.uint32
ALU = mybir.AluOpType
ACT = mybir.ActivationFunctionType
AX = mybir.AxisListType

P = 128
D = 1024
DC = D // P
TILES = 2
SEQ = TILES * P
EPS = 1e-6
NEG = -1e30
META = 16
HEAD = 64
NA_HEADS = 8
DIL_GROUPS, DIL_SLOTS = 3, 4
DIL_HEADS = DIL_GROUPS * DIL_SLOTS
GRID_W = 64
NA_WIN_COLS = 16
ROT_HALF = 8
ROPE_THETA = 500000.0
QK_HEADS = 2 * NA_HEADS + 2 * DIL_HEADS
PAIRS = QK_HEADS // 2
V_COLS = (NA_HEADS + DIL_HEADS) * HEAD
SB_HEADS = 8
GLA_HEADS, GLA_DK, GLA_DV = 4, 64, 128
RANK = 16
GLA_TAU = 16.0
LEVELS = 8
INTER, LAST = LEVELS, LEVELS + 1
PEER_HEADS, KEYS, TOPK = 8, 128, 16
SLOTS = PEER_HEADS * TOPK

RING = 8
ITERS = SLOTS // RING
DVE_SLOTS = (3, 7)
PE_SLOTS = tuple(s for s in range(RING) if s not in DVE_SLOTS)
PHASES = 4
PAIR_HEADS = 2
PICKS = PEER_HEADS // PAIR_HEADS
PICK_ITERS = ITERS // PICKS
WSLOTS = 4
UNIT = 2048
HALF = UNIT // 2
LOW_DVE = HALF // 2
BANKS = 5
OUT_BANK = BANKS

N_IN, N_BRANCH, N_OUT, N_Q1 = 23, 3, 4, 8
N_GATES = 8
N_SPLIT = 2 * (N_IN - N_GATES)
ACT_SPLIT = N_SPLIT - 4
ATT_UNITS = 4 + DIL_SLOTS
assert TILES * ATT_UNITS == 2 * N_GATES
N_FIRST = N_IN + N_BRANCH + N_OUT + N_Q1
N_TILE = 4 + 1 + 12 + 4 + 4
N_UNITS = N_FIRST + N_TILE
N_LOADS = N_FIRST + TILES * N_TILE

SIG_AT = PAIRS * SEQ + TILES * V_COLS

_at = 0
CONST = {}
for _name, _n in (("ident", P), ("decay", (LEVELS + 2) * P), ("pairs", LEVELS * P), ("later", P), ("ones", P),
                  ("causal", P), ("causal_neg", P), ("iota", TOPK), ("rope", TILES * 2 * ROT_HALF),
                  ("na_cols", GRID_W), ("decay_meta", META)):
    CONST[_name] = (_at, _at + _n)
    _at += _n
N_CONST = _at


def constants():
    c = np.zeros((P, N_CONST), np.float32)

    def put(name, a):
        lo, hi = CONST[name]
        c[:a.shape[0], lo:hi] = a.reshape(a.shape[0], hi - lo)

    i = np.arange(P)
    put("ident", np.eye(P, dtype=np.float32))
    decay = np.zeros((P, LEVELS + 2, P), np.float32)
    pairs = np.zeros((P, LEVELS, P), np.float32)
    pairs[:, 0] = np.eye(P)
    for level in range(1, LEVELS):
        half = 1 << (level - 1)
        mid = (i // (2 * half)) * 2 * half + half
        right = i >= mid
        s, t = i[:, None], i[None, :]
        decay[:, level] = np.where(right[None], (s >= mid[None]) & (s <= t), (s > t) & (s < mid[None]))
        pairs[:, level] = (mid[:, None] == mid[None]) & ~right[:, None] & right[None]
    decay[:, INTER] = i[:, None] <= i[None]
    decay[:, LAST] = i[:, None] > i[None]
    put("decay", decay)
    put("pairs", pairs)
    put("later", (i[:, None] >= i[None]).astype(np.float32))
    put("ones", np.ones((P, P), np.float32))
    put("causal", (i[:, None] < i[None]).astype(np.float32))
    put("causal_neg", np.where(i[:, None] < i[None], 0.0, NEG).astype(np.float32))
    put("iota", np.tile(np.arange(TOPK, dtype=np.float32), (P, 1)))
    freq = np.power(np.float32(ROPE_THETA), -np.arange(ROT_HALF, dtype=np.float32) * 2.0 / (2 * ROT_HALF))
    angle = np.arange(SEQ, dtype=np.float32)[:, None] * freq.astype(np.float32)[None]
    rope = np.stack([np.cos(angle), np.sin(angle)], 1).reshape(TILES, P, 2 * ROT_HALF)
    put("rope", rope.transpose(1, 0, 2).astype(np.float32))
    qc = i % GRID_W
    start = np.clip(qc - NA_WIN_COLS // 2, 0, GRID_W - NA_WIN_COLS)[:, None]
    kc = np.arange(GRID_W)[None]
    put("na_cols", np.where((kc >= start) & (kc < start + NA_WIN_COLS), 0.0, NEG).astype(np.float32))
    m = np.arange(META)
    put("decay_meta", (m[:, None] > m[None]).astype(np.float32))
    q = np.arange(SEQ)[:, None]
    k = np.arange(SEQ)[None]
    seen = np.stack([np.abs(q - k) <= 64, (q - k) % 4 == 0, (q - k) % 16 == 0], 1)
    dil = np.where(seen, 0.0, NEG).astype(np.float32).reshape(TILES, P, DIL_GROUPS * SEQ)
    return c, np.ascontiguousarray(dil.transpose(1, 0, 2))


def build(nc, a, out):
    ctx = ExitStack()
    with ctx:
        def sb(name, shape, dt=F32):
            return ctx.enter_context(nc.sbuf_tensor(name, [P, *shape], dt))

        sems = {}

        def sem(name):
            if name not in sems:
                sems[name] = ctx.enter_context(nc.semaphore(name))
            return sems[name]

        with ExitStack() as early:
            def sb_early(name, shape, dt=F32R):
                return early.enter_context(nc.sbuf_tensor(name, [P, *shape], dt))

            sb_early("behind", [SIG_AT], F32)
            hT_high = sb_early("hT_high", [DC, SEQ])
            hT_low = sb_early("hT_low", [DC, SEQ])
            sb_early("between", [RING * 2 * D - SIG_AT - TILES * 2 * D], F32)
            w_high = sb_early("w_high", [2, HALF])
            w_low = sb_early("w_low", [2, HALF])
        ring = sb("ring", [RING, 2 * D])
        query2T = sb("query2T", [PEER_HEADS, P])
        sbk = sb("sbk", [4, META + SEQ])
        sbv = sb("sbv", [3, 512])
        gv = sb("gv", [512])
        state = sb("state", [2, GLA_DV])
        diag = sb("diag", [RING, P])
        pick_tmp = sb("pick_tmp", [13 * PAIR_HEADS * TOPK + 1024 + PAIR_HEADS])
        wring = sb("wring", [WSLOTS, UNIT])
        work = sb("work", [7168])
        X = sb("X", [TILES, D])
        hn = sb("hn", [TILES, D])
        hT = sb("hT", [DC, META + SEQ])
        const = sb("const", [N_CONST])
        gain = sb("gain", [1, D])
        head_gain = sb("head_gain", [2, 512])
        gain_col = sb("gain_col", [3, DC])
        keys1 = sb("keys1", [2, KEYS])
        keys2 = sb("keys2", [PEER_HEADS, KEYS])
        pT = sb("pT", [2, SEQ])
        w_lr = sb("w_lr", [DC, RANK])
        w_gu = sb("w_gu", [GLA_HEADS * GLA_DK])
        eidx = sb("eidx", [TILES, SLOTS], U32)
        gates = sb("gates", [TILES, SLOTS])
        slot_idx = sb("slot_idx", [RING], U32)
        dot = sb("dot", [RING])
        act_dot = sb("act_dot", [RING])
        weight = sb("weight", [len(DVE_SLOTS)])
        fence = sb("fence", [1])
        stat = sb("stat", [32])
        hstat = sb("hstat", [2, QK_HEADS])
        amax = sb("amax", [4])
        signal_tmp = sb("signal_tmp", [1])
        asum = sb("asum", [TILES, 16])
        arec = sb("arec", [16])

        def cst(name, rows=P):
            lo, hi = CONST[name]
            return const[0:rows, lo:hi]

        ident = cst("ident")
        decay = cst("decay")
        pairs = cst("pairs").rearrange("p (l t) -> p l t", l=LEVELS)
        zeros = decay[:, 0:P]

        flat = ring[:, :, :].rearrange("p a b -> p (a b)")

        def cut(base, at, *shape):
            n = int(np.prod(shape))
            v = base[:, at:at + n]
            if len(shape) == 2:
                v = v.rearrange("p (a b) -> p a b", a=shape[0])
            if len(shape) == 3:
                v = v.rearrange("p (a b c) -> p a b c", a=shape[0], b=shape[1])
            return v

        qkT = cut(flat, 0, PAIRS, SEQ)
        val = cut(flat, PAIRS * SEQ, TILES, V_COLS)
        sig = cut(flat, SIG_AT, TILES, 2 * D)
        na_bias = cut(flat, 11776, NA_HEADS, 6 * GRID_W)
        dil_mask = cut(flat, 14848, TILES, DIL_GROUPS * SEQ)
        meta_x = cut(work, 4096, D)
        meta_h = cut(work, 4096 + D, D)
        raw = cut(work, 0, TILES, QK_HEADS * HEAD)
        sq = cut(work, 5120, 512)
        qk_gain = cut(work, 6400, 4, HEAD)
        rot = cut(work, 5632, 4, 2 * DIL_HEADS * ROT_HALF)
        prob = [hn[:, b, 0:768] for b in range(2)]
        probT = cut(work, 5632, 2, 768)
        attn = [raw[:, t, 0:768] for t in range(TILES)]
        qpT = cut(work, 0, 2 * PEER_HEADS, SEQ)
        tk = {n: cut(pick_tmp, PAIR_HEADS * TOPK * k, PAIR_HEADS, TOPK)
              for k, n in enumerate(("v1", "v2", "i1f", "i2f", "sc", "pos", "pa", "pb", "ia", "ib", "i1", "i2", "exp"))}
        at = len(tk) * PAIR_HEADS * TOPK
        cand = cut(pick_tmp, at, PAIR_HEADS, TOPK * TOPK)
        cand_gone = cut(pick_tmp, at + 512, PAIR_HEADS, TOPK * TOPK)
        top_sum = cut(pick_tmp, at + 1024, PAIR_HEADS)
        keys_gone = cut(pick_tmp, at, 2 * PAIR_HEADS, KEYS)
        onehot = cut(pick_tmp, at, 2, PAIR_HEADS * TOPK * TOPK)
        ple_gate = cut(work, 0, D)
        sb_log = cut(work, 0, 3, 512)
        sb_tmp = cut(work, 1536, 2, 512)
        sb_a = cut(work, 2560, 3, 512)
        sbq = cut(work, 4096, 4, P)
        gqT = cut(work, 4608, 2, P)
        gkT = cut(work, 4864, 2, META + P)
        lg = cut(work, 5152, 256)
        lrT = cut(work, 5408, META + P)
        silu = cut(work, 5552, 512)
        lg_m = cut(work, 6064, 256)
        klast = cut(work, 6320, 2, P)
        klm = cut(work, 6576, 2, META)
        gvm = cut(work, 6608, 512)
        expd = cut(work, 0, (LEVELS + 2) * P)
        gla_q = cut(work, 1280, LEVELS + 1, P)
        gla_k = cut(work, 2432, LEVELS + 1, P)
        gla_a = cut(work, 3584, LEVELS, P)
        gla_w = cut(work, 6064, 2, P)
        squares = cut(work, 1536, 512)

        acc = ctx.enter_context(nc.psum_tensor("acc", [P, 2, 512], F32))
        bank = [ctx.enter_context(nc.psum_tensor(f"bank{b}", [P, 512], F32)) for b in range(BANKS + 1)]

        na_sums = [acc[:, 0, :], bank[OUT_BANK][:, :]]
        dil_sums = [acc[:, 1, t * DIL_SLOTS * HEAD:(t + 1) * DIL_SLOTS * HEAD] for t in range(TILES)]

        job = {}
        turns = {"short": 0, "out": 0}

        def place(name):
            assert name not in job, name
            if name[0] in ("stick_o", "gla_o"):
                b, turn = OUT_BANK, turns["out"]
                turns["out"] += 1
            else:
                b, turn = turns["short"] % BANKS, turns["short"] // BANKS
                turns["short"] += 1
            job[name] = (b, turn)
            return bank[b]

        def filled(eng, name):
            b, turn = job[name]
            eng.wait_ge(sem(f"bank_filled{b}"), turn + 1)
            return bank[b]

        def drained(eng, name):
            b, turn = job[name]
            eng.wait_ge(sem(f"bank_drained{b}"), turn + 1)

        def drain_sem(name):
            return sem(f"bank_drained{job[name][0]}"), job[name][1] + 1

        def fills_bank(k):
            return k % 4 == 3 or k == N_SPLIT - 1

        def half_used(eng, k):
            if fills_bank(k):
                filled(eng, ("in", k // 4, TILES - 1))
            else:
                eng.wait_ge(sem("half_used"), k + 1 - (k + 1) // 4)

        def rows_parts(t):
            cols = slice(t * P, (t + 1) * P)
            return hT[:, :, META + t * P:META + (t + 1) * P], hT_high[:, :, cols], hT_low[:, :, cols]

        def weights_half(eng, k):
            n = k // 2
            eng.wait_ge(sem(f"weights_in{n % WSLOTS}"), 16 * (n // WSLOTS + 1))
            if k >= 2:
                half_used(eng, k - 2)
            return wring[:, n % WSLOTS, (k % 2) * HALF:(k % 2 + 1) * HALF], w_high[:, k % 2, :], w_low[:, k % 2, :]

        def na_head(u, i):
            return 4 * (u // 2) + u % 2 + 2 * i

        NORMS = ["ffn0", "ffn1", "meta", "ple0", "n10", "n20", "ple1", "n11", "n21", "f0", "f1"]
        norm_no = {n: i for i, n in enumerate(NORMS)}
        mix_inv = stat[:, len(NORMS):len(NORMS) + TILES]
        GAIN_COL = {"mix": 0, "meta": 2, "ple": 1, "n1": 2}
        GAIN_ROW = {"ffn": 0, "n2": 1, "f": 2}

        def key_rows(k):
            return META if k == 0 else P

        def stick_tmp(k):
            return silu[0:META, :] if k == 0 else sb_tmp[:, k - 1, :]

        def norm_place(name):
            if name == "meta":
                return None, meta_x[0:META, :], meta_h[0:META, :], slice(0, META), META
            t = int(name[-1])
            return t, X[:, t, :], hn[:, t, :], slice(META + t * P, META + (t + 1) * P), P

        X_STATE = {"ffn0": 1, "ffn1": 2, "ple0": 3, "n10": 4, "n20": 5, "ple1": 6, "n11": 7, "n21": 8,
                   "f0": 9, "f1": 10}
        PHASE_TILE = [0, 1, 0, 1]
        PHASE_OPEN = [1, 3, 6, 9]

        def block2_steps(t):
            ple, n1, n2 = f"ple{t}", f"n1{t}", f"n2{t}"

            def own(step, g):
                return [(step, 2, g)] if t == 1 else []

            return {0: [("norm_rows", ple), ("norm_cols", ple), *own("pick_keys", 1), ("ple_gate", t, 0)],
                    1: [("ple_gate", t, 1), ("ple_up", t), ("norm_rows", n1)],
                    2: [("norm_cols", n1), ("sbk", t)],
                    3: [*own("pick", 1), ("sbq", t), ("low_rank", t), ("stick_scores", t, 0)],
                    4: [("stick_log", t, 0), ("gla_keys", t), ("gate_up", t)],
                    5: [*own("pick_keys", 2), ("stick_sums", t, 0), *own("pick", 2), ("stick_scores", t, 1), ("sbv", t)],
                    6: [("stick_log", t, 1), ("stick_out", t, 0), ("gv", t)],
                    7: [*own("pick_keys", 3), ("stick_sums", t, 1), *own("pick", 3), ("gr", t)],
                    8: [("stick_out", t, 1), ("gla_start", t), ("gla_decay", t, 0)],
                    9: [("gla_qk", t, 0), ("gla_heads", t, 0), ("gla_decay", t, 1)],
                    10: [("gla_qk", t, 1), ("gla_heads", t, 1), ("gla_end", t)],
                    11: [("mixed_rows", t), ("mixed_cols", t), ("out2", t, 0)],
                    12: [("out2", t, 1), ("norm_rows", n2)],
                    13: [("norm_cols", n2), ("query2", t, 0)],
                    14: [("pick_keys", 2 + t, 0), ("query2", t, 1)],
                    15: [("pick", 2 + t, 0)]}

        PLAN = [{} for _ in range(PHASES)]

        def plan(phase, steps):
            for turn, names in steps.items():
                PLAN[phase].setdefault(turn, []).extend(names)

        for g in range(1, PICKS):
            plan(0, {2 * g - 2: [("query1", g)], 2 * g - 1: [("pick_keys", 0, g)], 2 * g: [("pick", 0, g)]})
            plan(3, {3 * g - 2: [("pick_keys", 3, g)], 3 * g - 1: [("pick", 3, g)]})
        for g in range(PICKS):
            plan(0, {2 * g + 7: [("pick_keys", 1, g)], 2 * g + 8: [("pick", 1, g)]})
        plan(0, {6: [("norm_rows", "meta"), ("norm_cols", "meta")]})
        plan(1, block2_steps(0))
        plan(2, block2_steps(1))
        plan(3, {6: [("final", 0)]})

        def segments(phase):
            turns_at = sorted(PLAN[phase])
            if turns_at[0]:
                yield [], 0, turns_at[0]
            for k, turn in enumerate(turns_at):
                yield PLAN[phase][turn], turn, turns_at[k + 1] if k + 1 < len(turns_at) else ITERS

        block = ctx.enter_context(nc.Block())

        @block.tensor
        def _(pe):
            units = [0]

            def unit():
                n = units[0]
                units[0] += 1
                pe.wait_ge(sem(f"weights_in{n % WSLOTS}"), 16 * (n // WSLOTS + 1))
                return wring[:, n % WSLOTS, :]

            def begun(ins):
                ins.then_inc(sem("unit_begun"), 1)

            def open_bank(name):
                b = place(name)
                n, turn = job[name]
                if turn:
                    pe.wait_ge(sem(f"bank_drained{n}"), turn)
                return b

            def fill(ins, name):
                ins.then_inc(sem(f"bank_filled{job[name][0]}"), 1)

            def turn_rows(name, src, rows, chunks=DC):
                for half in range(-(-chunks // 4)):
                    b = open_bank((name, half))
                    n = min(4, chunks - 4 * half)
                    for i in range(n):
                        c = 4 * half + i
                        ins = nc.tensor.transpose(b[:, i * rows:(i + 1) * rows], src[:, c * P:(c + 1) * P],
                                                  ident[0:rows, 0:rows])
                    fill(ins, (name, half))

            def norm(name):
                _, _, rows, _, n = norm_place(name)
                pe.wait_ge(sem("rows_normed"), norm_no[name] + 1)
                turn_rows(name, rows, n)

            def to_rows(b, lo, w, cols, n_cols=256, rows=None, first=None):
                m = cols.stop - cols.start
                wv = w.rearrange("p (c n) -> p c n", c=DC)
                for c in range(DC):
                    ins = nc.tensor.matmul(b[0:m, lo:lo + n_cols], hT[:, c, cols], wv[:, c, :],
                                           start=(c == 0), stop=(c == DC - 1))
                    if c == 0 and first:
                        begun(ins)
                return ins

            def to_cols(b, w, cols, first=True, at=0):
                m = cols.stop - cols.start
                wv = w.rearrange("p (c n) -> p c n", c=DC)
                for ct in range(2):
                    for c in range(DC):
                        ins = nc.tensor.matmul(b[:, at + ct * m:at + (ct + 1) * m], wv[:, c, ct * P:(ct + 1) * P],
                                               hT[:, c, cols], start=(c == 0), stop=(c == DC - 1))
                        if first and ct == 0 and c == 0:
                            begun(ins)
                return ins

            tile_cols = [slice(META + t * P, META + (t + 1) * P) for t in range(TILES)]

            pe.wait_ge(sem("ident_in"), 16)
            for t in range(TILES):
                pe.wait_ge(sem(f"x_in{t}"), 16)
                turn_rows(f"mix{t}", X[:, t, :], P)

            def project_in(u):
                unit()
                names = [("in", u // 2, t) for t in range(TILES)]
                if u % 2 == 0:
                    for name in names:
                        open_bank(name)
                lo = 256 * (u % 2)
                for half in range(2):
                    k = 2 * u + half
                    if k < ACT_SPLIT:
                        pe.wait_ge(sem("high_ready"), k + 1)
                        pe.wait_ge(sem("low_ready_dve"), k + 1)
                    else:
                        pe.wait_ge(sem("high_ready_act"), k + 1 - ACT_SPLIT)
                    pe.wait_ge(sem("low_ready_pool"), k + 1)
                    wh, wl = [v[:, k % 2, :].rearrange("p (c n) -> p c n", c=DC // 2) for v in (w_high, w_low)]
                    for t in range(TILES):
                        if k < 2:
                            pe.wait_ge(sem("rows_low_pool" if half else "rows_low_dve"), t + 1)
                        sums = bank[job[names[t]][0]][:, lo:lo + 256]
                        for i in range(DC // 2):
                            c = half * DC // 2 + i
                            xh, xl = [v[:, c, t * P:(t + 1) * P] for v in (hT_high, hT_low)]
                            for j, (x, w) in enumerate(((xh, wh), (xl, wh), (xh, wl))):
                                ins = nc.tensor.matmul(sums, x, w[:, i, :], start=(c + j == 0), stop=(c + j == DC + 1))
                                if half == 0 and t == 0 and i + j == 0:
                                    begun(ins)
                        if fills_bank(k):
                            fill(ins, names[t])
                        elif t == TILES - 1:
                            ins.then_inc(sem("half_used"), 1)

            def project_gate(g, t, w):
                fill(to_rows(open_bank(("gate", g, t)), 0, w, tile_cols[t], first=(t == 0)), ("gate", g, t))

            for u in range(N_IN - N_GATES):
                project_in(u)
            pe.wait_ge(sem("const_in"), 16)
            for t in range(TILES):
                pe.wait_ge(sem("qk_ready"), t + 1)
                turn_rows(("qkT", t), raw[:, t, :], P, PAIRS)
            for t in range(TILES):
                drained(pe, (("qkT", t), 4))

            def scores(n):
                t, u = divmod(n, ATT_UNITS)
                q_cols = slice(t * P, (t + 1) * P)
                for i in range(2 if u < 4 else 3):
                    if u < 4:
                        qh, kh = na_head(u, i), NA_HEADS + na_head(u, i)
                    else:
                        qh = 2 * NA_HEADS + i * DIL_SLOTS + u - 4
                        kh = qh + DIL_HEADS
                    if i % 2 == 0:
                        b = open_bank(("score", t, u, i // 2))
                    e = HEAD * (qh % 2)
                    ins = nc.tensor.matmul(b[:, (i % 2) * SEQ:(i % 2 + 1) * SEQ], qkT[e:e + HEAD, qh // 2, q_cols],
                                           qkT[e:e + HEAD, kh // 2, :], start=True, stop=True)
                    if i == 1 or (u >= 4 and i == 2):
                        fill(ins, ("score", t, u, i // 2))

            def turn_probs(n):
                t, u = divmod(n, ATT_UNITS)
                pe.wait_ge(sem("prob_ready"), n + 1)
                turn_rows(("probT", t, u), prob[n % 2], P, 4 if u < 4 else 6)

            def weigh(n):
                t, u = divmod(n, ATT_UNITS)
                drained(pe, (("probT", t, u), 0 if u < 4 else 1))
                if n == 0:
                    drained(pe, ("in", 7, 1))
                pt = probT[:, n % 2, :]
                for i in range(2 if u < 4 else 1):
                    blocks = 2 if u < 4 else 6
                    for k in range(blocks):
                        if u < 4:
                            h = na_head(u, i)
                            o, col = na_sums[t][:, h * HEAD:(h + 1) * HEAD], h * HEAD
                            p = pt[:, (2 * i + k) * P:(2 * i + k + 1) * P]
                        else:
                            o = dil_sums[t][:, (u - 4) * HEAD:(u - 3) * HEAD]
                            col = (NA_HEADS + (k // 2) * DIL_SLOTS + u - 4) * HEAD
                            p = pt[:, k * P:(k + 1) * P]
                        ins = nc.tensor.matmul(o, p, val[:, k % 2, col:col + HEAD], start=(k == 0), stop=(k == blocks - 1))
                ins.then_inc(sem("weighed"), 1)

            scores(0)
            scores(1)
            for n in range(TILES * ATT_UNITS):
                turn_probs(n)
                if n % 2 == 0:
                    gate_unit = unit()
                project_gate(n // 2, n % 2, gate_unit)
                if n + 2 < TILES * ATT_UNITS:
                    scores(n + 2)
                weigh(n)
            for t in range(TILES):
                pe.wait_ge(sem("attn_ready"), t + 1)
                turn_rows(("attnT", t), attn[t], P, 6)
            for t in range(TILES):
                drained(pe, (("attnT", t), 1))
            for half in range(2):
                w = unit().rearrange("p (c n) -> p c n", c=4)
                for t in range(TILES):
                    b = open_bank(("na", half, t))
                    for c in range(4):
                        ins = nc.tensor.matmul(b[:, :], hT[:, c, tile_cols[t]], w[:, c, :], start=(c == 0), stop=(c == 3))
                        if c == 0 and t == 0:
                            begun(ins)
                    fill(ins, ("na", half, t))
            w = unit().rearrange("p (c n) -> p c n", c=2)
            for t in range(TILES):
                for half in range(2):
                    b = open_bank(("dil", half, t))
                    for c in range(2):
                        ins = nc.tensor.matmul(b[:, :], hT[:, 4 + c, tile_cols[t]], w[:, c, half * 512:(half + 1) * 512],
                                               start=(c == 0), stop=(c == 1))
                        if c == 0 and t == 0 and half == 0:
                            begun(ins)
                    fill(ins, ("dil", half, t))
            for t in range(TILES):
                pe.wait_ge(sem("merged"), t + 1)
                turn_rows(("mergedT", t), hn[:, t, :], P)

            out_units = []
            for t in range(TILES):
                drained(pe, (("mergedT", t), 1))
                for half in range(2):
                    b = open_bank(("out1", half, t))
                    for u in range(2):
                        if t == 0:
                            out_units.append(unit())
                        ins = to_rows(b, 256 * u, out_units[2 * half + u], tile_cols[t], first=(t == (half + u > 0)))
                    fill(ins, ("out1", half, t))

            def query1(g):
                w = [unit() for _ in range(PAIR_HEADS)]
                for t in range(TILES):
                    if g == 0:
                        norm(f"ffn{t}")
                        drained(pe, (f"ffn{t}", 1))
                    b = open_bank(("query1", g, t))
                    for i in range(PAIR_HEADS):
                        ins = to_cols(b, w[i], tile_cols[t], first=(t == (i > 0)), at=2 * P * i)
                    fill(ins, ("query1", g, t))
                    if t == 0 and g == 0:
                        pick_keys(0, 0)

            def key_scores(phase, g):
                t = PHASE_TILE[phase]
                for half in range(2):
                    b = open_bank(("key", phase, g, half))
                    for i in range(PAIR_HEADS):
                        h = PAIR_HEADS * g + i
                        e = HEAD * half
                        if phase < 2:
                            q, k = qpT[:, 2 * h + half, t * P:(t + 1) * P], keys1[:, half, :]
                        else:
                            q, k = query2T[e:e + HEAD, h, :], keys2[e:e + HEAD, h, :]
                        ins = nc.tensor.matmul(b[:, i * P:(i + 1) * P], q, k, start=True, stop=True)
                    fill(ins, ("key", phase, g, half))

            def pick_keys(phase, g):
                if phase < 2:
                    drained(pe, ("query1", g, PHASE_TILE[phase]))
                elif g % 2 == 0:
                    drained(pe, ("query2", phase - 2, g // 2))
                key_scores(phase, g)

            pe.wait_ge(sem("small_in"), SMALL_IN)
            query1(0)

            def norm_cols(name):
                norm(name)
                drained(pe, (name, 1))

            def ple_gate_(t, half):
                name = ("ple_gate", t, half)
                b = open_bank(name)
                for u in range(2):
                    ins = to_rows(b, 256 * u, unit(), tile_cols[t], first=True)
                fill(ins, name)

            def ple_up(t):
                w = unit().rearrange("p (c n) -> p c n", c=2)
                for half in range(2):
                    b = open_bank(("ple", t, half))
                    for c in range(2):
                        ins = nc.tensor.matmul(b[:, :], pT[:, c, t * P:(t + 1) * P], w[:, c, half * 512:(half + 1) * 512],
                                               start=(c == 0), stop=(c == 1))
                        if c == 0 and half == 0:
                            begun(ins)
                    fill(ins, ("ple", t, half))

            def block2_cols(t):
                return slice(0, META + P) if t == 0 else tile_cols[t]

            def sbk_(t):
                for i in range(2):
                    fill(to_cols(open_bank(("sbk", t, i)), unit(), block2_cols(t)), ("sbk", t, i))

            def sbq_(t):
                b = open_bank(("sbq", t))
                for i in range(2):
                    ins = to_cols(b, unit(), tile_cols[t], at=2 * P * i)
                fill(ins, ("sbq", t))

            def low_rank(t):
                kc = block2_cols(t)
                b = open_bank(("lr", t))
                for c in range(DC):
                    ins = nc.tensor.matmul(b[0:RANK, 0:kc.stop - kc.start], w_lr[:, c, :], hT[:, c, kc], start=(c == 0), stop=(c == DC - 1))
                fill(ins, ("lr", t))

            def gla_keys(t):
                fill(to_cols(open_bank(("gk", t)), unit(), block2_cols(t)), ("gk", t))
                fill(to_cols(open_bank(("gq", t)), unit(), tile_cols[t]), ("gq", t))

            def gate_up(t):
                drained(pe, ("lr", t))
                b = open_bank(("z", t))
                ins = nc.tensor.matmul(b[:, 0:256], lrT[0:RANK + 1, META:META + P], w_gu[0:RANK + 1, :], start=True, stop=True)
                fill(ins, ("z", t))
                if t == 0:
                    b = open_bank("z_meta")
                    ins = nc.tensor.matmul(b[0:META, 0:256], lrT[0:RANK + 1, 0:META], w_gu[0:RANK + 1, :], start=True, stop=True)
                    fill(ins, "z_meta")

            def token_rows(name, t, meta):
                b = open_bank((name, t))
                bm = open_bank((name, "meta")) if meta else None
                for i in range(2):
                    w = unit()
                    ins = to_rows(b, 256 * i, w, tile_cols[t], first=True)
                    if i == 1:
                        fill(ins, (name, t))
                    if meta:
                        ins = to_rows(bm, 256 * i, w, slice(0, META))
                        if i == 1:
                            fill(ins, (name, "meta"))

            def sbv_(t):
                token_rows("sbv", t, t == 0)

            def gv_(t):
                token_rows("gv", t, t == 0)

            def gr(t):
                token_rows("gr", t, False)

            def key_blocks(t):
                out = [(slice(0, META), 0, META)]
                return out + [(tile_cols[k], 1 + k, P) for k in range(t + 1)]

            def stick_scores(t, hg):
                if hg == 0:
                    drained(pe, ("sbq", t))
                    drained(pe, ("sbk", t, 1))
                e = HEAD * hg
                for k, (cols, _, n) in enumerate(key_blocks(t)):
                    b = open_bank(("stick_z", t, hg, k))
                    for i in range(4):
                        ins = nc.tensor.matmul(b[0:n, i * P:(i + 1) * P], sbk[e:e + HEAD, i, cols],
                                               sbq[e:e + HEAD, i, :], start=True, stop=True)
                    fill(ins, ("stick_z", t, hg, k))

            def stick_sums(t, hg):
                kbs = key_blocks(t)
                for k, (cols, _, n) in reversed(list(enumerate(kbs))):
                    b = open_bank(("stick_w", t, hg, k))
                    if k == len(kbs) - 1:
                        nc.tensor.matmul(b[0:n, :], ident, cst("causal_neg").unsqueeze(1).to_broadcast([P, 4, P]), start=True, stop=False)
                    pe.wait_ge(sem("stick_log"), STICK_BASE[t] + hg * len(kbs) + len(kbs) - k)
                    for later in range(k + 1, len(kbs)):
                        nc.tensor.matmul(b[0:n, :], cst("ones")[:, 0:n], sb_log[:, later, :], start=(later == k + 1), stop=False)
                    for i in range(4):
                        e = HEAD * hg
                        nc.tensor.matmul(b[0:n, i * P:(i + 1) * P], sbk[e:e + HEAD, i, cols],
                                         sbq[e:e + HEAD, i, :], start=False, stop=False)
                    ins = nc.tensor.matmul(b[0:n, :], cst("later", n)[:, 0:n], sb_log[0:n, k, :], start=False, stop=True)
                    fill(ins, ("stick_w", t, hg, k))

            def stick_out(t, hg):
                kbs = key_blocks(t)
                out_bank = open_bank(("stick_o", t)) if hg == 0 else bank[OUT_BANK]
                drained(pe, ("sbv", t))
                if t == 0:
                    drained(pe, ("sbv", "meta"))
                for k in range(len(kbs)):
                    drained(pe, ("stick_w", t, hg, k))
                for i in range(4):
                    h = 2 * i + hg
                    for k, (_, vi, n) in enumerate(kbs):
                        ins = nc.tensor.matmul(out_bank[:, h * HEAD:(h + 1) * HEAD], sb_a[0:n, k, i * P:(i + 1) * P],
                                               sbv[0:n, vi, h * HEAD:(h + 1) * HEAD],
                                               start=(k == 0), stop=(k == len(kbs) - 1))
                if hg == 0:
                    ins.then_inc(sem("stick_half"), 1)
                else:
                    fill(ins, ("stick_o", t))

            def gla_start(t):
                if t == 0:
                    drained(pe, ("gv", "meta"))
                    pe.wait_ge(sem("log_decay_meta"), 1)
                    b = open_bank("decay_meta")
                    for dt in range(2):
                        ins = nc.tensor.matmul(b[:, dt * META:(dt + 1) * META], lg_m[0:META, dt * P:(dt + 1) * P],
                                               cst("decay_meta", META), start=True, stop=True)
                    fill(ins, "decay_meta")
                    pe.wait_ge(sem("key_meta"), 1)
                    b = open_bank("klast_meta")
                    for dt in range(2):
                        ins = nc.tensor.transpose(b[0:META, dt * P:(dt + 1) * P], klm[:, dt, :], ident)
                    fill(ins, "klast_meta")
                    drained(pe, "klast_meta")
                    b = open_bank("state_meta")
                    for h in range(GLA_HEADS):
                        ins = nc.tensor.matmul(b[:, h * P:(h + 1) * P], klast[0:META, h // 2, :], gvm[0:META, h * P:(h + 1) * P],
                                               start=True, stop=True)
                    fill(ins, "state_meta")

            def gla_decay(t, dt):
                if dt == 0:
                    pe.wait_ge(sem("log_decay"), t + 1)
                    drained(pe, ("gk", t))
                for i in range(3):
                    b = open_bank(("decay", t, dt, i))
                    n = min(512, (LEVELS + 2) * P - 512 * i)
                    ins = nc.tensor.matmul(b[:, 0:n], lg[:, dt * P:(dt + 1) * P], decay[:, 512 * i:512 * i + n],
                                           start=True, stop=True)
                    fill(ins, ("decay", t, dt, i))

            def gla_heads(t, dt):
                out_bank = bank[OUT_BANK]
                if dt == 0:
                    open_bank(("gla_o", t))
                    drained(pe, ("gv", t))
                    drained(pe, "state0" if t else "state_meta")
                pe.wait_ge(sem("gla_qk"), 2 * t + dt + 1)
                if t == 0:
                    b = open_bank(("klast", t, dt))
                    fill(nc.tensor.transpose(b[:, 0:P], gla_k[:, LEVELS, :], ident), ("klast", t, dt))
                for h in (2 * dt, 2 * dt + 1):
                    e = HEAD * (h % 2)
                    for half in range(2):
                        b = open_bank(("gla_a", t, h, half))
                        for i in range(4):
                            level = 4 * half + i
                            ins = nc.tensor.matmul(b[:, i * P:(i + 1) * P], gla_k[e:e + HEAD, level, :],
                                                   gla_q[e:e + HEAD, level, :], start=True, stop=True)
                        fill(ins, ("gla_a", t, h, half))
                for h in (2 * dt, 2 * dt + 1):
                    e = HEAD * (h % 2)
                    o = out_bank[:, h * P:(h + 1) * P]
                    pe.wait_ge(sem("gla_weights"), GLA_HEADS * t + h + 1)
                    nc.tensor.matmul(o, gla_w[:, h % 2, :], gv[:, h * P:(h + 1) * P], start=True, stop=False)
                    if h % 2:
                        pe.wait_ge(sem("gla_first_head"), 2 * t + dt + 1)
                    ins = nc.tensor.matmul(o, gla_q[e:e + HEAD, INTER, :], state[e:e + HEAD, dt, :], start=False, stop=True)
                    if h % 2 == 0:
                        ins.then_inc(sem("gla_first_head"), 1)
                if dt:
                    fill(ins, ("gla_o", t))
                else:
                    ins.then_inc(sem("gla_half"), 1)

            def gla_end(t):
                if t == 0:
                    drained(pe, ("klast", t, 1))
                    b = open_bank("state0")
                    for h in range(GLA_HEADS):
                        ins = nc.tensor.matmul(b[:, h * P:(h + 1) * P], klast[:, h // 2, :], gv[:, h * P:(h + 1) * P],
                                               start=True, stop=True)
                    fill(ins, "state0")

            def mixed_cols(t):
                pe.wait_ge(sem("mixed"), 2 * t + 2)
                turn_rows(("mixedT", t), hn[:, t, :], P)
                drained(pe, (("mixedT", t), 1))

            def out2(t, half):
                name = ("out2", half, t)
                b = open_bank(name)
                for u in range(2):
                    ins = to_rows(b, 256 * u, unit(), tile_cols[t], first=True)
                fill(ins, name)

            def query2(t, i):
                b = open_bank(("query2", t, i))
                for k in range(2):
                    ins = to_cols(b, unit(), tile_cols[t], at=2 * P * k)
                fill(ins, ("query2", t, i))

            STEPS = {"query1": query1, "pick_keys": pick_keys, "norm_cols": norm_cols, "ple_gate": ple_gate_, "ple_up": ple_up,
                     "sbk": sbk_, "sbq": sbq_, "low_rank": low_rank, "gla_keys": gla_keys, "gate_up": gate_up,
                     "sbv": sbv_, "gv": gv_, "gr": gr, "stick_scores": stick_scores, "stick_sums": stick_sums,
                     "stick_out": stick_out, "gla_start": gla_start, "gla_decay": gla_decay, "gla_heads": gla_heads,
                     "gla_end": gla_end, "mixed_cols": mixed_cols, "out2": out2, "query2": query2}

            def background(steps):
                for name, *where in steps:
                    if name in STEPS:
                        STEPS[name](*where)

            for phase in range(PHASES):
                pe.wait_ge(sem("x_ready"), PHASE_OPEN[phase])
                if phase == 0:
                    pe.wait_ge(sem("attn_ready"), 2)
                for half in range(2):
                    nc.tensor.matmul(acc[:, half, :], zeros, decay[:, 0:512], start=True, stop=False)
                for steps, lo, hi in segments(phase):
                    background(steps)
                    with pe.Fori(phase * ITERS + lo, phase * ITERS + hi) as it:
                        for n, s in enumerate(PE_SLOTS):
                            pe.wait_ge(sem("diag_ready"), it * len(PE_SLOTS) + n + 1)
                            for half in range(2):
                                ins = nc.tensor.matmul(acc[:, half, :], diag[:, s, :],
                                                       ring[:, s, D + half * 512:D + (half + 1) * 512],
                                                       start=False, stop=False)
                            ins.then_inc(sem("slot_free"), 1)
                for half in range(2):
                    ins = nc.tensor.matmul(acc[:, half, :], zeros, decay[:, 0:512], start=False, stop=True)
                ins.then_inc(sem("peer_sum"), 1)

        @block.gpsimd
        def _(pool):
            nc.gpsimd.memset(fence[:, :], 0.0).then_inc(sem("fence_set"), 1)
            pool.wait_ge(sem("fence_set"), 1)

            for k in range(N_SPLIT):
                if k < TILES:
                    rows, high, low = rows_parts(k)
                    pool.wait_ge(sem("rows_high"), k + 1)
                    mine = slice(DC // 2, DC)
                    nc.gpsimd.tensor_tensor(low[:, mine], rows[:, mine], high[:, mine].bitcast(F32), ALU.subtract).then_inc(sem("rows_low_pool"), 1)
                w, high, low = weights_half(pool, k)
                if k < ACT_SPLIT:
                    pool.wait_ge(sem("high_ready"), k + 1)
                else:
                    pool.wait_ge(sem("high_ready_act"), k + 1 - ACT_SPLIT)
                mine = slice(LOW_DVE if k < ACT_SPLIT else 0, HALF)
                nc.gpsimd.tensor_tensor(low[:, mine], w[:, mine], high[:, mine].bitcast(F32), ALU.subtract).then_inc(sem("low_ready_pool"), 1)

            pool.wait_ge(sem("const_in"), 16)
            pool.wait_ge(sem("bias_in"), 16)
            bias = na_bias.rearrange("p h (j k) -> p (h j) k", k=GRID_W)
            cols = cst("na_cols").unsqueeze(1).to_broadcast([P, NA_HEADS * 6, GRID_W])
            nc.gpsimd.tensor_tensor(bias, bias, cols, ALU.add).then_inc(sem("bias_ready"), 1)

            def gather(table, tile, it, i, s):
                nc.gpsimd.tensor_copy(slot_idx[:, s:s + 1], eidx[:, tile, bass.ds(i * RING + s, 1)]).then_inc(sem("idx_copied"), 1)
                pool.wait_ge(sem("idx_copied"), it * RING + s + 1)
                nc.gpsimd.tensor_tensor(fence[:, :], fence[:, :], fence[:, :], ALU.add)
                nc.gpsimd.indirect_dma_start(
                    out=ring[:, s, :], out_offset=None, in_=table,
                    in_offset=bass.IndirectOffsetOnAxis(ap=slot_idx[:, s:s + 1], axis=0)).then_inc(sem(f"row_in{s}"), 16)

            for phase in range(PHASES):
                tile = PHASE_TILE[phase]
                table = a["experts1"] if phase < 2 else a["experts2"]
                for g in range(PICKS):
                    pool.wait_ge(sem("experts_picked"), phase * PICKS + g + 1)
                    first = g * PICK_ITERS
                    if phase == 0 and g == 0:
                        pool.wait_ge(sem("merged"), 2)
                        for s in range(RING):
                            gather(table, tile, 0, 0, s)
                        first = 1
                    with pool.Fori(first, (g + 1) * PICK_ITERS) as i:
                        for s in range(RING):
                            users, signal = (DVE_SLOTS, "slot_free_dve") if s in DVE_SLOTS else (PE_SLOTS, "slot_free")
                            pool.wait_ge(sem(signal), (i + (phase * ITERS - 1)) * len(users) + users.index(s) + 1)
                            gather(table, tile, i + phase * ITERS, i, s)

        @block.sync
        def _(sp):
            def load(n, s, at):
                sp.dma_start(wring[:, s, :], a["weights"][at]).then_inc(sem(f"weights_in{s}"), 16)

            for t in range(TILES):
                sp.dma_start(X[:, t, :], a["x"][t * P:(t + 1) * P, :]).then_inc(sem(f"x_in{t}"), 16)
            for s in range(WSLOTS):
                load(s, s, s)
            turns = N_UNITS // WSLOTS
            with sp.Fori(1, turns) as i:
                for s in range(WSLOTS):
                    sp.wait_ge(sem("unit_begun"), i * WSLOTS + s - WSLOTS + 2)
                    load(None, s, i * WSLOTS + s)
            for n in range(turns * WSLOTS, (turns + 1) * WSLOTS):
                sp.wait_ge(sem("unit_begun"), n - WSLOTS + 2)
                load(n, n % WSLOTS, n if n < N_UNITS else n - N_TILE)
            with sp.Fori(turns + 1, N_LOADS // WSLOTS) as i:
                for s in range(WSLOTS):
                    sp.wait_ge(sem("unit_begun"), i * WSLOTS + s - WSLOTS + 2)
                    load(None, s, i * WSLOTS + s - N_TILE)
            for t in range(TILES):
                sp.wait_ge(sem("rows_normed"), norm_no[f"f{t}"] + 1)
                sp.dma_start(out[t * P:(t + 1) * P, :], hn[:, t, :]).then_inc(sem("out_written"), 16)
            sp.wait_ge(sem("out_written"), 32)

        @block.scalar
        def _(act):
            own = [0]

            def mark(ins):
                ins.then_inc(sem("act_step"), 1)
                own[0] += 1
                return own[0]

            def after(n):
                act.wait_ge(sem("act_step"), n)

            def step(ins):
                after(mark(ins))

            def drain(ins, name):
                s, _ = drain_sem(name)
                ins.then_inc(s, 1)

            act.dma_start(const[:, 0:P], a["const"][:, 0:P]).then_inc(sem("ident_in"), 16)
            act.dma_start(gain_col[:, :, :], a["gain_col"]).then_inc(sem("gain_col_in"), 16)
            def inv_rms(v, width, last=None):
                step(nc.scalar.activation(v, v, ACT.Ln, scale=1.0 / width, bias=EPS))
                ins = nc.scalar.activation(v, v, ACT.Exp, scale=-0.5)
                if last:
                    ins.then_inc(sem(last), 1)
                else:
                    step(ins)

            def norm(name):
                _, x, rows, cols, n = norm_place(name)
                k = norm_no[name]
                if name in X_STATE:
                    act.wait_ge(sem("x_ready"), X_STATE[name])
                else:
                    act.wait_ge(sem("meta_in"), 16)
                v = stat[0:n, k:k + 1]
                step(nc.scalar.activation(rows, x, ACT.Square, accum_out=v))
                inv_rms(v, D, "inv_rms")

            def norm_cols(name):
                if name[:-1] in ("ffn", "n2"):
                    turned(name, norm_place(name)[3])

            def turned(name, cols, chunks=DC):
                for half in range(-(-chunks // 4)):
                    b = filled(act, (name, half))
                    n = min(4, chunks - 4 * half)
                    drain(nc.scalar.copy(hT[:, 4 * half:4 * half + n, cols],
                                         b[:, 0:n * P].rearrange("p (c t) -> p c t", c=n)), (name, half))

            tile_cols = [slice(META + t * P, META + (t + 1) * P) for t in range(TILES)]
            for t in range(TILES):
                act.wait_ge(sem(f"x_in{t}"), 16)
                step(nc.scalar.activation(hn[:, t, :], X[:, t, :], ACT.Square, accum_out=mix_inv[:, t:t + 1]))
            step(nc.scalar.activation(mix_inv, mix_inv, ACT.Ln, scale=1.0 / D, bias=EPS))
            step(nc.scalar.activation(mix_inv, mix_inv, ACT.Exp, scale=-0.5))
            for blk in range(5):
                for t in range(TILES):
                    b = filled(act, ("in", blk, t))
                    if blk or t:
                        act.wait_ge(sem("squares_summed"), 2 * blk + t)
                    step(nc.scalar.activation(sq, b[:, :], ACT.Square, scale=mix_inv[:, t:t + 1]))
                    drain(nc.scalar.activation(raw[:, t, blk * 512:(blk + 1) * 512], b[:, :], ACT.Copy,
                                               scale=mix_inv[:, t:t + 1]), ("in", blk, t))
                if blk == 0:
                    act.dma_start(const[:, P:], a["const"][:, P:]).then_inc(sem("const_in"), 16)
                    act.dma_start(qk_gain, a["qk_gain"].partition_broadcast(P)).then_inc(sem("qk_gain_in"), 16)
                elif blk == 1:
                    act.dma_start(na_bias, a["na_bias"]).then_inc(sem("bias_in"), 16)
                elif blk == 2:
                    act.dma_start(dil_mask, a["dil_mask"]).then_inc(sem("masks_in"), 16)
            act.wait_ge(sem("squares_summed"), 10)
            inv_rms(hstat[:, :, :], HEAD, "qk_inv_rms")
            small = [(gain[:, :, :], a["gain"][0:1].partition_broadcast(P)),
                     (head_gain[:, :, :], a["head_gain"].partition_broadcast(P)),
                     (keys1[:, :, :], a["keys1"]), (keys2[:, :, :], a["keys2"]), (pT[:, :, :], a["pT"]),
                     (w_lr[:, :, :], a["w_lr"]), (w_gu[0:RANK + 1, :], a["w_gu"])]
            for dst, src in small:
                act.dma_start(dst, src).then_inc(sem("small_in"), 16)
            assert SMALL_IN == 16 * len(small)
            for blk in range(5, 8):
                for k in range(ACT_SPLIT + 2 * (blk - 5), min(ACT_SPLIT + 2 * (blk - 4), N_SPLIT)):
                    w, high, _ = weights_half(act, k)
                    nc.scalar.copy(high, w).then_inc(sem("high_ready_act"), 1)
                n = 512 if blk < 7 else 256
                for t in range(TILES):
                    b = filled(act, ("in", blk, t))
                    drain(nc.scalar.activation(val[:, t, (blk - 5) * 512:(blk - 5) * 512 + n], b[:, 0:n], ACT.Copy,
                                               scale=mix_inv[:, t:t + 1]), ("in", blk, t))
            for t in range(TILES):
                for j in range(5):
                    b = filled(act, (("qkT", t), j))
                    drain(nc.scalar.copy(qkT[:, 4 * j:4 * j + 4, t * P:(t + 1) * P],
                                         b[:, :].rearrange("p (c t) -> p c t", c=4)), (("qkT", t), j))

            def probs(n):
                t, u = divmod(n, ATT_UNITS)
                act.wait_ge(sem("score_max"), n + 1)
                p = prob[n % 2]
                if u < 4:
                    for i in range(2):
                        v = p[:, i * SEQ:(i + 1) * SEQ]
                        ins = nc.scalar.activation(v, v, ACT.Exp, bias=amax[:, 2 * (n % 2) + i:2 * (n % 2) + i + 1],
                                                   accum_out=asum[:, t, na_head(u, i):na_head(u, i) + 1])
                else:
                    ins = nc.scalar.activation(p, p, ACT.Exp, bias=amax[:, 2 * (n % 2):2 * (n % 2) + 1],
                                               accum_out=asum[:, t, 4 + u:5 + u])
                ins.then_inc(sem("prob_ready"), 1)

            probs(0)
            for n in range(TILES * ATT_UNITS):
                t, u = divmod(n, ATT_UNITS)
                for half in range(1 if u < 4 else 2):
                    b = filled(act, (("probT", t, u), half))
                    if half == 0 and n >= 2:
                        act.wait_ge(sem("weighed"), n - 1)
                    w = 512 if half == 0 else 256
                    drain(nc.scalar.copy(probT[:, n % 2, 512 * half:512 * half + w], b[:, 0:w]), (("probT", t, u), half))
                if n + 1 < TILES * ATT_UNITS:
                    probs(n + 1)
                g, tile = divmod(n, TILES)
                b = filled(act, ("gate", g, tile))
                drain(nc.scalar.activation(sig[:, tile, 256 * g:256 * (g + 1)], b[:, 0:256], ACT.Sigmoid,
                                           scale=mix_inv[:, tile:tile + 1]), ("gate", g, tile))
            for t in range(TILES):
                turned(("attnT", t), tile_cols[t], 6)
            act.dma_start(meta_x[0:META, :], a["meta"]).then_inc(sem("meta_in"), 16)
            for t in range(TILES):
                turned(("mergedT", t), tile_cols[t])
            def next_gain(row, last):
                act.wait_ge(sem("rows_normed"), norm_no[last] + 1)
                act.dma_start(gain[:, :, :], a["gain"][row:row + 1].partition_broadcast(P)).then_inc(sem("next_gain_in"), 16)

            def query1(g):
                for t in range(TILES):
                    if g == 0:
                        norm_cols(f"ffn{t}")
                    if g == 0 and t == 0:
                        norm("ffn1")
                    b = filled(act, ("query1", g, t))
                    drain(nc.scalar.copy(qpT[:, 4 * g:4 * g + 4, t * P:(t + 1) * P],
                                         b[:, :].rearrange("p (c t) -> p c t", c=4)), ("query1", g, t))

            def pick(phase, g):
                act.wait_ge(sem("top_shifted"), PICKS * phase + g + 1)
                nc.scalar.activation(tk["exp"], tk["exp"], ACT.Exp).then_inc(sem("top_exp"), 1)

            norm("ffn0")
            query1(0)
            next_gain(1, "ffn1")
            pick(0, 0)

            def ple_gate_(t, half):
                b = filled(act, ("ple_gate", t, half))
                drain(nc.scalar.activation(ple_gate[:, half * 512:(half + 1) * 512], b[:, :], ACT.Sigmoid), ("ple_gate", t, half))

            def log_sigmoid(name, rows, dst, signal):
                b = filled(act, name)
                step(nc.scalar.activation(dst, b[0:rows, 0:256], ACT.Abs))
                step(nc.scalar.activation(dst, dst, ACT.Exp, scale=-1.0))
                nc.scalar.activation(dst, dst, ACT.Ln, bias=1.0).then_inc(sem(signal), 1)

            def new_cols(t):
                return (0, META + P) if t == 0 else (META + P, P)

            def sbk_(t):
                at, n = new_cols(t)
                for i in range(2):
                    b = filled(act, ("sbk", t, i))
                    drain(nc.scalar.copy(sbk[:, 2 * i:2 * i + 2, at:at + n],
                                         b[:, 0:2 * n].rearrange("p (c t) -> p c t", c=2)), ("sbk", t, i))

            def sbq_(t):
                b = filled(act, ("sbq", t))
                drain(nc.scalar.mul(sbq, b[:, :].rearrange("p (c t) -> p c t", c=4), HEAD ** -0.5), ("sbq", t))

            def low_rank(t):
                _, n = new_cols(t)
                b = filled(act, ("lr", t))
                act.wait_ge(sem("ones_set"), t + 1)
                drain(nc.scalar.copy(lrT[0:RANK, META + P - n:META + P], b[0:RANK, 0:n]), ("lr", t))

            def gla_keys(t):
                _, n = new_cols(t)
                b = filled(act, ("gk", t))
                drain(nc.scalar.copy(gkT[:, :, META + P - n:META + P], b[:, 0:2 * n].rearrange("p (c t) -> p c t", c=2)), ("gk", t))
                b = filled(act, ("gq", t))
                drain(nc.scalar.mul(gqT, b[:, 0:2 * P].rearrange("p (c t) -> p c t", c=2), GLA_DK ** -0.5), ("gq", t))

            def gate_up(t):
                log_sigmoid(("z", t), P, lg, "log_gate")
                if t == 0:
                    log_sigmoid("z_meta", META, lg_m[0:META, :], "log_gate_meta")

            def token_rows(name, t, dst, dst_meta):
                b = filled(act, (name, t))
                drain(nc.scalar.copy(dst, b[:, :]), (name, t))
                if t == 0:
                    b = filled(act, (name, "meta"))
                    drain(nc.scalar.copy(dst_meta, b[0:META, :]), (name, "meta"))

            def sbv_(t):
                token_rows("sbv", t, sbv[:, 1 + t, :], sbv[0:META, 0, :])

            def gv_(t):
                token_rows("gv", t, gv[:, :], gvm[0:META, :])

            def gr(t):
                b = filled(act, ("gr", t))
                nc.scalar.activation(silu, b[:, :], ACT.Sigmoid).then_inc(sem("gr_sigmoid"), 1)

            def stick_scores(t, hg):
                nkb = t + 2
                done = {}
                for k in reversed(range(nkb)):
                    b = filled(act, ("stick_z", t, hg, k))
                    if hg:
                        act.wait_ge(sem("stick_log"), STICK_BASE[t] + nkb - k)
                    done[k] = mark(nc.scalar.activation(stick_tmp(k), b[0:key_rows(k), :], ACT.Abs))
                for k in reversed(range(nkb)):
                    after(done[k])
                    done[k] = mark(nc.scalar.activation(stick_tmp(k), stick_tmp(k), ACT.Exp, scale=-1.0))
                for k in reversed(range(nkb)):
                    after(done[k])
                    nc.scalar.activation(stick_tmp(k), stick_tmp(k), ACT.Ln, bias=1.0).then_inc(sem("stick_soft"), 1)

            def stick_sums(t, hg):
                if hg:
                    act.wait_ge(sem("stick_half"), t + 1)
                for k in reversed(range(t + 2)):
                    n = META if k == 0 else P
                    b = filled(act, ("stick_w", t, hg, k))
                    drain(nc.scalar.activation(sb_a[0:n, k, :], b[0:n, :], ACT.Exp), ("stick_w", t, hg, k))

            def gla_start(t):
                if t == 0:
                    b = filled(act, "decay_meta")
                    drain(nc.scalar.activation(klm, b[:, 0:2 * META].rearrange("p (c t) -> p c t", c=2), ACT.Exp), "decay_meta")
                    b = filled(act, "klast_meta")
                    drain(nc.scalar.copy(klast[0:META, :, :], b[0:META, 0:2 * P].rearrange("p (c t) -> p c t", c=2)), "klast_meta")

            def gla_decay(t, dt):
                if dt:
                    act.wait_ge(sem("gla_qk"), 2 * t + 1)
                for i in range(3):
                    n = min(512, (LEVELS + 2) * P - 512 * i)
                    b = filled(act, ("decay", t, dt, i))
                    drain(nc.scalar.activation(expd[:, 512 * i:512 * i + n], b[:, 0:n], ACT.Exp), ("decay", t, dt, i))

            def gla_heads(t, dt):
                if t == 0:
                    b = filled(act, ("klast", t, dt))
                    if dt == 0:
                        filled(act, "state_meta")
                    drain(nc.scalar.copy(klast[:, dt, :], b[:, 0:P]), ("klast", t, dt))

            def head_norms(t):
                act.wait_ge(sem("mix_squares"), t + 1)
                v = [hstat[:, 0, 0:SB_HEADS], hstat[:, 1, 0:GLA_HEADS]]
                n = [mark(nc.scalar.activation(v[k], v[k], ACT.Ln, scale=1.0 / width, bias=EPS)) for k, width in enumerate((HEAD, GLA_DV))]
                for k in range(2):
                    after(n[k])
                    nc.scalar.activation(v[k], v[k], ACT.Exp, scale=-0.5).then_inc(sem("mix_inv_rms"), 1)

            def mixed_cols(t):
                turned(("mixedT", t), tile_cols[t])

            def query2(t, i):
                b = filled(act, ("query2", t, i))
                drain(nc.scalar.copy(query2T[:, 4 * i:4 * i + 4, :], b[:, :].rearrange("p (c t) -> p c t", c=4)), ("query2", t, i))

            def final(t):
                next_gain(2, "n21")
                norm(f"f{t}")

            STEPS = {"query1": query1, "pick": pick, "norm_rows": norm, "norm_cols": norm_cols, "ple_gate": ple_gate_, "sbk": sbk_,
                     "sbq": sbq_, "low_rank": low_rank, "gla_keys": gla_keys, "gate_up": gate_up, "sbv": sbv_, "gv": gv_, "gr": gr,
                     "stick_scores": stick_scores, "stick_sums": stick_sums, "gla_start": gla_start, "gla_decay": gla_decay,
                     "gla_heads": gla_heads, "mixed_rows": head_norms, "mixed_cols": mixed_cols, "query2": query2, "final": final}

            def background(steps):
                for name, *where in steps:
                    if name in STEPS:
                        STEPS[name](*where)

            for phase in range(PHASES):
                for steps, lo, hi in segments(phase):
                    background(steps)
                    with act.Fori(phase * ITERS + lo, phase * ITERS + hi) as it:
                        for s in range(RING):
                            act.wait_ge(sem("dots"), it * RING + s + 1)
                            nc.scalar.activation(act_dot[:, s:s + 1], dot[:, s:s + 1], ACT.Gelu).then_inc(sem("gelu"), 1)
            norm("f1")

        @block.vector
        def _(dve):
            own = [0]

            def mark(ins):
                ins.then_inc(sem("dve_step"), 1)
                own[0] += 1
                return own[0]

            def after(n):
                dve.wait_ge(sem("dve_step"), n)

            def step(ins):
                after(mark(ins))

            def drain(ins, name):
                s, n = drain_sem(name)
                ins.then_inc(s, 1)
                dve.wait_ge(s, n)

            def norm(name):
                _, x, rows, cols, n = norm_place(name)
                k = norm_no[name]
                dve.wait_ge(sem("inv_rms"), k + 1)
                kind = name if name == "meta" else name[:-1]
                if kind in GAIN_ROW:
                    if kind == "ffn":
                        dve.wait_ge(sem("small_in"), SMALL_IN)
                    else:
                        dve.wait_ge(sem("next_gain_in"), 16 * GAIN_ROW[kind])
                    ins = nc.vector.scalar_tensor_tensor(out=rows, in0=x, scalar=stat[0:n, k:k + 1],
                                                         in1=gain[:, 0, :], op0=ALU.mult, op1=ALU.mult)
                    ins.then_inc(sem("rows_normed"), 1)
                    return
                nc.vector.tensor_scalar(rows, x, stat[0:n, k:k + 1], None, ALU.mult).then_inc(sem("rows_normed"), 1)

            def norm_cols(name):
                _, _, _, cols, n = norm_place(name)
                kind = name if name == "meta" else name[:-1]
                if kind in GAIN_ROW:
                    return
                g = gain_col[:, GAIN_COL[kind], :]
                for half in range(2):
                    b = filled(dve, (name, half))
                    drain(nc.vector.tensor_tensor(hT[:, 4 * half:4 * half + 4, cols],
                                                  b[:, 0:4 * n].rearrange("p (c t) -> p c t", c=4),
                                                  g[:, 4 * half:4 * half + 4].unsqueeze(2).to_broadcast([P, 4, n]), ALU.mult), (name, half))

            def split(k):
                w, high, low = weights_half(dve, k)
                nc.vector.tensor_copy(high, w).then_inc(sem("high_ready"), 1)
                dve.wait_ge(sem("high_ready"), k + 1)
                mine = slice(0, LOW_DVE)
                nc.vector.tensor_tensor(low[:, mine], w[:, mine], high[:, mine].bitcast(F32), ALU.subtract) \
                    .then_inc(sem("low_ready_dve"), 1)

            dve.wait_ge(sem("gain_col_in"), 16)
            for t in range(TILES):
                norm_cols(f"mix{t}")
                rows, high, low = rows_parts(t)
                nc.vector.tensor_copy(high, rows).then_inc(sem("rows_high"), 1)
                dve.wait_ge(sem("rows_high"), t + 1)
                mine = slice(0, DC // 2)
                nc.vector.tensor_tensor(low[:, mine], rows[:, mine], high[:, mine].bitcast(F32), ALU.subtract).then_inc(sem("rows_low_dve"), 1)
                split(t)
            for k in range(2, 4):
                split(k)
            for blk in range(5):
                for k in range(4 * blk + 4, 4 * blk + 8):
                    split(k)
                    t = k - 4 * blk - 6
                    if t >= 0:
                        drained(dve, ("in", blk, t))
                        nc.vector.tensor_reduce(hstat[:, t, 8 * blk:8 * blk + 8], sq.rearrange("p (h d) -> p h d", d=HEAD),
                                                AX.X, ALU.add).then_inc(sem("squares_summed"), 1)
            for k in range(N_SPLIT - 6, ACT_SPLIT):
                split(k)
            dve.wait_ge(sem("const_in"), 16)
            dve.wait_ge(sem("qk_gain_in"), 16)
            for t in range(TILES):
                dve.wait_ge(sem("qk_inv_rms"), 1)
                r = raw[:, t, :].rearrange("p (h d) -> p h d", d=HEAD)
                step(nc.vector.tensor_tensor(r, r, hstat[:, t, :].unsqueeze(2).to_broadcast([P, QK_HEADS, HEAD]), ALU.mult))
                at = 0
                for k, heads in enumerate((NA_HEADS, NA_HEADS, DIL_HEADS, DIL_HEADS)):
                    v = r[:, at:at + heads, :]
                    step(nc.vector.tensor_tensor(v, v, qk_gain[:, k, :].unsqueeze(1).to_broadcast([P, heads, HEAD]), ALU.mult))
                    at += heads
                x1 = r[:, 2 * NA_HEADS:, 0:ROT_HALF]
                x2 = r[:, 2 * NA_HEADS:, ROT_HALF:2 * ROT_HALF]
                rope = cst("rope")[:, t * 2 * ROT_HALF:(t + 1) * 2 * ROT_HALF]
                cos, sin = [rope[:, k * ROT_HALF:(k + 1) * ROT_HALF].unsqueeze(1).to_broadcast([P, 2 * DIL_HEADS, ROT_HALF]) for k in range(2)]
                p = [rot[:, k, :].rearrange("p (h d) -> p h d", d=ROT_HALF) for k in range(4)]
                for dst, u, v in ((p[0], x1, cos), (p[1], x2, sin), (p[2], x2, cos), (p[3], x1, sin)):
                    step(nc.vector.tensor_tensor(dst, u, v, ALU.mult))
                step(nc.vector.tensor_tensor(x1, p[0], p[1], ALU.subtract))
                nc.vector.tensor_tensor(x2, p[2], p[3], ALU.add).then_inc(sem("qk_ready"), 1)
            dve.wait_ge(sem("masks_in"), 16)
            dve.wait_ge(sem("bias_ready"), 1)
            def divide(t):
                dve.wait_ge(sem("weighed"), 8 * (t + 1))
                step(nc.vector.reciprocal(arec[:, 0:12], asum[:, t, 0:12]))
                step(nc.vector.tensor_tensor(attn[t][:, 0:512].rearrange("p (h d) -> p h d", d=HEAD),
                                             na_sums[t].rearrange("p (h d) -> p h d", d=HEAD),
                                             arec[:, 0:8].unsqueeze(2).to_broadcast([P, 8, HEAD]), ALU.mult))
                ins = nc.vector.tensor_tensor(attn[t][:, 512:768].rearrange("p (h d) -> p h d", d=HEAD),
                                              dil_sums[t].rearrange("p (h d) -> p h d", d=HEAD),
                                              arec[:, 8:12].unsqueeze(2).to_broadcast([P, 4, HEAD]), ALU.mult)
                ins.then_inc(sem("attn_ready"), 1)

            for t in range(TILES):
                for u in range(8):
                    n = 8 * t + u
                    if n == ATT_UNITS + 2:
                        divide(0)
                    if n >= 2:
                        filled(dve, (("probT", (n - 2) // 8, (n - 2) % 8), 0 if (n - 2) % 8 < 4 else 1))
                    p = prob[n % 2]
                    m = amax[:, 2 * (n % 2):2 * (n % 2) + 2]
                    if u < 4:
                        b = filled(dve, ("score", t, u, 0))
                        j = 2 - 2 * t
                        pv = p[:, 0:512].rearrange("p (h k) -> p h k", h=2)
                        drain(nc.vector.scalar_tensor_tensor(out=pv, in0=b[:, :].rearrange("p (h k) -> p h k", h=2), scalar=HEAD ** -0.5,
                                                             in1=na_bias[:, na_head(u, 0):na_head(u, 1) + 1:2, j * GRID_W:(j + 4) * GRID_W],
                                                             op0=ALU.mult, op1=ALU.add), ("score", t, u, 0))
                        nc.vector.tensor_reduce(m, pv, AX.X, ALU.max, negate=True).then_inc(sem("score_max"), 1)
                    else:
                        for half in range(2):
                            w = 512 if half == 0 else 256
                            c = slice(512 * half, 512 * half + w)
                            b = filled(dve, ("score", t, u, half))
                            drain(nc.vector.scalar_tensor_tensor(out=p[:, c], in0=b[:, 0:w], scalar=HEAD ** -0.5, in1=dil_mask[:, t, c],
                                                                 op0=ALU.mult, op1=ALU.add), ("score", t, u, half))
                        nc.vector.tensor_reduce(m[:, 0:1], p, AX.X, ALU.max, negate=True).then_inc(sem("score_max"), 1)
            divide(1)
            for half in range(2):
                c = slice(512 * half, 512 * half + 512)
                for t in range(TILES):
                    b = filled(dve, ("na", half, t))
                    drain(nc.vector.tensor_tensor(hn[:, t, c], sig[:, t, c], b[:, :], ALU.mult), ("na", half, t))
            for t in range(TILES):
                for half in range(2):
                    c = slice(512 * half, 512 * half + 512)
                    b = filled(dve, ("dil", half, t))
                    g = sig[:, t, D + 512 * half:D + 512 * half + 512]
                    drain(nc.vector.tensor_tensor(g, g, b[:, :], ALU.mult), ("dil", half, t))
                    ins = nc.vector.tensor_tensor(hn[:, t, c], hn[:, t, c], g, ALU.add)
                    if half:
                        ins.then_inc(sem("merged"), 1)

            for t in range(TILES):
                for half in range(2):
                    c = slice(512 * half, 512 * half + 512)
                    b = filled(dve, ("out1", half, t))
                    drain(nc.vector.tensor_tensor(X[:, t, c], X[:, t, c], b[:, :], ALU.add), ("out1", half, t))
                nc.vector.tensor_copy(signal_tmp[:, :], X[:, t, 0:1]).then_inc(sem("x_ready"), 1)
                norm(f"ffn{t}")

            u32 = {n: v.bitcast(U32) for n, v in tk.items()}

            def top16(sources, last_read=None):
                done = [own[0]] * len(sources)
                for k, (src, gone, v, i) in enumerate(sources):
                    done[k] = mark(nc.vector.max(v[:, 0:8], src))
                for k, (src, gone, v, i) in enumerate(sources):
                    after(done[k])
                    mark(nc.vector.max_index(i[:, 0:8], v[:, 0:8], src))
                for k, (src, gone, v, i) in enumerate(sources):
                    ins = nc.vector.match_replace(gone, v[:, 0:8], src, -3.0e38)
                    if last_read and last_read[k]:
                        drain(ins, last_read[k])
                    else:
                        done[k] = mark(ins)
                for k, (src, gone, v, i) in enumerate(sources):
                    after(done[k])
                    done[k] = mark(nc.vector.max(v[:, 8:16], gone))
                for k, (src, gone, v, i) in enumerate(sources):
                    after(done[k])
                    n = mark(nc.vector.max_index(i[:, 8:16], v[:, 8:16], gone))
                after(n)

            def pick_keys(phase, g):
                sources = []
                for half, (v, ix) in enumerate((("v1", "i1"), ("v2", "i2"))):
                    b = filled(dve, ("key", phase, g, half))
                    for i in range(PAIR_HEADS):
                        sources.append((b[:, i * KEYS:(i + 1) * KEYS], keys_gone[:, 2 * half + i, :], tk[v][:, i, :], u32[ix][:, i, :]))
                top16(sources, [None, ("key", phase, g, 0), None, ("key", phase, g, 1)])

            def pick(phase, g):
                t = PHASE_TILE[phase]
                here = slice(PAIR_HEADS * g * TOPK, PAIR_HEADS * (g + 1) * TOPK)
                pairs_of = lambda v: v.rearrange("p (h k) -> p h k", h=PAIR_HEADS)
                flat_of = lambda v: v.rearrange("p h k -> p (h k)")
                for h in range(PAIR_HEADS):
                    n = mark(nc.vector.tensor_tensor(cand[:, h, :].rearrange("p (a b) -> p a b", a=TOPK),
                                                     tk["v1"][:, h, :].unsqueeze(2).to_broadcast([P, TOPK, TOPK]),
                                                     tk["v2"][:, h, :].unsqueeze(1).to_broadcast([P, TOPK, TOPK]), ALU.add))
                after(n)
                top16([(cand[:, h, :], cand_gone[:, h, :], tk["sc"][:, h, :], u32["pos"][:, h, :]) for h in range(PAIR_HEADS)])
                nc.vector.tensor_tensor(tk["exp"], tk["sc"], tk["sc"][:, :, 0:1].to_broadcast([P, PAIR_HEADS, TOPK]), ALU.subtract) \
                    .then_inc(sem("top_shifted"), 1)
                mark(nc.vector.tensor_single_scalar(u32["pa"], u32["pos"], 4, ALU.logical_shift_right))
                mark(nc.vector.tensor_single_scalar(u32["pb"], u32["pos"], TOPK - 1, ALU.bitwise_and))
                mark(nc.vector.tensor_copy(tk["i1f"], u32["i1"]))
                after(mark(nc.vector.tensor_copy(tk["i2f"], u32["i2"])))
                o = [onehot[:, k, :].rearrange("p (h k a) -> p h k a", h=PAIR_HEADS, k=TOPK) for k in range(2)]
                o3 = [onehot[:, k, :].rearrange("p (h a) -> p h a", a=TOPK) for k in range(2)]
                chosen = (("pa", "i1f", "ia"), ("pb", "i2f", "ib"))
                wide = [P, PAIR_HEADS * TOPK, TOPK]
                n = [mark(nc.vector.tensor_tensor(o3[k], flat_of(u32[place_]).unsqueeze(2).to_broadcast(wide),
                                                  cst("iota").unsqueeze(1).to_broadcast(wide), ALU.is_equal))
                     for k, (place_, _, _) in enumerate(chosen)]
                for k, (_, keys, _) in enumerate(chosen):
                    after(n[k])
                    n[k] = mark(nc.vector.tensor_tensor(o[k], o[k], tk[keys].unsqueeze(2).to_broadcast([P, PAIR_HEADS, TOPK, TOPK]), ALU.mult))
                for k, (_, _, dst) in enumerate(chosen):
                    after(n[k])
                    n[k] = mark(nc.vector.tensor_reduce(flat_of(tk[dst]), o3[k], AX.X, ALU.add))
                after(n[1])
                if phase >= 2:
                    dve.wait_ge(sem("peer_sum"), phase - 1)
                n = mark(nc.vector.scalar_tensor_tensor(out=pairs_of(eidx[:, t, here]), in0=tk["ia"], scalar=float(KEYS), in1=tk["ib"],
                                                        op0=ALU.mult, op1=ALU.add))
                dve.wait_ge(sem("top_exp"), PICKS * phase + g + 1)
                step(nc.vector.tensor_reduce(top_sum, tk["exp"], AX.X, ALU.add))
                step(nc.vector.reciprocal(top_sum, top_sum))
                nc.vector.tensor_tensor(pairs_of(gates[:, t, here]), tk["exp"],
                                        top_sum.unsqueeze(2).to_broadcast([P, PAIR_HEADS, TOPK]), ALU.mult).then_inc(sem("experts_picked"), 1)
                dve.wait_ge(sem("experts_picked"), PICKS * phase + g + 1)

            pick_keys(0, 0)
            pick(0, 0)

            def ple_up(t):
                for half in range(2):
                    c = slice(512 * half, 512 * half + 512)
                    drained(dve, ("ple_gate", t, half))
                    b = filled(dve, ("ple", t, half))
                    drain(nc.vector.tensor_tensor(ple_gate[:, c], ple_gate[:, c], b[:, :], ALU.mult), ("ple", t, half))
                nc.vector.tensor_tensor(X[:, t, :], X[:, t, :], ple_gate, ALU.add).then_inc(sem("x_ready"), 1)

            def log_sigmoid(name, rows, dst, signal):
                b, _ = job[name]
                z = bank[b]
                drain(nc.vector.scalar_tensor_tensor(out=dst, in0=z[0:rows, 0:256], scalar=0.0, in1=dst, op0=ALU.min, op1=ALU.subtract), name)
                nc.vector.tensor_scalar(dst, dst, 1.0 / GLA_TAU, None, ALU.mult).then_inc(sem(signal), 1)

            def low_rank(t):
                dve.wait_ge(sem("x_ready"), X_STATE[f"n1{t}"])
                nc.vector.memset(lrT[0:32, :], 1.0).then_inc(sem("ones_set"), 1)

            def gate_up(t):
                dve.wait_ge(sem("log_gate"), t + 1)
                log_sigmoid(("z", t), P, lg, "log_decay")
                if t == 0:
                    dve.wait_ge(sem("log_gate_meta"), 1)
                    log_sigmoid("z_meta", META, lg_m[0:META, :], "log_decay_meta")

            def gr(t):
                dve.wait_ge(sem("gr_sigmoid"), t + 1)
                b, _ = job[("gr", t)]
                drain(nc.vector.tensor_tensor(silu, silu, bank[b][:, :], ALU.mult), ("gr", t))
                step(nc.vector.tensor_tensor(silu, silu, head_gain[:, 1, :], ALU.mult))

            def stick_log(t, hg):
                nkb = t + 2
                for k in reversed(range(nkb)):
                    n = META if k == 0 else P
                    b = bank[job[("stick_z", t, hg, k)][0]]
                    tmp = stick_tmp(k)
                    dve.wait_ge(sem("stick_soft"), STICK_BASE[t] + hg * nkb + nkb - k)
                    if hg:
                        filled(dve, ("stick_w", t, 0, 0))
                    lv = sb_log[0:n, k, :]
                    drain(nc.vector.scalar_tensor_tensor(out=lv, in0=b[0:n, :], scalar=0.0, in1=tmp, op0=ALU.max, op1=ALU.add), ("stick_z", t, hg, k))
                    if k == nkb - 1:
                        lq = lv.rearrange("p (h q) -> p h q", h=4)
                        ins = nc.vector.scalar_tensor_tensor(out=lq, in0=lq, scalar=-1.0, in1=cst("causal").unsqueeze(1).to_broadcast([P, 4, P]),
                                                             op0=ALU.mult, op1=ALU.mult)
                    else:
                        ins = nc.vector.tensor_scalar(lv, lv, -1.0, None, ALU.mult)
                    ins.then_inc(sem("stick_log"), 1)

            def stick_out(t, hg):
                if hg:
                    attention_sums("stick_o", t, 0)

            def attention_sums(name, t, half):
                b = filled(dve, (name, t))
                o = hn[:, t, 512 * half:512 * half + 512]
                heads = GLA_HEADS if half else SB_HEADS
                drain(nc.vector.tensor_copy(o, b[:, :]), (name, t))
                step(nc.vector.tensor_tensor(squares, o, o, ALU.mult))
                ins = nc.vector.tensor_reduce(hstat[:, half, 0:heads], squares.rearrange("p (h d) -> p h d", h=heads), AX.X, ALU.add)
                if half:
                    ins.then_inc(sem("mix_squares"), 1)
                else:
                    step(ins)

            def gla_start(t):
                if t == 0:
                    drained(dve, "decay_meta")
                    nc.vector.tensor_tensor(klm, klm, gkT[:, :, 0:META], ALU.mult).then_inc(sem("key_meta"), 1)
                    b = filled(dve, "state_meta")
                    for h in range(GLA_HEADS):
                        e = HEAD * (h % 2)
                        ins = nc.vector.tensor_copy(state[e:e + HEAD, h // 2, :], b[e:e + HEAD, h * P:(h + 1) * P])
                        if h < GLA_HEADS - 1:
                            step(ins)
                        else:
                            drain(ins, "state_meta")

            def gla_qk(t, dt):
                for i in range(3):
                    drained(dve, ("decay", t, dt, i))
                ev = expd.rearrange("p (l t) -> p l t", t=P)
                if dt:
                    dve.wait_ge(sem("gla_half"), t + 1)
                mark(nc.vector.tensor_tensor(gla_q, ev[:, 0:LEVELS + 1, :], gqT[:, dt, :].unsqueeze(1).to_broadcast([P, LEVELS + 1, P]), ALU.mult))
                if t == 0:
                    mark(nc.vector.tensor_copy(arec[:, dt:dt + 1], ev[:, INTER, P - 1:P]))
                kk = gkT[:, dt, META:META + P]
                mark(nc.vector.tensor_tensor(gla_k[:, LEVELS, :], ev[:, LAST, :], kk, ALU.mult))
                nc.vector.tensor_tensor(gla_k[:, 0:LEVELS, :], ev[:, 0:LEVELS, :], kk.unsqueeze(1).to_broadcast([P, LEVELS, P]), ALU.mult) \
                    .then_inc(sem("gla_qk"), 1)

            def gla_heads(t, dt):
                for h in (2 * dt, 2 * dt + 1):
                    if h:
                        dve.wait_ge(sem("gla_weights"), GLA_HEADS * t + h)
                    for half in range(2):
                        b = filled(dve, ("gla_a", t, h, half))
                        ls = slice(4 * half, 4 * half + 4)
                        drain(nc.vector.tensor_tensor(gla_a[:, ls, :], b[:, :].rearrange("p (l t) -> p l t", l=4), pairs[:, ls, :], ALU.mult),
                              ("gla_a", t, h, half))
                    nc.vector.tensor_reduce(gla_w[:, h % 2, :], gla_a.rearrange("p l t -> p t l"), AX.X, ALU.add) \
                        .then_inc(sem("gla_weights"), 1)

            def gla_end(t):
                attention_sums("gla_o", t, 1)
                if t == 0:
                    b = filled(dve, "state0")
                    for h in range(GLA_HEADS):
                        e = HEAD * (h % 2)
                        ins = nc.vector.scalar_tensor_tensor(out=state[e:e + HEAD, h // 2, :], in0=state[e:e + HEAD, h // 2, :],
                                                             scalar=arec[e:e + HEAD, h // 2:h // 2 + 1], in1=b[e:e + HEAD, h * P:(h + 1) * P],
                                                             op0=ALU.mult, op1=ALU.add)
                        if h < GLA_HEADS - 1:
                            step(ins)
                        else:
                            drain(ins, "state0")

            def mixed_rows(t):
                for k, (heads, w, factor) in enumerate(((SB_HEADS, HEAD, head_gain[:, 0, :]), (GLA_HEADS, GLA_DV, silu))):
                    o = hn[:, t, 512 * k:512 * k + 512]
                    ov = o.rearrange("p (h d) -> p h d", h=heads)
                    dve.wait_ge(sem("mix_inv_rms"), 2 * t + k + 1)
                    step(nc.vector.tensor_tensor(ov, ov, hstat[:, k, 0:heads].unsqueeze(2).to_broadcast([P, heads, w]), ALU.mult))
                    nc.vector.tensor_tensor(o, o, factor, ALU.mult).then_inc(sem("mixed"), 1)

            def out2(t, half):
                c = slice(512 * half, 512 * half + 512)
                name = ("out2", half, t)
                b = filled(dve, name)
                drain(nc.vector.tensor_tensor(X[:, t, c], X[:, t, c], b[:, :], ALU.add), name)
                if half:
                    nc.vector.tensor_copy(signal_tmp[:, :], X[:, t, 0:1]).then_inc(sem("x_ready"), 1)

            def final(t):
                norm(f"f{t}")

            STEPS = {"pick_keys": pick_keys, "pick": pick, "norm_rows": norm, "norm_cols": norm_cols, "ple_up": ple_up,
                     "low_rank": low_rank, "gate_up": gate_up, "gr": gr, "stick_log": stick_log, "stick_out": stick_out,
                     "gla_start": gla_start, "gla_qk": gla_qk, "gla_heads": gla_heads, "gla_end": gla_end,
                     "mixed_rows": mixed_rows, "out2": out2, "final": final}

            def background(steps):
                for name, *where in steps:
                    if name in STEPS:
                        STEPS[name](*where)

            for phase in range(PHASES):
                t = PHASE_TILE[phase]
                for steps, lo, hi in segments(phase):
                    background(steps)
                    with dve.Fori(lo, hi) as i:
                        it = i + phase * ITERS
                        def finish(s):
                            dve.wait_ge(sem("gelu"), it * RING + s + 1)
                            gate = gates[:, t, bass.ds(i * RING + s, 1)]
                            if s in PE_SLOTS:
                                nc.vector.tensor_scalar(diag[:, s, :], ident, act_dot[:, s:s + 1], gate,
                                                        ALU.mult, ALU.mult).then_inc(sem("diag_ready"), 1)
                            else:
                                n = DVE_SLOTS.index(s)
                                nc.vector.tensor_tensor(weight[:, n:n + 1], act_dot[:, s:s + 1], gate, ALU.mult).then_inc(sem("weight_ready"), 1)
                                dve.wait_ge(sem("weight_ready"), it * len(DVE_SLOTS) + n + 1)
                                nc.vector.scalar_tensor_tensor(out=X[:, t, :], in0=ring[:, s, D:], scalar=weight[:, n:n + 1], in1=X[:, t, :],
                                                               op0=ALU.mult, op1=ALU.add).then_inc(sem("slot_free_dve"), 1)

                        for s in range(RING):
                            dve.wait_ge(sem(f"row_in{s}"), (it + 1) * 16)
                            u = ring[:, s, 0:D]
                            nc.vector.tensor_tensor_reduce(out=u, in0=u, in1=hn[:, t, :], scale=1.0, scalar=0.0, op0=ALU.mult, op1=ALU.add,
                                                           accum_out=dot[:, s:s + 1]).then_inc(sem("dots"), 1)
                            if s:
                                finish(s - 1)
                        finish(RING - 1)
                dve.wait_ge(sem("peer_sum"), phase + 1)
                dve.wait_ge(sem("slot_free_dve"), (phase + 1) * ITERS * len(DVE_SLOTS))
                rows = X[:, t, :].rearrange("p (h d) -> p h d", h=2)
                nc.vector.tensor_tensor(rows, rows, acc[:, :, :], ALU.add).then_inc(sem("x_ready"), 1)
            norm("f1")


SMALL_IN = 16 * 7
STICK_BASE = [0, 4]


def units_of(w, width=256):
    n = w.shape[1]
    return [np.ascontiguousarray(w[:, c:c + width].reshape(w.shape[0] // P, P, width).transpose(1, 0, 2)).reshape(P, -1)
            for c in range(0, n, width)]


def layout(i):
    const, dil = constants()
    w_in = i["w_in"][0]
    w_in = np.concatenate([w_in[:, 0:1024], w_in[:, 1536:3072], w_in[:, 1024:1536], w_in[:, 3072:5888]], 1)
    units = units_of(w_in)
    units += units_of(i["w_branch_na"][0], 512) + units_of(i["w_branch_dil"][0], 1024)
    units += units_of(i["w_out"][0]) + units_of(i["peer_w_query"][0])
    units += units_of(i["w_ple_gate"][0]) + units_of(i["w_ple"][0], 1024)
    w2 = i["w_in_2"][0]
    for lo, hi in ((512, 1024), (0, 512), (1792, 2048), (1536, 1792), (1024, 1536), (2048, 2560), (2560, 3072)):
        units += units_of(w2[:, lo:hi])
    units += units_of(i["w_out_2"][0]) + units_of(i["w_peer_q_2"][0])
    assert len(units) == N_UNITS and all(u.shape == (P, UNIT) for u in units)
    qc = np.arange(P) % GRID_W
    half = np.arange(P) // GRID_W
    rows = np.arange(6)[None, :, None] + 5 - half[:, None, None]
    cols = np.clip(np.arange(GRID_W)[None, None] - qc[:, None, None] + NA_WIN_COLS - 1, 0, 2 * NA_WIN_COLS - 2)
    bias = i["na_rel_bias"][0][:, rows, cols].transpose(1, 0, 2, 3)
    qk = np.stack([i["qk_norm_na"][0, 0], i["qk_norm_na"][0, 1], i["qk_norm_dil"][0, 0], i["qk_norm_dil"][0, 1]])
    cols_of = lambda g: g.reshape(DC, P).T
    keys2 = np.concatenate([i["sub_keys1_2"][0].transpose(2, 0, 1), i["sub_keys2_2"][0].transpose(2, 0, 1)], 0)
    return {
        "x": i["x"][0],
        "meta": i["meta_tokens_2"],
        "weights": np.stack(units),
        "const": const,
        "dil_mask": dil,
        "na_bias": bias.reshape(P, NA_HEADS, 6 * GRID_W),
        "gain": np.stack([i["norm_ffn"][0], i["norm2_g_2"][0], i["norm_f_g_2"]]),
        "head_gain": np.stack([i["sb_norm_g_2"][0], i["gla_norm_g_2"][0]]),
        "gain_col": np.stack([cols_of(i["norm_mix"][0]), cols_of(i["norm_ple"][0]), cols_of(i["norm1_g_2"][0])], 1),
        "qk_gain": qk,
        "keys1": i["peer_sub_keys"][0].transpose(2, 0, 1),
        "keys2": keys2,
        "pT": i["p"][0, 0].T.reshape(2, P, SEQ).transpose(1, 0, 2),
        "w_lr": w2[:, 3072:3088].reshape(DC, P, RANK).transpose(1, 0, 2),
        "w_gu": np.concatenate([i["w_gate_up_2"][0], i["b_gate_up_2"]], 0),
        "experts1": np.concatenate([i["peer_expert_u"][0], i["peer_expert_v"][0]], 1),
        "experts2": np.concatenate([i["expert_u_2"][0], i["expert_v_2"][0]], 1),
    }


def kernel(**inputs):
    import concourse.bacc as bacc
    from concourse.bass_utils import run_bass_kernel_spmd

    nc = bacc.Bacc("TRN2", target_bir_lowering=False, num_devices=1)
    arrays = {"in_" + k: np.ascontiguousarray(v) for k, v in layout({k: np.asarray(v) for k, v in inputs.items()}).items()}
    aps = {k[3:]: nc.dram_tensor(k, v.shape, mybir.dt.from_np(v.dtype), kind="ExternalInput").ap() for k, v in arrays.items()}
    out = nc.dram_tensor("out", (SEQ, D), F32, kind="ExternalOutput").ap()
    build(nc, aps, out)
    r = run_bass_kernel_spmd(nc, [arrays], core_ids=[0])
    return r.results[0]["out"].reshape(1, SEQ, D)
```
